# Optimizing a Trainium2 kernel written in Bass

```python
import math
import jax, jax.numpy as jnp
from jax import lax
import numpy as np

D_MODEL = 1024
BATCH = 1
SEQ = 512
DEPTH = 1

N_HEADS = 8
QK_NOPE_DIM = 64
QK_ROPE_DIM = 32
QK_HEAD_DIM = QK_NOPE_DIM + QK_ROPE_DIM
V_HEAD_DIM = 64
Q_LORA_RANK = 384
KV_LORA_RANK = 256
ROPE_THETA = 10000.0
Q_BLOCK = 128
SSM_WIDTH = 512
SSM_GROUP = 16
SSM_GROUPS = SSM_WIDTH // SSM_GROUP
SSM_STATE = 64
DT_MIN = 0.001
DT_MAX = 0.1
N_BRANCHES = 2
D_FF = 2816
CONV_WIDTH = 3
EPS = 1e-6

OFF_CQ = 0
OFF_CKV = OFF_CQ + Q_LORA_RANK
OFF_KR = OFF_CKV + KV_LORA_RANK
OFF_U = OFF_KR + QK_ROPE_DIM
OFF_GATE = OFF_U + SSM_WIDTH
D_IN = OFF_GATE + N_BRANCHES * D_MODEL

kernel_name = "hybrid_mla_s5_gated_convffn"

def _rmsnorm(x, g):
    xf = x.astype(jnp.float32)
    y = xf * lax.rsqrt(jnp.mean(xf * xf, axis=-1, keepdims=True) + EPS)
    return (y * g.astype(jnp.float32)).astype(x.dtype)

def _rope(x, cos, sin):
    half = x.shape[-1] // 2
    x1, x2 = x[..., :half], x[..., half:]
    return jnp.concatenate([x1 * cos - x2 * sin, x2 * cos + x1 * sin], axis=-1)

def _rope_tables(positions, dtype):
    inv_freq = ROPE_THETA ** (-jnp.arange(0, QK_ROPE_DIM, 2, dtype=jnp.float32) / QK_ROPE_DIM)
    ang = positions.astype(jnp.float32)[..., None] * inv_freq
    return jnp.cos(ang).astype(dtype), jnp.sin(ang).astype(dtype)

def _mla(c_q, c_kv, k_r, cos, sin, q_norm, w_uq, kv_norm, w_uk, w_uv):
    B, L, _ = c_q.shape
    q = (_rmsnorm(c_q, q_norm) @ w_uq).reshape(B, L, N_HEADS, QK_HEAD_DIM)
    q_nope = q[..., :QK_NOPE_DIM]
    q_rope = _rope(q[..., QK_NOPE_DIM:], cos[:, :, None, :], sin[:, :, None, :])
    ckv = _rmsnorm(c_kv, kv_norm)
    k_nope = (ckv @ w_uk).reshape(B, L, N_HEADS, QK_NOPE_DIM)
    v = (ckv @ w_uv).reshape(B, L, N_HEADS, V_HEAD_DIM)
    k_rope = _rope(k_r, cos, sin)
    scale = 1.0 / math.sqrt(QK_HEAD_DIM)
    nblk = L // Q_BLOCK
    qn_blk = q_nope.reshape(B, nblk, Q_BLOCK, N_HEADS, QK_NOPE_DIM).transpose(1, 0, 2, 3, 4)
    qr_blk = q_rope.reshape(B, nblk, Q_BLOCK, N_HEADS, QK_ROPE_DIM).transpose(1, 0, 2, 3, 4)
    k_idx = jnp.arange(L)

    def block(args):
        qn, qr, i = args
        s = jnp.einsum('bqhd,bkhd->bhqk', qn, k_nope) + jnp.einsum('bqhd,bkd->bhqk', qr, k_rope)
        s = s.astype(jnp.float32) * scale
        q_idx = i * Q_BLOCK + jnp.arange(Q_BLOCK)
        s = jnp.where(k_idx[None, :] <= q_idx[:, None], s, -jnp.inf)
        p = jax.nn.softmax(s, axis=-1).astype(v.dtype)
        return jnp.einsum('bhqk,bkhd->bqhd', p, v)

    out = lax.map(block, (qn_blk, qr_blk, jnp.arange(nblk)))
    return out.transpose(1, 0, 2, 3, 4).reshape(B, L, N_HEADS * V_HEAD_DIM)

def _ssm_combine(e1, e2):
    a1r, a1i, b1r, b1i = e1
    a2r, a2i, b2r, b2i = e2
    return (a2r * a1r - a2i * a1i,
            a2r * a1i + a2i * a1r,
            a2r * b1r - a2i * b1i + b2r,
            a2r * b1i + a2i * b1r + b2i)

def _s5(u, lam_re, lam_im, log_dt, b_re, b_im, c_re, c_im, d_skip, w_glu, b_glu):
    B, L, _ = u.shape
    uf = u.astype(jnp.float32).reshape(B, L, SSM_GROUPS, SSM_GROUP)
    dt = jnp.exp(log_dt.astype(jnp.float32))[:, None]
    lr = lam_re.astype(jnp.float32)
    li = lam_im.astype(jnp.float32)
    mag = jnp.exp(lr * dt)
    ang = li * dt
    a_re, a_im = mag * jnp.cos(ang), mag * jnp.sin(ang)
    den = lr * lr + li * li
    n_re, n_im = a_re - 1.0, a_im
    z_re = (n_re * lr + n_im * li) / den
    z_im = (n_im * lr - n_re * li) / den
    br, bi = b_re.astype(jnp.float32), b_im.astype(jnp.float32)
    bb_re = z_re[..., None] * br - z_im[..., None] * bi
    bb_im = z_re[..., None] * bi + z_im[..., None] * br
    bu_re = jnp.einsum('blgh,gph->blgp', uf, bb_re)
    bu_im = jnp.einsum('blgh,gph->blgp', uf, bb_im)
    a_seq_re = jnp.broadcast_to(a_re, (L, SSM_GROUPS, SSM_STATE))
    a_seq_im = jnp.broadcast_to(a_im, (L, SSM_GROUPS, SSM_STATE))

    def scan_one(bur, bui):
        _, _, sr, si = lax.associative_scan(_ssm_combine, (a_seq_re, a_seq_im, bur, bui), axis=0)
        return sr, si

    s_re, s_im = jax.vmap(scan_one)(bu_re, bu_im)
    y = (jnp.einsum('blgp,ghp->blgh', s_re, c_re.astype(jnp.float32))
         - jnp.einsum('blgp,ghp->blgh', s_im, c_im.astype(jnp.float32))
         + d_skip.astype(jnp.float32) * uf)
    y = jax.nn.gelu(y.reshape(B, L, SSM_WIDTH), approximate=True)
    y = y * jax.nn.sigmoid(y @ w_glu.astype(jnp.float32) + b_glu.astype(jnp.float32))
    return y.astype(u.dtype)

def _causal_dwconv(h, w, b):
    L = h.shape[1]
    hp = jnp.pad(h, ((0, 0), (CONV_WIDTH - 1, 0), (0, 0)))
    out = b
    for k in range(CONV_WIDTH):
        out = out + w[k] * hp[:, k:k + L, :]
    return out

def _conv_ffn(x, w_up, conv_w, conv_b, w_down):
    h = _causal_dwconv(x @ w_up, conv_w, conv_b)
    gate, val = h[..., :D_FF], h[..., D_FF:]
    return (jax.nn.gelu(gate, approximate=True) * val) @ w_down

def setup_inputs(seed: int = 0) -> dict:
    key = jax.random.key(seed)
    ks = iter(jax.random.split(key, 40))

    def nrm(shape, scale):
        return jax.random.normal(next(ks), shape, jnp.float32) * scale

    def gain(n):
        return 1.0 + nrm((DEPTH, n), 0.02)

    x = jax.random.normal(next(ks), (BATCH, SEQ, D_MODEL), jnp.float32)
    offs = jax.random.randint(next(ks), (BATCH, 1), 0, 1024, dtype=jnp.int32)
    positions = offs + jnp.arange(SEQ, dtype=jnp.int32)[None, :]
    lam_im0 = math.pi * jnp.arange(SSM_STATE, dtype=jnp.float32)
    return {
        "x": x,
        "positions": positions,
        "mix_norm_pre": gain(D_MODEL),
        "w_in": nrm((DEPTH, D_MODEL, D_IN), D_MODEL ** -0.5),
        "q_norm": gain(Q_LORA_RANK),
        "w_uq": nrm((DEPTH, Q_LORA_RANK, N_HEADS * QK_HEAD_DIM), Q_LORA_RANK ** -0.5),
        "kv_norm": gain(KV_LORA_RANK),
        "w_uk": nrm((DEPTH, KV_LORA_RANK, N_HEADS * QK_NOPE_DIM), KV_LORA_RANK ** -0.5),
        "w_uv": nrm((DEPTH, KV_LORA_RANK, N_HEADS * V_HEAD_DIM), KV_LORA_RANK ** -0.5),
        "ssm_lambda_re": -0.5 + nrm((DEPTH, SSM_GROUPS, SSM_STATE), 0.01),
        "ssm_lambda_im": lam_im0 + nrm((DEPTH, SSM_GROUPS, SSM_STATE), 0.01),
        "ssm_log_dt": jax.random.uniform(next(ks), (DEPTH, SSM_GROUPS), jnp.float32,
                                          math.log(DT_MIN), math.log(DT_MAX)),
        "ssm_b_re": nrm((DEPTH, SSM_GROUPS, SSM_STATE, SSM_GROUP), (2.0 * SSM_GROUP) ** -0.5),
        "ssm_b_im": nrm((DEPTH, SSM_GROUPS, SSM_STATE, SSM_GROUP), (2.0 * SSM_GROUP) ** -0.5),
        "ssm_c_re": nrm((DEPTH, SSM_GROUPS, SSM_GROUP, SSM_STATE), (2.0 * SSM_STATE) ** -0.5),
        "ssm_c_im": nrm((DEPTH, SSM_GROUPS, SSM_GROUP, SSM_STATE), (2.0 * SSM_STATE) ** -0.5),
        "ssm_d": nrm((DEPTH, SSM_GROUPS, SSM_GROUP), 1.0),
        "w_glu": nrm((DEPTH, SSM_WIDTH, SSM_WIDTH), SSM_WIDTH ** -0.5),
        "b_glu": nrm((DEPTH, SSM_WIDTH), 0.01),
        "w_branch_attn": nrm((DEPTH, N_HEADS * V_HEAD_DIM, D_MODEL), (N_HEADS * V_HEAD_DIM) ** -0.5),
        "w_branch_ssm": nrm((DEPTH, SSM_WIDTH, D_MODEL), SSM_WIDTH ** -0.5),
        "b_gate": nrm((DEPTH, N_BRANCHES * D_MODEL), 0.01),
        "w_out": nrm((DEPTH, D_MODEL, D_MODEL), D_MODEL ** -0.5),
        "mix_norm_post": gain(D_MODEL),
        "ffn_norm_pre": gain(D_MODEL),
        "w_up": nrm((DEPTH, D_MODEL, 2 * D_FF), D_MODEL ** -0.5),
        "conv_w": nrm((DEPTH, CONV_WIDTH, 2 * D_FF), CONV_WIDTH ** -0.5),
        "conv_b": nrm((DEPTH, 2 * D_FF), 0.01),
        "w_down": nrm((DEPTH, D_FF, D_MODEL), D_FF ** -0.5),
        "ffn_norm_post": gain(D_MODEL),
    }

def reference(x, positions, mix_norm_pre, w_in, q_norm, w_uq, kv_norm, w_uk, w_uv,
              ssm_lambda_re, ssm_lambda_im, ssm_log_dt, ssm_b_re, ssm_b_im, ssm_c_re, ssm_c_im,
              ssm_d, w_glu, b_glu, w_branch_attn, w_branch_ssm, b_gate, w_out, mix_norm_post,
              ffn_norm_pre, w_up, conv_w, conv_b, w_down, ffn_norm_post):
    B, L, _ = x.shape
    cos, sin = _rope_tables(positions, x.dtype)
    for layer in range(DEPTH):
        hn = _rmsnorm(x, mix_norm_pre[layer])
        proj = hn @ w_in[layer]
        c_q = proj[..., OFF_CQ:OFF_CKV]
        c_kv = proj[..., OFF_CKV:OFF_KR]
        k_r = proj[..., OFF_KR:OFF_U]
        u = proj[..., OFF_U:OFF_GATE]
        gate_logits = proj[..., OFF_GATE:] + b_gate[layer]
        attn = _mla(c_q, c_kv, k_r, cos, sin, q_norm[layer], w_uq[layer],
                    kv_norm[layer], w_uk[layer], w_uv[layer])
        ssm = _s5(u, ssm_lambda_re[layer], ssm_lambda_im[layer], ssm_log_dt[layer],
                  ssm_b_re[layer], ssm_b_im[layer], ssm_c_re[layer], ssm_c_im[layer],
                  ssm_d[layer], w_glu[layer], b_glu[layer])
        gates = jax.nn.sigmoid(gate_logits.astype(jnp.float32)).astype(x.dtype)
        gates = gates.reshape(B, L, N_BRANCHES, D_MODEL)
        merged = (gates[:, :, 0] * (attn @ w_branch_attn[layer])
                  + gates[:, :, 1] * (ssm @ w_branch_ssm[layer]))
        x = x + _rmsnorm(merged @ w_out[layer], mix_norm_post[layer])
        hn = _rmsnorm(x, ffn_norm_pre[layer])
        ff = _conv_ffn(hn, w_up[layer], conv_w[layer], conv_b[layer], w_down[layer])
        x = x + _rmsnorm(ff, ffn_norm_post[layer])
    return x


_drawn_inputs = setup_inputs


def setup_inputs(seed=0):
    import zlib

    import numpy as np

    out = dict(_drawn_inputs(seed))
    spreads = {}
    factors = {'mix_norm_pre': 2.688,
     'q_norm': 8.0,
     'kv_norm': 5.877,
     'ssm_lambda_re': 200.0,
     'b_glu': 64.0,
     'b_gate': 8.0,
     'mix_norm_post': 3.459,
     'ffn_norm_pre': 3.403,
     'conv_b': 6.779,
     'ffn_norm_post': 54.333,
     'ssm_lambda_im': 64.0,
     'ssm_log_dt': 64.0,
     'ssm_b_re': 64.0,
     'ssm_b_im': 64.0,
     'ssm_c_re': 64.0,
     'ssm_c_im': 64.0}
    for name, (base, spread) in spreads.items():
        noise = np.random.default_rng([zlib.crc32(name.encode()), seed]).standard_normal(out[name].shape)
        drawn = base * np.exp(spread * noise) if base else spread * noise
        out[name] = __import__('jax').numpy.asarray(drawn.astype(out[name].dtype))
    for name, factor in factors.items():
        out[name] = (out[name] * factor).astype(out[name].dtype)
    return out
```

```python
from contextlib import ExitStack
import math

import numpy as np

import concourse.bass as bass
from concourse import mybir
from concourse.alu_op_type import AluOpType as ALU

ACT = mybir.ActivationFunctionType
F32 = mybir.dt.float32
F32R = mybir.dt.float32r
I32 = mybir.dt.int32
AX_X = mybir.AxisListType.X

P = 128
D = 1024
L = 512
NH = 8
NOPE = 64
ROPE = 32
QK = NOPE + ROPE
VD = 64
RQ = 384
RKV = 256
WS = 512
GROUPS = 32
GH = 16
NS = 64
FF = 2816
EPS = 1e-6
TT = L // P
KD = D // P
KQ = RQ // P
KKV = RKV // P
NG = 2 * D // P
NF = FF // P
NU = WS // P
HG = NH // 2
CH = 512
RING = 4
HALF = 2 * GH

PAIRS = GROUPS // 2
SUB = 4
NC = L // SUB
PPT = 4

O_CQ, O_CKV, O_KR, O_U, O_GATE = 0, RQ, RQ + RKV, RQ + RKV + ROPE, RQ + RKV + ROPE + WS

ROUND = 12582912.0
TWO_PI = (6.28125, 0.001934051513671875, 2 * math.pi - 6.28125 - 0.001934051513671875)
PI_IN = 3.1415925
LN2 = (0.693359375, math.log(2) - 0.693359375)
EXP_TAYLOR = [1 / math.factorial(n) for n in range(8)]
MASKED = -3.0e38

GATES_EARLY = 2
GATES_ATTN = 5


def stream_plan():
    order = []

    def add(name, parts):
        order.extend((name, i) for i in range(parts))

    for j in range(KQ):
        add(("cq", j), 2)
    for j in range(KKV):
        add(("ckv", j), 2)
    add(("kr", 0), 2)
    gate = 0
    for _ in range(GATES_EARLY):
        add(("gate", gate), 2)
        gate += 1
    add(("uv", 0), KKV)
    for g in range(2):
        for m in range(3):
            add(("uq", 3 * g + m), 1)
        add(("uk", g), 1)
        for _ in range(GATES_ATTN):
            add(("gate", gate), 2)
            gate += 1
    for j in range(NU):
        add(("u", j), 2)
    while gate < NG:
        add(("gate", gate), 2)
        gate += 1
    for m in range(NU):
        add(("glu", m), 1)
    for m in range(KD):
        add(("attn_out", m), 1)
        add(("ssm_out", m), 1)
    for j in range(KD):
        add(("w_out", j), 2)
    for f in range(NF):
        add(("up", f), 2)
        add(("up", NF + f), 2)
    for f in range(NF):
        add(("down", f), 2)
    first, end = {}, {}
    for n, (name, _) in enumerate(order):
        first.setdefault(name, n)
        end[name] = n + 1
    return order, first, end


ORDER, FIRST, END = stream_plan()
NCHUNK = len(ORDER)

V_QN, V_KVN = 0, KQ
V_BG = V_KVN + KKV
V_BGLU = V_BG + NG
V_INV = V_BGLU + NU
V_EVEN, V_ODD, V_SIGN = V_INV + 1, V_INV + 2, V_INV + 3
V_CONV = V_SIGN + 1
NV = V_CONV + 4 * 2 * NF

S_NAMES = ["lr", "li", "ldt", "dt", "y", "n", "r", "p", "mag", "ang", "k", "sn", "cs", "ar", "ai",
           "den", "nr", "t0", "t1", "t2", "zr", "zi", "m4"]
S_NAMES += [f"a{k}{c}" for k in (2, 3, 4) for c in "ri"]
S_NAMES += [f"w{k}{c}" for k in (1, 2, 4, 8, 16, 32, 64, 128, 256) for c in "ri"]
SI = {n: i for i, n in enumerate(S_NAMES)}

KB = 1024
BASE = 16512


def build(nc, w_stream, x, positions, vecs, norms, ssm_small, ssm_bc, ssm_d, out):
    x_t = x.rearrange("(t p) d -> t p d", p=P)
    out_t = out.rearrange("(t p) d -> t p d", p=P)
    ctx = ExitStack()
    with ctx:
        def at(name, offset, shape, dt=F32):
            return nc.alloc_sbuf_tensor_at(name, shape, dt, offset=BASE + offset)

        raw = at("raw", 0, [P, RING, CH])
        w_hi = at("w_hi", 8 * KB, [P, RING, CH], F32R)
        w_lo = at("w_lo", 16 * KB, [P, RING, CH], F32R)
        xT_hi = at("xT_hi", 24 * KB, [P, KD, L], F32R)
        xT_lo = at("xT_lo", 40 * KB, [P, KD, L], F32R)
        ident = at("ident", 56 * KB, [P, P])
        causal = at("causal", 56 * KB + 512, [P, P])
        ones = at("ones", 57 * KB, [P, P])
        vec = at("vec", 57 * KB + 512, [P, NV])
        stat = at("stat", 58 * KB + 576, [P, 4, 4 * TT])
        rowst = at("rowst", 58 * KB + 832, [P, 4, 4])
        small = at("small", 58 * KB + 896, [P, len(S_NAMES), PAIRS])
        k_int = at("k_int", 62 * KB, [P, PAIRS], I32)
        d_skip = at("d_skip", 62 * KB + 64, [HALF, PAIRS])
        hb_gate = at("hb_gate", 62 * KB + 128, [P, NG])
        hb_glu = at("hb_glu", 62 * KB + 192, [P, NU])
        R = 62 * KB + 256

        def reg(name, kb, shape, dt=F32):
            return at(name, R + int(kb * KB), shape, dt)

        x_in = reg("x_in", 60, [P, TT, D])
        xn = reg("xn", 76, [P, 2, D])
        g_mix_pre = reg("g_mix_pre", 84, [P, D])
        x_sq = reg("x_sq", 20, [P, 2, D])
        c_raw = reg("c_raw", 20, [P, KQ + KKV, L])
        c_sq = reg("c_sq", 30, [P, KQ + KKV, L])
        r_bc = reg("r_bc", 40, [P, 2, L])
        cn_hi = reg("cn_hi", 0, [P, KQ + KKV, L], F32R)
        cn_lo = reg("cn_lo", 10, [P, KQ + KKV, L], F32R)
        gates = reg("gates", 113, [P, NG, L])
        G8 = 113 + 16
        kr_hi = reg("kr_hi", G8, [P, 2, L], F32R)
        kr_lo = reg("kr_lo", G8 + 4, [P, 2, L], F32R)
        cos_t = reg("cos_t", G8 + 8, [P, L])
        sin_t = reg("sin_t", G8 + 10, [P, L])
        qr_hi = reg("qr_hi", G8 + 12, [P, L], F32R)
        qr_lo = reg("qr_lo", G8 + 14, [P, L], F32R)
        rot_a = reg("rot_a", 93, [P, L])
        rot_b = reg("rot_b", 95, [P, L])
        rot_p = reg("rot_p", 88, [P, 2, L])
        pos_i = reg("pos_i", 54, [P, L], I32)
        ang = reg("ang", 50, [P, L])
        ang_k = reg("ang_k", 52, [P, L])
        q_hi = reg("q_hi", 20, [P, HG, L], F32R)
        q_lo = reg("q_lo", 28, [P, HG, L], F32R)
        k_hi = reg("k_hi", 36, [P, HG, L], F32R)
        k_lo = reg("k_lo", 44, [P, HG, L], F32R)
        v_hi = reg("v_hi", 52, [P, TT, L], F32R)
        v_lo = reg("v_lo", 60, [P, TT, L], F32R)
        pT_hi = reg("pT_hi", 68, [P, TT, L], F32R)
        pT_lo = reg("pT_lo", 76, [P, TT, L], F32R)
        prob = reg("prob", 84, [P, 2, L])
        at_hi = reg("at_hi", 97, [P, NU, L], F32R)
        at_lo = reg("at_lo", 105, [P, NU, L], F32R)
        u_hi = reg("u_hi", 0, [P, NU, PPT, NC], F32R)
        u_lo = reg("u_lo", 8, [P, NU, PPT, NC], F32R)
        rot_c = reg("rot_c", 16, [P, PAIRS, NC])
        rot_s = reg("rot_s", 24, [P, PAIRS, NC])
        ab = reg("ab", 32, [P, SUB, 2, PAIRS, GH])
        ca = reg("ca", 40, [P, SUB + 1, 2, PAIRS, GH])
        ba_blk = reg("ba_blk", 50, [P, 2, PPT, SUB, HALF])
        ca_blk = reg("ca_blk", 54, [P, 2, PPT, SUB + 1, HALF])
        ba_hi = reg("ba_hi", 59, [P, 2, PPT, P], F32R)
        ba_lo = reg("ba_lo", 63, [P, 2, PPT, P], F32R)
        ca_hi = reg("ca_hi", 67, [P, 2, PPT, SUB, HALF], F32R)
        ca_lo = reg("ca_lo", 71, [P, 2, PPT, SUB, HALF], F32R)
        kn_hi = reg("kn_hi", 75, [P, PPT, SUB, HALF], F32R)
        kn_lo = reg("kn_lo", 77, [P, PPT, SUB, HALF], F32R)
        z_t = reg("z_t", 79, [P, 2, L])
        m_t = reg("m_t", 83, [P, 2, L])
        s_hi = reg("s_hi", 87, [P, 2, PPT, NC], F32R)
        s_lo = reg("s_lo", 91, [P, 2, PPT, NC], F32R)
        decay = reg("decay", 95, [P, PPT, NC])
        bc_in = reg("bc_in", 87, [P, 4, PAIRS, GH])
        bt = reg("bt", 91, [P, 2, PAIRS, GH])
        rt = reg("rt", 79, [P, 2, PAIRS * NC // 2])
        y_f = [reg(f"y_f{i}", 2 * i, [P, L]) for i in range(NU)]
        y_hi = reg("y_hi", 16, [P, NU, L], F32R)
        y_lo = reg("y_lo", 24, [P, NU, L], F32R)
        glu_t = reg("glu_t", 32, [P, 2, L])
        glu_y = reg("glu_y", 36, [P, 2, L])
        ss_hi = reg("ss_hi", 40, [P, NU, L], F32R)
        ss_lo = reg("ss_lo", 48, [P, NU, L], F32R)
        mg_hi = reg("mg_hi", 56, [P, KD, L], F32R)
        mg_lo = reg("mg_lo", 72, [P, KD, L], F32R)
        mg_t = reg("mg_t", 88, [P, 2, 2, L])
        x1 = reg("x1", 0, [P, TT, D])
        g_mix_post = reg("g_mix_post", 16, [P, D])
        g_ffn_pre = reg("g_ffn_pre", 20, [P, D])
        xn2 = reg("xn2", 24, [P, 2, D])
        sq = reg("sq", 32, [P, D])
        ff = reg("ff", 36, [P, NF, L])
        g_ffn_post = reg("g_ffn_post", 16, [P, D])
        conv = reg("conv", 80, [P, 2, 2, L])
        gelu = reg("gelu", 88, [P, 2, L])
        ff_hi = [reg(f"ff_hi{i}", 92 + 4 * i, [P, L], F32R) for i in range(2)]
        ff_lo = [reg(f"ff_lo{i}", 94 + 4 * i, [P, L], F32R) for i in range(2)]

        ps = ctx.enter_context(nc.psum_tensor("ps", [P, 8, L], F32))

        def sem(name):
            return ctx.enter_context(nc.semaphore(name))

        x_landed = [sem(f"x_landed{t}") for t in range(TT)]
        raw_landed = [sem(f"raw_landed{s}") for s in range(RING)]
        (g_landed, vec_landed, pos_landed, small_landed, bc_landed, x1_landed, gmid_landed,
         gpost_landed, rope_landed, out_written) = [sem(n) for n in (
             "g_landed", "vec_landed", "pos_landed", "small_landed", "bc_landed", "x1_landed",
             "gmid_landed", "gpost_landed", "rope_landed", "out_written")]
        consts_ready = sem("consts_ready")
        weights_hi, weights_split, chunks_multiplied = sem("weights_hi"), sem("weights_split"), sem("chunks_multiplied")
        dve_step = sem("dve_step")
        sq_summed, ms_ready, rms_ready, xn_ready = sem("sq_summed"), sem("ms_ready"), sem("rms_ready"), sem("xn_ready")
        x_transposed, xT_rounded, xT_split = sem("x_transposed"), sem("xT_rounded"), sem("xT_split")
        x1_ready = sem("x1_ready")
        c_copied, c_squared, c_sums, c_totals = sem("c_copied"), sem("c_squared"), sem("c_sums"), sem("c_totals")
        c_ms, c_rms, cn_ready, cn_rounded, cn_split = (
            sem("c_ms"), sem("c_rms"), sem("cn_ready"), sem("cn_rounded"), sem("cn_split"))
        angle_ready, sine_ready = sem("angle_ready"), sem("sine_ready")
        kr_ready, kr_rounded, kr_split = sem("kr_ready"), sem("kr_rounded"), sem("kr_split")
        gate_done = sem("gate_done")
        v_rounded, v_split = sem("v_rounded"), sem("v_split")
        q_rounded, q_split, k_rounded, k_split = sem("q_rounded"), sem("q_split"), sem("k_rounded"), sem("k_split")
        qr_ready, qr_rounded, qr_split = sem("qr_ready"), sem("qr_rounded"), sem("qr_split")
        scores_done, max_ready, exp_done, probs_ready = sem("scores_done"), sem("max_ready"), sem("exp_done"), sem("probs_ready")
        probs_transposed, pT_rounded, pT_split = sem("probs_transposed"), sem("pT_rounded"), sem("pT_split")
        heads_done, at_rounded, at_split = sem("heads_done"), sem("at_rounded"), sem("at_split")
        u_rounded, u_split = sem("u_rounded"), sem("u_split")
        compacts_ready, blocks_ready, ba_transposed, kn_done = (
            sem("compacts_ready"), sem("blocks_ready"), sem("ba_transposed"), sem("kn_done"))
        skip_added, mats_rounded, mats_split = sem("skip_added"), sem("mats_rounded"), sem("mats_split")
        bu_done, states_ready, states_rounded, states_split = (
            sem("bu_done"), sem("states_ready"), sem("states_rounded"), sem("states_split"))
        y_summed, y_done, y_rounded, y_split = sem("y_summed"), sem("y_done"), sem("y_rounded"), sem("y_split")
        glu_tanh, glu_ready, ss_rounded, ss_split = sem("glu_tanh"), sem("glu_ready"), sem("ss_rounded"), sem("ss_split")
        mg_ready, mg_rounded, mg_split = sem("mg_ready"), sem("mg_rounded"), sem("mg_split")
        tokens_summed = sem("tokens_summed")
        conv_begun, conv_step, conv_done, gelu_done, ff_ready = (
            sem("conv_begun"), sem("conv_step"), sem("conv_done"), sem("gelu_done"), sem("ff_ready"))
        ff_rounded, ff_split = sem("ff_rounded"), sem("ff_split")
        out_ready = sem("out_ready")

        block = ctx.enter_context(nc.Block())

        PRE, POST, FPRE, FPOST = 0, TT, 2 * TT, 3 * TT

        def st(row, n):
            return stat[:, row, n:n + 1]

        def sm(name):
            return small[:, SI[name], :]

        @block.sync
        def _(sp):
            def load(c, s):
                sp.dma_start(raw[:, s, :], w_stream[bass.ds(c, 1), :, :].rearrange("c p n -> p (c n)")
                             ).then_inc(raw_landed[s], 16)

            for s in range(RING):
                load(s, s)
            whole = NCHUNK // RING
            with sp.Fori(1, whole) as i:
                for s in range(RING):
                    sp.wait_ge(weights_split, RING * i + (s + 1 - RING))
                    load(RING * i + s, s)
            for s in range(NCHUNK % RING):
                sp.wait_ge(weights_split, RING * whole + s + 1 - RING)
                load(RING * whole + s, s)
            for t in range(TT):
                sp.wait_ge(out_ready, t + 1)
                sp.dma_start(out_t[t, :, :], x1[:, t, :]).then_inc(out_written, 16)
            sp.wait_ge(out_written, 16 * TT)

        @block.gpsimd
        def _(pool):
            pool.memset(ident[:, :], 0.0).then_inc(consts_ready, 1)
            pool.memset(causal[:, :], 0.0).then_inc(consts_ready, 1)
            pool.memset(ones[:, :], 1.0).then_inc(consts_ready, 1)
            pool.wait_ge(consts_ready, 3)
            pool.affine_select(out=ident[:, :], in_=ident[:, :], compare_op=ALU.not_equal, fill=1.0,
                               base=0, pattern=[[-1, P]], channel_multiplier=1).then_inc(consts_ready, 1)
            pool.affine_select(out=causal[:, :], in_=causal[:, :], compare_op=ALU.is_ge, fill=MASKED,
                               base=0, pattern=[[-1, P]], channel_multiplier=1).then_inc(consts_ready, 1)

            def split(i, s, first):
                pool.wait_ge(raw_landed[s], 16 * i + 16)
                if not first:
                    pool.wait_ge(chunks_multiplied, RING * i + (s + 1 - RING))
                pool.tensor_tensor(w_hi[:, s, 0:1], raw[:, s, 0:1], ones[:, 0:1], ALU.mult)
                pool.tensor_scalar(w_hi[:, s, 1:CH], raw[:, s, 1:CH], 1.0, 1.0, ALU.mult, ALU.mult).then_inc(weights_hi, 1)
                pool.wait_ge(weights_hi, RING * i + s + 1)
                pool.tensor_tensor(w_lo[:, s, :], raw[:, s, :], w_hi[:, s, :].bitcast(F32),
                                   ALU.subtract).then_inc(weights_split, 1)

            for s in range(RING):
                split(0, s, True)
            whole = NCHUNK // RING
            with pool.Fori(1, whole) as i:
                for s in range(RING):
                    split(i, s, False)
            for s in range(NCHUNK % RING):
                split(whole, s, False)

        @block.tensor
        def _(pe):
            def three(o, wh, wl, xh, xl, start, stop):
                pe.matmul(o, wh, xh, start=start, stop=False, skip_group_check=True)
                pe.matmul(o, wh, xl, start=False, stop=False, skip_group_check=True)
                return pe.matmul(o, wl, xh, start=False, stop=stop, skip_group_check=True)

            def transpose_x(n):
                t = n % TT
                src = xn if n < TT else xn2
                pe.wait_ge(xn_ready, n + 1)
                for k in range(KD):
                    last = pe.transpose(ps[:, 2 * t + k // 4, (k % 4) * P:(k % 4 + 1) * P],
                                        src[:, t % 2, k * P:(k + 1) * P], ident[:, :])
                last.then_inc(x_transposed, 1)

            def chunk(name, part, bank, hi, lo, k0, nk, start, stop):
                c = FIRST[name] + part
                s = c % RING
                pe.wait_ge(weights_split, c + 1)
                for k in range(nk):
                    last = three(ps[:, bank, :], w_hi[:, s, k * P:(k + 1) * P], w_lo[:, s, k * P:(k + 1) * P],
                                 hi[:, k0 + k, :], lo[:, k0 + k, :], start and k == 0, stop and k == nk - 1)
                last.then_inc(chunks_multiplied, 1)

            def in_half(name, part, bank):
                chunk(name, part, bank, xT_hi, xT_lo, 4 * part, 4, part == 0, part == 1)

            def gate_half(n, part):
                if part == 0 and n >= 2:
                    pe.wait_ge(gate_done, n - 1)
                in_half(("gate", n), part, 6 + n % 2)

            def in_tile(name, bank):
                in_half(name, 0, bank)
                in_half(name, 1, bank)

            pe.wait_ge(consts_ready, 5)
            for t in range(TT):
                transpose_x(PRE + t)
            pe.wait_ge(xT_split, 2 * TT)
            for j in range(KQ):
                in_tile(("cq", j), j)
            for j in range(KKV):
                in_tile(("ckv", j), KQ + j)
            in_tile(("kr", 0), 5)
            gate_half(0, 0)
            gate_half(0, 1)
            pe.wait_ge(c_sums, 2)
            pe.wait_ge(c_copied, 2)
            for b in range(2):
                last = pe.matmul(ps[:, b, :], ones[:, :], c_sq[:, (0, KQ)[b], :], start=True, stop=True)
            last.then_inc(c_totals, 1)
            gate_half(1, 0)
            gate_half(1, 1)
            pe.wait_ge(cn_split, KQ + KKV)
            for kk in range(KKV):
                c = FIRST[("uv", 0)] + kk
                s = c % RING
                pe.wait_ge(weights_split, c + 1)
                for t in range(TT):
                    tok = slice(t * P, (t + 1) * P)
                    last = three(ps[:, t, :], cn_hi[:, KQ + kk, tok], cn_lo[:, KQ + kk, tok],
                                 w_hi[:, s, :], w_lo[:, s, :], kk == 0, kk == KKV - 1)
                last.then_inc(chunks_multiplied, 1)

            UNITS = HG * TT
            gate = GATES_EARLY
            for g in range(2):
                if g == 0:
                    pe.wait_ge(v_split, TT)
                    pe.wait_ge(kr_ready, 1)
                else:
                    pe.wait_ge(pT_split, UNITS)
                    pe.wait_ge(at_split, HG)
                for m, bank in enumerate((4, 5, 2)):
                    chunk(("uq", 3 * g + m), 0, bank, cn_hi, cn_lo, 0, KQ, True, True)
                c = FIRST[("uk", g)]
                s = c % RING
                pe.wait_ge(weights_split, c + 1)
                for m, bank in enumerate((3, 0)):
                    for k in range(KKV):
                        cols = slice((2 * m + k) * P, (2 * m + k + 1) * P)
                        last = three(ps[:, bank, :], w_hi[:, s, cols], w_lo[:, s, cols],
                                     cn_hi[:, KQ + k, :], cn_lo[:, KQ + k, :], k == 0, k == KKV - 1)
                last.then_inc(chunks_multiplied, 1)
                gate_half(gate, 0)
                gate_half(gate, 1)
                gate += 1

                pe.wait_ge(q_split, HG * (g + 1))
                pe.wait_ge(k_split, HG * (g + 1))
                pe.wait_ge(rope_landed, 16 * 4 * HG * 2 * (g + 1))

                def scores(u):
                    h, i = u // TT, u % TT
                    if u >= 2:
                        pe.wait_ge(exp_done, UNITS * g + u - 1)
                    tok = slice(i * P, (i + 1) * P)
                    n = (i + 1) * P
                    three(ps[:, u % 2, 0:n], q_hi[:, h, tok], q_lo[:, h, tok],
                          k_hi[:, h, 0:n], k_lo[:, h, 0:n], True, True).then_inc(scores_done, 1)

                def turn_probs(u):
                    if u >= 2 or g:
                        pe.wait_ge(pT_split, UNITS * g + u - 1)
                    pe.wait_ge(probs_ready, UNITS * g + u + 1)
                    for j in range(u % TT + 1):
                        last = pe.transpose(ps[:, 2 + u % 2, j * P:(j + 1) * P],
                                            prob[:, u % 2, j * P:(j + 1) * P], ident[:, :])
                    last.then_inc(probs_transposed, 1)

                def values(h):
                    head = HG * g + h
                    pe.wait_ge(pT_split, UNITS * g + TT * (h + 1))
                    if head >= 2:
                        pe.wait_ge(at_split, 2 * (head // 2))
                    pair = slice((head // 2) * P, (head // 2 + 1) * P)
                    for j in range(TT):
                        last = three(ps[:, 4 + h % 2, j * P:L], v_hi[:, j, pair], v_lo[:, j, pair],
                                     pT_hi[:, j, j * P:L], pT_lo[:, j, j * P:L], j == 0, j == TT - 1)
                    last.then_inc(heads_done, 1)

                half = 0
                for t in range(UNITS + 3):
                    if t >= 6 and (t - 6) % TT == 0:
                        values((t - 6) // TT)
                    if 2 <= t < UNITS + 2:
                        turn_probs(t - 2)
                    if t < UNITS:
                        scores(t)
                    if t % 2 == 1 and half < 2 * (GATES_ATTN - 1):
                        gate_half(gate + half // 2, half % 2)
                        half += 1
                gate += half // 2

            for j in range(NU):
                if j == 2:
                    pe.wait_ge(pT_split, 2 * UNITS)
                in_tile(("u", j), j)
            for it in range(NU):
                if it:
                    gate_half(gate, 0)
                    gate_half(gate, 1)
                    gate += 1
                pe.wait_ge(u_split, NU)
                pe.wait_ge(blocks_ready, 8 * (it + 1))
                for c in range(2):
                    for q in range(PPT):
                        last = pe.transpose(ps[:, c, q * P:(q + 1) * P],
                                            ba_blk[:, c, q, :, :].rearrange("p s h -> p (s h)"), ident[:, :])
                last.then_inc(ba_transposed, 1)
                for q in range(PPT):
                    for c in range(2):
                        last = pe.matmul(ps[0:HALF, 2, q * P:(q + 1) * P], ba_blk[:, c, q, SUB - 1, :],
                                         ca_blk[:, c, q, 0:SUB, :].rearrange("p s h -> p (s h)"),
                                         start=(c == 0), stop=(c == 1), skip_group_check=True)
                last.then_inc(kn_done, 1)
                pe.wait_ge(mats_split, 2 * it + 1)
                for c in range(2):
                    for q in range(PPT):
                        last = three(ps[:, 3 + c, q * NC:(q + 1) * NC], ba_hi[:, c, q, :], ba_lo[:, c, q, :],
                                     u_hi[:, it, q, :], u_lo[:, it, q, :], True, True)
                last.then_inc(bu_done, 1)
                if it == 0:
                    gate_half(gate, 0)
                    gate_half(gate, 1)
                    gate += 1
                pe.wait_ge(mats_split, 2 * it + 2)
                pe.wait_ge(states_split, it + 1)
                for q in range(PPT):
                    o = ps[:, 5, q * NC:(q + 1) * NC]
                    three(o, kn_hi[:, q, :, :].rearrange("p s h -> p (s h)"), kn_lo[:, q, :, :].rearrange("p s h -> p (s h)"),
                          u_hi[:, it, q, :], u_lo[:, it, q, :], True, False)
                    for c in range(2):
                        last = three(o, ca_hi[:, c, q, :, :].rearrange("p s h -> p (s h)"),
                                     ca_lo[:, c, q, :, :].rearrange("p s h -> p (s h)"),
                                     s_hi[:, c, q, :], s_lo[:, c, q, :], False, c == 1)
                last.then_inc(y_summed, 1)

            pe.wait_ge(y_split, NU)
            for m in range(NU):
                chunk(("glu", m), 0, m, y_hi, y_lo, 0, NU, True, True)
            for m in range(KD):
                b = 2 * (m % 2)
                if m >= 2:
                    pe.wait_ge(mg_ready, m - 1)
                else:
                    pe.wait_ge(glu_ready, NU)
                chunk(("attn_out", m), 0, b, at_hi, at_lo, 0, NU, True, True)
                if m == 0:
                    pe.wait_ge(ss_split, NU)
                chunk(("ssm_out", m), 0, b + 1, ss_hi, ss_lo, 0, NU, True, True)

            def token_sums(c, stat_hi, stat_lo, tiles, half, start, stop, ready=None):
                s = c % RING
                for t in tiles:
                    if ready is not None:
                        ready(t)
                    tok = slice(t * P, (t + 1) * P)
                    last = three(ps[:, 2 * t + half, :], stat_hi[:, tok], stat_lo[:, tok],
                                 w_hi[:, s, :], w_lo[:, s, :], start, stop)
                return last

            def merged_read(t):
                if t == 0:
                    pe.wait_ge(mg_split, KD)

            for j in range(KD - 2):
                pe.wait_ge(mg_split, j + 1)
                for half in range(2):
                    c = FIRST[("w_out", j)] + half
                    pe.wait_ge(weights_split, c + 1)
                    token_sums(c, mg_hi[:, j, :], mg_lo[:, j, :], (2, 3, 0, 1), half, j == 0, False,
                               merged_read if j == 0 else None).then_inc(chunks_multiplied, 1)
            for t in range(TT):
                for j in (KD - 2, KD - 1):
                    for half in range(2):
                        c = FIRST[("w_out", j)] + half
                        pe.wait_ge(weights_split, c + 1)
                        last = token_sums(c, mg_hi[:, j, :], mg_lo[:, j, :], (t,), half, False, j == KD - 1)
                        if t == TT - 1:
                            last.then_inc(chunks_multiplied, 1)
                if t < TT - 1:
                    last.then_inc(tokens_summed, 1)
            for t in range(TT):
                transpose_x(TT + t)

            pe.wait_ge(xT_split, 4 * TT)
            up0 = FIRST[("up", 0)]

            def up_pair(i, b, first):
                if not first:
                    pe.wait_ge(conv_done, 4 * i + 2 * b - 2)
                for v in range(2):
                    for part in range(2):
                        q = 4 * b + 2 * v + part
                        s = (up0 + q) % RING
                        pe.wait_ge(weights_split, 8 * i + (up0 + q + 1))
                        for k in range(4):
                            last = three(ps[:, 2 * b + v, :], w_hi[:, s, k * P:(k + 1) * P],
                                         w_lo[:, s, k * P:(k + 1) * P], xT_hi[:, 4 * part + k, :],
                                         xT_lo[:, 4 * part + k, :], part == 0 and k == 0, part == 1 and k == 3)
                        last.then_inc(chunks_multiplied, 1)

            for b in range(2):
                up_pair(0, b, True)
            with pe.Fori(1, NF // 2) as i:
                for b in range(2):
                    up_pair(i, b, False)

            down0 = FIRST[("down", 0)]

            def down_pair(i, first):
                for b in range(2):
                    pe.wait_ge(ff_split, 2 * i + (b + 1))
                    for half in range(2):
                        q = 2 * b + half
                        pe.wait_ge(weights_split, 4 * i + (down0 + q + 1))
                        token_sums(down0 + q, ff_hi[b], ff_lo[b], (2, 3, 0, 1), half, first and b == 0, False
                                   ).then_inc(chunks_multiplied, 1)

            pe.wait_ge(conv_done, 2 * NF)
            down_pair(0, True)
            with pe.Fori(1, NF // 2 - 1) as i:
                down_pair(i, False)
            for t in range(TT):
                for b in range(2):
                    for half in range(2):
                        c = FIRST[("down", NF - 2 + b)] + half
                        pe.wait_ge(ff_split, NF - 1 + b)
                        pe.wait_ge(weights_split, c + 1)
                        last = token_sums(c, ff_hi[b], ff_lo[b], (t,), half, False, b == 1)
                        if t == TT - 1:
                            last.then_inc(chunks_multiplied, 1)
                if t < TT - 1:
                    last.then_inc(tokens_summed, 1)

        def cv(row, v, f):
            at0 = V_CONV + (2 * row + v) * NF
            return vec[:, at0 + f:at0 + f + 1] if isinstance(f, int) else vec[:, bass.ds(f + at0, 1)]

        def ff_tile(f):
            return ff[:, f, :] if isinstance(f, int) else ff[:, bass.ds(f, 1), :].rearrange("p a n -> p (a n)")

        def token_bank(t):
            return ps[:, 2 * t:2 * t + 2, :].rearrange("p b n -> p (b n)")

        def tokens_ready(eng, n):
            t = n % TT
            if t < TT - 1:
                eng.wait_ge(tokens_summed, (TT - 1) * (n // (2 * TT)) + t + 1)
            else:
                eng.wait_ge(chunks_multiplied, END[("w_out", KD - 1)] if n < FPOST else NCHUNK)

        @block.scalar
        def _(act):
            for t in range(TT):
                act.dma_start(x_in[:, t, :], x_t[t, :, :]).then_inc(x_landed[t], 16)
            act.dma_start(g_mix_pre[:, :], norms[0:1, :].partition_broadcast(P).rearrange("p a d -> p (a d)")).then_inc(g_landed, 16)
            act.dma_start(pos_i[:, :], positions.partition_broadcast(P).rearrange("p a d -> p (a d)")).then_inc(pos_landed, 16)
            act.dma_start(vec[:, :], vecs).then_inc(vec_landed, 16)
            act.dma_start(small[:, 0:3, :], ssm_small).then_inc(small_landed, 16)
            act.dma_start(d_skip[:, :], ssm_d).then_inc(small_landed, 16)

            def square_sum(n, squares, src):
                act.activation(squares, src, ACT.Square, accum_out=st(0, n)).then_inc(sq_summed, 1)

            def root(n):
                act.wait_ge(ms_ready, n + 1)
                act.activation(st(2, n), st(1, n), ACT.Sqrt).then_inc(rms_ready, 1)

            def round_xT(n):
                t = n % TT
                act.wait_ge(x_transposed, n + 1)
                for b in range(2):
                    act.activation(xT_hi[:, 4 * b:4 * b + 4, t * P:(t + 1) * P],
                                   ps[:, 2 * t + b, :].rearrange("p (k n) -> p k n", k=4),
                                   ACT.Copy).then_inc(xT_rounded, 1)

            for t in range(TT):
                act.wait_ge(x_landed[t], 16)
                if t >= 2:
                    act.wait_ge(sq_summed, t - 1)
                square_sum(PRE + t, x_sq[:, t % 2, :], x_in[:, t, :])
                root(PRE + t)
                if t >= 1:
                    round_xT(t - 1)
            round_xT(TT - 1)

            act.wait_ge(angle_ready, 1)
            act.activation(sin_t[:, :], ang[:, :], ACT.Sin).then_inc(sine_ready, 1)
            act.wait_ge(angle_ready, 2)
            act.activation(cos_t[:, :], ang[:, :], ACT.Sin).then_inc(sine_ready, 1)
            act.wait_ge(angle_ready, 3)
            act.activation(sm("sn"), sm("r"), ACT.Sin).then_inc(sine_ready, 1)
            act.wait_ge(angle_ready, 4)
            act.activation(sm("cs"), sm("r"), ACT.Sin).then_inc(sine_ready, 1)

            for j in range(KQ + KKV):
                name = ("cq", j) if j < KQ else ("ckv", j - KQ)
                act.wait_ge(chunks_multiplied, END[name])
                act.activation(c_raw[:, j, :], ps[:, j, :], ACT.Copy).then_inc(c_copied, 1)
                act.activation(c_sq[:, j, :], ps[:, j, :], ACT.Square).then_inc(c_squared, 1)
            act.wait_ge(kr_ready, 3)
            act.activation(kr_hi[:, :, :], rot_p[:, :, :], ACT.Copy).then_inc(kr_rounded, 1)

            def gate_tanh(n):
                act.wait_ge(chunks_multiplied, END[("gate", n)])
                act.activation(gates[:, n, :], ps[:, 6 + n % 2, :], ACT.Tanh, bias=hb_gate[:, n:n + 1],
                               scale=0.5).then_inc(gate_done, 1)

            act.wait_ge(c_ms, 2)
            act.activation(r_bc[:, :, :], r_bc[:, :, :], ACT.Sqrt).then_inc(c_rms, 1)
            gate_tanh(0)
            for j in range(KQ + KKV):
                act.wait_ge(cn_ready, j + 1)
                act.activation(cn_hi[:, j, :], c_raw[:, j, :], ACT.Copy).then_inc(cn_rounded, 1)
            gate_tanh(1)
            act.wait_ge(chunks_multiplied, END[("uv", 0)])
            for t in range(TT):
                act.activation(v_hi[:, t, :], ps[:, t, :], ACT.Copy).then_inc(v_rounded, 1)

            UNITS = HG * TT
            gate = GATES_EARLY
            scale = 1.0 / math.sqrt(QK)
            for g in range(2):
                if g:
                    act.wait_ge(scores_done, UNITS * g)
                for m, bank in enumerate((4, 5)):
                    act.wait_ge(chunks_multiplied, END[("uq", 3 * g + m)])
                    for e in range(2):
                        act.activation(q_hi[0:NOPE, 2 * m + e, :], ps[e * NOPE:(e + 1) * NOPE, bank, :],
                                       ACT.Copy, scale=scale).then_inc(q_rounded, 1)
                if g == 0:
                    act.wait_ge(kr_split, 1)
                for src, dst in ((kr_hi, k_hi), (kr_lo, k_lo)):
                    for c in range(2):
                        for h in range(HG):
                            act.dma_start(dst[NOPE + 32 * c:NOPE + 32 * (c + 1), h, :].bitcast(F32),
                                          src[64 * c:64 * c + 32, h % 2, :].bitcast(F32)).then_inc(rope_landed, 16)
                act.wait_ge(qr_ready, g + 1)
                act.activation(qr_hi[:, :], rot_a[:, :], ACT.Copy, scale=scale).then_inc(qr_rounded, 1)
                act.wait_ge(chunks_multiplied, END[("uk", g)])
                for m, bank in enumerate((3, 0)):
                    for e in range(2):
                        act.activation(k_hi[0:NOPE, 2 * m + e, :], ps[e * NOPE:(e + 1) * NOPE, bank, :],
                                       ACT.Copy).then_inc(k_rounded, 1)
                act.wait_ge(qr_split, g + 1)
                for src, dst in ((qr_hi, q_hi), (qr_lo, q_lo)):
                    for c in range(2):
                        for h in range(HG):
                            act.dma_start(dst[NOPE + 32 * c:NOPE + 32 * (c + 1), h, :].bitcast(F32),
                                          src[64 * c + 32 * (h // 2):64 * c + 32 * (h // 2) + 32, :].bitcast(F32)).then_inc(rope_landed, 16)
                gate_tanh(gate)
                gate += 1

                def round_pair(pair):
                    act.wait_ge(heads_done, HG * g + 2 * pair + 2)
                    for e in range(2):
                        act.activation(at_hi[e * VD:(e + 1) * VD, 2 * g + pair, :], ps[e * VD:(e + 1) * VD, 4 + e, :],
                                       ACT.Copy).then_inc(at_rounded, 1)

                for t in range(UNITS + 3):
                    if t == 12:
                        round_pair(0)
                    if t < UNITS:
                        n = (t % TT + 1) * P
                        act.wait_ge(max_ready, UNITS * g + t + 1)
                        if t >= 2:
                            act.wait_ge(probs_transposed, UNITS * g + t - 1)
                        act.activation(prob[:, t % 2, 0:n], ps[:, t % 2, 0:n], ACT.Exp, bias=rowst[:, 0, t % 4:t % 4 + 1],
                                       accum_out=rowst[:, 1, t % 4:t % 4 + 1]).then_inc(exp_done, 1)
                    if 2 <= t < UNITS + 2:
                        u = t - 2
                        i = u % TT
                        act.wait_ge(probs_transposed, UNITS * g + u + 1)
                        if u >= TT or g:
                            act.wait_ge(heads_done, HG * g + u // TT)
                        act.activation(pT_hi[:, 0:i + 1, i * P:(i + 1) * P],
                                       ps[:, 2 + u % 2, 0:(i + 1) * P].rearrange("p (j n) -> p j n", n=P),
                                       ACT.Copy).then_inc(pT_rounded, 1)
                    if t % 4 == 1 and t > 4:
                        gate_tanh(gate)
                        gate += 1
                round_pair(1)

            act.dma_start(bc_in[:, :, :, :], ssm_bc).then_inc(bc_landed, 16)
            for j in range(NU):
                act.wait_ge(chunks_multiplied, END[("u", j)])
                for s in range(SUB):
                    for q in range(PPT):
                        ins = act.activation(u_hi[HALF * s:HALF * (s + 1), j, q, :],
                                             ps[HALF * q:HALF * (q + 1), j, s::SUB], ACT.Copy)
                        ins.then_inc(u_rounded, 1)

            for it in range(NU):
                pr = slice(it * PPT, (it + 1) * PPT)
                if it == 0:
                    act.wait_ge(compacts_ready, 1)
                else:
                    act.wait_ge(kn_done, it)
                    act.wait_ge(mats_split, 2 * it)
                for c in range(2):
                    for e in range(2):
                        rows, cols = slice(NS * e, NS * (e + 1)), slice(GH * e, GH * (e + 1))
                        act.activation(ba_blk[rows, c, :, :, cols], ab[rows, :, c, pr, :].rearrange("p s q h -> p q s h"),
                                       ACT.Copy).then_inc(blocks_ready, 1)
                        act.activation(ca_blk[rows, c, :, :, cols], ca[rows, :, c, pr, :].rearrange("p s q h -> p q s h"),
                                       ACT.Copy).then_inc(blocks_ready, 1)
                act.wait_ge(blocks_ready, 8 * (it + 1))
                if it:
                    act.wait_ge(y_summed, it)
                for c in range(2):
                    act.activation(ca_hi[:, c, :, :, :], ca_blk[:, c, :, 1:SUB + 1, :], ACT.Copy).then_inc(mats_rounded, 1)
                act.wait_ge(ba_transposed, it + 1)
                for c in range(2):
                    act.activation(ba_hi[:, c, :, :], ps[:, c, :].rearrange("p (q n) -> p q n", q=PPT),
                                   ACT.Copy).then_inc(mats_rounded, 1)
                act.wait_ge(skip_added, it + 1)
                for s in range(SUB):
                    act.activation(kn_hi[HALF * s:HALF * (s + 1), :, s:SUB, :],
                                   ps[0:HALF, 2, :].rearrange("p (q t h) -> p q t h", q=PPT, t=SUB)[:, :, 0:SUB - s, :],
                                   ACT.Copy).then_inc(mats_rounded, 1)
                gate_tanh(gate)
                gate += 1
                act.wait_ge(states_ready, it + 1)
                act.activation(s_hi[:, :, :, 1:NC], z_t[:, :, :].rearrange("p c (q n) -> p c q n", q=PPT)[:, :, :, 0:NC - 1],
                               ACT.Copy).then_inc(states_rounded, 1)
                act.wait_ge(y_summed, it + 1)
                for s in range(SUB):
                    for q in range(PPT):
                        act.activation(y_f[it][HALF * q:HALF * (q + 1), s::SUB],
                                       ps[HALF * s:HALF * (s + 1), 5, q * NC:(q + 1) * NC],
                                       ACT.Gelu_apprx_tanh).then_inc(y_done, 1)
            for j in range(NU):
                act.wait_ge(y_done, SUB * PPT * (j + 1))
                act.activation(y_hi[:, j, :], y_f[j][:, :], ACT.Copy).then_inc(y_rounded, 1)
            for m in range(NU):
                act.wait_ge(chunks_multiplied, END[("glu", m)])
                if m >= 2:
                    act.wait_ge(glu_ready, m - 1)
                act.activation(glu_t[:, m % 2, :], ps[:, m, :], ACT.Tanh, bias=hb_glu[:, m:m + 1],
                               scale=0.5).then_inc(glu_tanh, 1)
                act.wait_ge(glu_ready, m + 1)
                act.activation(ss_hi[:, m, :], glu_y[:, m % 2, :], ACT.Copy, scale=0.5).then_inc(ss_rounded, 1)
            for m in range(KD):
                act.wait_ge(mg_ready, m + 1)
                act.activation(mg_hi[:, m, :], mg_t[:, m % 2, 0, :], ACT.Copy, scale=0.5).then_inc(mg_rounded, 1)
                if m == 0:
                    act.wait_ge(ss_split, NU)
                    for t in range(TT):
                        act.dma_start(x1[:, t, :], x_t[t, :, :]).then_inc(x1_landed, 16)
                    act.wait_ge(chunks_multiplied, END[("glu", NU - 1)])
                    for n, dst in ((1, g_mix_post), (2, g_ffn_pre)):
                        act.dma_start(dst[:, :], norms[n:n + 1, :].partition_broadcast(P).rearrange("p a d -> p (a d)")).then_inc(gmid_landed, 16)

            act.wait_ge(chunks_multiplied, END[("ssm_out", KD - 1)])
            for t in range(TT):
                tokens_ready(act, POST + t)
                if t:
                    act.wait_ge(sq_summed, POST + 2 * t)
                square_sum(POST + 2 * t, sq[:, :], token_bank(t))
                root(POST + 2 * t)
                act.wait_ge(x1_ready, t + 1)
                square_sum(POST + 2 * t + 1, sq[:, :], x1[:, t, :])
                root(POST + 2 * t + 1)
                if t:
                    round_xT(TT + t - 1)
            round_xT(2 * TT - 1)
            act.wait_ge(xn_ready, 2 * TT)
            act.dma_start(g_ffn_post[:, :], norms[3:4, :].partition_broadcast(P).rearrange("p a d -> p (a d)")).then_inc(gpost_landed, 16)

            up0 = FIRST[("up", 0)]

            def up_pair(i, b, f, first):
                for v in range(2):
                    act.wait_ge(chunks_multiplied, 8 * i + (up0 + 4 * b + 2 * v + 2))
                    if not first:
                        act.wait_ge(ff_ready, 2 * i + (b - 1))
                    act.activation(conv[:, b, v, :], ps[:, 2 * b + v, :], ACT.Identity,
                                   bias=cv(3, v, f), scale=cv(2, v, f)).then_inc(conv_begun, 1)
                act.wait_ge(conv_done, 4 * i + (2 * b + 1))
                act.activation(gelu[:, b, :], conv[:, b, 0, :], ACT.Gelu_apprx_tanh).then_inc(gelu_done, 1)

            for b in range(2):
                up_pair(0, b, b, True)
            with act.Fori(1, NF // 2) as i:
                for b in range(2):
                    up_pair(i, b, 2 * i + b, False)

            down0 = FIRST[("down", 0)]

            def ff_round(i, b, f, first):
                if not first:
                    act.wait_ge(chunks_multiplied, 4 * i + (down0 + 2 * b - 2))
                act.activation(ff_hi[b][:, :], ff_tile(f), ACT.Copy).then_inc(ff_rounded, 1)

            act.wait_ge(ff_ready, NF)
            for b in range(2):
                ff_round(0, b, b, True)
            with act.Fori(1, NF // 2) as i:
                for b in range(2):
                    ff_round(i, b, 2 * i + b, False)
            for t in range(TT):
                tokens_ready(act, FPOST + t)
                act.wait_ge(sq_summed, FPOST + t)
                square_sum(FPOST + t, sq[:, :], token_bank(t))
                root(FPOST + t)

        @block.vector
        def _(dve):
            steps = [0]

            def link(ins):
                ins.then_inc(dve_step, 1)
                steps[0] += 1
                dve.wait_ge(dve_step, steps[0])

            def tt(o, a, b, op):
                link(dve.tensor_tensor(o, a, b, op))

            def ts(o, a, s1, s2, op0, op1):
                link(dve.tensor_scalar(o, a, s1, s2, op0, op1))

            def stt(o, a, s, b, op0, op1):
                link(dve.scalar_tensor_tensor(out=o, in0=a, scalar=s, in1=b, op0=op0, op1=op1))

            def rsqrt_mean(n, count):
                dve.wait_ge(sq_summed, n + 1)
                dve.tensor_scalar(st(1, n), st(0, n), 1.0 / count, EPS, ALU.mult, ALU.add).then_inc(ms_ready, 1)
                dve.wait_ge(rms_ready, n + 1)
                link(dve.reciprocal(st(3, n), st(2, n)))

            def split_xT(n):
                t = n % TT
                for b in range(2):
                    dve.wait_ge(xT_rounded, 2 * n + b + 1)
                    o = (slice(None), slice(4 * b, 4 * b + 4), slice(t * P, (t + 1) * P))
                    dve.tensor_tensor(xT_lo[o], ps[:, 2 * t + b, :].rearrange("p (k n) -> p k n", k=4),
                                      xT_hi[o].bitcast(F32), ALU.subtract).then_inc(xT_split, 1)

            for t in range(TT):
                rsqrt_mean(PRE + t, D)
                if t == 0:
                    dve.wait_ge(g_landed, 16)
                if t >= 2:
                    dve.wait_ge(x_transposed, t - 1)
                dve.scalar_tensor_tensor(out=xn[:, t % 2, :], in0=x_in[:, t, :], scalar=st(3, PRE + t),
                                         in1=g_mix_pre[:, :], op0=ALU.mult, op1=ALU.mult).then_inc(xn_ready, 1)
                if t:
                    split_xT(t - 1)
            split_xT(TT - 1)

            def reduce_angle(a, k):
                ts(k, a, 1.0 / (2 * math.pi), ROUND, ALU.mult, ALU.add)
                ts(k, k, ROUND, None, ALU.subtract, ALU.bypass)
                for part in TWO_PI:
                    stt(a, k, -part, a, ALU.mult, ALU.add)

            def quarter_turn(a, k):
                ts(a, a, math.pi / 2, None, ALU.add, ALU.bypass)
                ts(k, a, math.pi, -2 * math.pi, ALU.is_gt, ALU.mult)
                tt(a, a, k, ALU.add)

            def clamp(a, signal):
                dve.tensor_scalar(a, a, PI_IN, -PI_IN, ALU.min, ALU.max).then_inc(angle_ready, 1)
                dve.wait_ge(angle_ready, signal)

            dve.wait_ge(pos_landed, 16)
            dve.wait_ge(vec_landed, 16)
            link(dve.tensor_copy(ang[:, :], pos_i[:, :]))
            ts(ang[:, :], ang[:, :], vec[:, V_INV:V_INV + 1], None, ALU.mult, ALU.bypass)
            reduce_angle(ang[:, :], ang_k[:, :])
            clamp(ang[:, :], 1)
            dve.wait_ge(sine_ready, 1)
            quarter_turn(ang[:, :], ang_k[:, :])
            clamp(ang[:, :], 2)
            ts(sin_t[:, :], sin_t[:, :], vec[:, V_SIGN:V_SIGN + 1], None, ALU.mult, ALU.bypass)
            ts(hb_gate[:, :], vec[:, V_BG:V_BG + NG], 0.5, None, ALU.mult, ALU.bypass)
            ts(hb_glu[:, :], vec[:, V_BGLU:V_BGLU + NU], 0.5, None, ALU.mult, ALU.bypass)

            def exponential(o, y):
                n, r, p = sm("n"), sm("r"), sm("p")
                ts(sm("y"), y, -90.0, 89.0, ALU.max, ALU.min)
                ts(n, sm("y"), 1.0 / math.log(2), ROUND, ALU.mult, ALU.add)
                ts(n, n, ROUND, None, ALU.subtract, ALU.bypass)
                stt(r, n, -LN2[0], sm("y"), ALU.mult, ALU.add)
                stt(r, n, -LN2[1], r, ALU.mult, ALU.add)
                ts(p, r, EXP_TAYLOR[7], None, ALU.mult, ALU.bypass)
                for c in EXP_TAYLOR[6:0:-1]:
                    stt(p, p, c, r, ALU.add, ALU.mult)
                ts(p, p, 1.0, None, ALU.add, ALU.bypass)
                ts(n, n, -127.0, 128.0, ALU.max, ALU.min)
                ts(n, n, 127.0, None, ALU.add, ALU.bypass)
                link(dve.tensor_copy(k_int[:, :], n))
                ts(k_int[:, :], k_int[:, :], 23, None, ALU.logical_shift_left, ALU.bypass)
                tt(o, p, k_int[:, :].bitcast(F32), ALU.mult)

            def cmul(outs, a, b, t0, t1):
                tt(t0, a[0], b[0], ALU.mult)
                tt(t1, a[1], b[1], ALU.mult)
                tt(outs[0], t0, t1, ALU.subtract)
                tt(t0, a[0], b[1], ALU.mult)
                tt(t1, a[1], b[0], ALU.mult)
                tt(outs[1], t0, t1, ALU.add)

            dve.wait_ge(small_landed, 32)
            exponential(sm("dt"), sm("ldt"))
            tt(sm("t0"), sm("lr"), sm("dt"), ALU.mult)
            exponential(sm("mag"), sm("t0"))
            tt(sm("ang"), sm("li"), sm("dt"), ALU.mult)
            link(dve.tensor_copy(sm("r"), sm("ang")))
            reduce_angle(sm("r"), sm("k"))
            clamp(sm("r"), 3)
            dve.wait_ge(sine_ready, 3)
            quarter_turn(sm("r"), sm("k"))
            clamp(sm("r"), 4)
            dve.wait_ge(sine_ready, 4)
            tt(sm("ar"), sm("mag"), sm("cs"), ALU.mult)
            tt(sm("ai"), sm("mag"), sm("sn"), ALU.mult)
            tt(sm("t0"), sm("lr"), sm("lr"), ALU.mult)
            tt(sm("t1"), sm("li"), sm("li"), ALU.mult)
            tt(sm("den"), sm("t0"), sm("t1"), ALU.add)
            link(dve.reciprocal(sm("den"), sm("den")))
            ts(sm("nr"), sm("ar"), -1.0, None, ALU.add, ALU.bypass)
            tt(sm("t0"), sm("nr"), sm("lr"), ALU.mult)
            tt(sm("t1"), sm("ai"), sm("li"), ALU.mult)
            tt(sm("t0"), sm("t0"), sm("t1"), ALU.add)
            tt(sm("zr"), sm("t0"), sm("den"), ALU.mult)
            tt(sm("t0"), sm("ai"), sm("lr"), ALU.mult)
            tt(sm("t1"), sm("nr"), sm("li"), ALU.mult)
            tt(sm("t0"), sm("t0"), sm("t1"), ALU.subtract)
            tt(sm("zi"), sm("t0"), sm("den"), ALU.mult)
            a = {1: (sm("ar"), sm("ai"))}
            for k in (2, 3, 4):
                a[k] = (sm(f"a{k}r"), sm(f"a{k}i"))
                cmul(a[k], a[k - 1], a[1], sm("t0"), sm("t1"))
            tt(sm("m4"), sm("mag"), sm("mag"), ALU.mult)
            tt(sm("m4"), sm("m4"), sm("m4"), ALU.mult)
            w = {1: (sm("cs"), sm("sn"))}
            for k in (2, 4, 8, 16, 32, 64, 128, 256):
                w[k] = (sm(f"w{k}r"), sm(f"w{k}i"))
                cmul(w[k], w[k // 2], w[k // 2], sm("t0"), sm("t1"))
                tt(sm("t0"), w[k][0], w[k][0], ALU.mult)
                tt(sm("t1"), w[k][1], w[k][1], ALU.mult)
                tt(sm("t0"), sm("t0"), sm("t1"), ALU.add)
                ts(sm("t0"), sm("t0"), -0.5, 1.5, ALU.mult, ALU.add)
                tt(w[k][0], w[k][0], sm("t0"), ALU.mult)
                tt(w[k][1], w[k][1], sm("t0"), ALU.mult)

            dve.wait_ge(c_squared, KQ)
            tt(c_sq[:, 0, :], c_sq[:, 0, :], c_sq[:, 1, :], ALU.add)
            dve.tensor_tensor(c_sq[:, 0, :], c_sq[:, 0, :], c_sq[:, 2, :], ALU.add).then_inc(c_sums, 1)
            dve.wait_ge(c_squared, KQ + KKV)
            dve.tensor_tensor(c_sq[:, KQ, :], c_sq[:, KQ, :], c_sq[:, KQ + 1, :], ALU.add).then_inc(c_sums, 1)

            def rotate(bank):
                tt(rot_a[:, :], ps[:, bank, :], cos_t[:, :], ALU.mult)
                tt(rot_b[0:64, :], ps[64:P, bank, :], sin_t[64:P, :], ALU.mult)
                tt(rot_b[64:P, :], ps[0:64, bank, :], sin_t[0:64, :], ALU.mult)

            dve.wait_ge(chunks_multiplied, END[("kr", 0)])
            rotate(5)
            dve.tensor_tensor(rot_a[:, :], rot_a[:, :], rot_b[:, :], ALU.add).then_inc(kr_ready, 1)
            dve.wait_ge(kr_ready, 1)
            for e, col in enumerate((V_EVEN, V_ODD)):
                dve.tensor_scalar(rot_p[:, e, :], rot_a[:, :], vec[:, col:col + 1], None, ALU.mult, ALU.bypass
                                  ).then_inc(kr_ready, 1)
            dve.wait_ge(kr_rounded, 1)
            dve.wait_ge(kr_ready, 3)
            dve.tensor_tensor(kr_lo[:, :, :], rot_p[:, :, :], kr_hi[:, :, :].bitcast(F32), ALU.subtract).then_inc(kr_split, 1)

            dve.wait_ge(c_totals, 1)
            for b, count in enumerate((RQ, RKV)):
                dve.tensor_scalar(r_bc[:, b, :], ps[:, b, :], 1.0 / count, EPS, ALU.mult, ALU.add).then_inc(c_ms, 1)
            dve.wait_ge(c_rms, 1)
            link(dve.reciprocal(r_bc[:, :, :], r_bc[:, :, :]))
            dve.wait_ge(c_copied, KQ + KKV)
            for j in range(KQ + KKV):
                dve.scalar_tensor_tensor(out=c_raw[:, j, :], in0=c_raw[:, j, :], scalar=vec[:, V_QN + j:V_QN + j + 1],
                                         in1=r_bc[:, int(j >= KQ), :], op0=ALU.mult, op1=ALU.mult).then_inc(cn_ready, 1)
            for j in range(KQ + KKV):
                dve.wait_ge(cn_rounded, j + 1)
                dve.tensor_tensor(cn_lo[:, j, :], c_raw[:, j, :], cn_hi[:, j, :].bitcast(F32), ALU.subtract).then_inc(cn_split, 1)
            for t in range(TT):
                dve.wait_ge(v_rounded, t + 1)
                dve.tensor_tensor(v_lo[:, t, :], ps[:, t, :], v_hi[:, t, :].bitcast(F32), ALU.subtract).then_inc(v_split, 1)

            UNITS = HG * TT
            scale = 1.0 / math.sqrt(QK)
            for g in range(2):
                if g:
                    dve.wait_ge(scores_done, UNITS * g)
                for m, bank in enumerate((4, 5)):
                    for e in range(2):
                        dve.wait_ge(q_rounded, HG * g + 2 * m + e + 1)
                        o = (slice(0, NOPE), 2 * m + e, slice(None))
                        dve.scalar_tensor_tensor(out=q_lo[o], in0=ps[e * NOPE:(e + 1) * NOPE, bank, :], scalar=scale,
                                                 in1=q_hi[o].bitcast(F32), op0=ALU.mult, op1=ALU.subtract).then_inc(q_split, 1)
                dve.wait_ge(chunks_multiplied, END[("uq", 3 * g + 2)])
                rotate(2)
                dve.tensor_tensor(rot_a[:, :], rot_a[:, :], rot_b[:, :], ALU.add).then_inc(qr_ready, 1)
                dve.wait_ge(qr_ready, g + 1)
                dve.wait_ge(qr_rounded, g + 1)
                dve.scalar_tensor_tensor(out=qr_lo[:, :], in0=rot_a[:, :], scalar=scale, in1=qr_hi[:, :].bitcast(F32),
                                         op0=ALU.mult, op1=ALU.subtract).then_inc(qr_split, 1)
                for m, bank in enumerate((3, 0)):
                    for e in range(2):
                        dve.wait_ge(k_rounded, HG * g + 2 * m + e + 1)
                        o = (slice(0, NOPE), 2 * m + e, slice(None))
                        dve.tensor_tensor(k_lo[o], ps[e * NOPE:(e + 1) * NOPE, bank, :], k_hi[o].bitcast(F32),
                                          ALU.subtract).then_inc(k_split, 1)

                def split_pair(pair):
                    for e in range(2):
                        dve.wait_ge(at_rounded, HG * g + 2 * pair + e + 1)
                        o = (slice(e * VD, (e + 1) * VD), 2 * g + pair, slice(None))
                        dve.tensor_tensor(at_lo[o], ps[e * VD:(e + 1) * VD, 4 + e, :], at_hi[o].bitcast(F32),
                                          ALU.subtract).then_inc(at_split, 1)

                for t in range(UNITS + 3):
                    if t == 12:
                        split_pair(0)
                    if t < UNITS:
                        i = t % TT
                        n = (i + 1) * P
                        dve.wait_ge(scores_done, UNITS * g + t + 1)
                        own = ps[:, t % 2, i * P:n]
                        tt(own, own, causal[:, :], ALU.add)
                        dve.tensor_reduce(rowst[:, 0, t % 4:t % 4 + 1], ps[:, t % 2, 0:n], AX_X, ALU.max,
                                          negate=True).then_inc(max_ready, 1)
                    if 1 <= t < UNITS + 1:
                        u = t - 1
                        n = (u % TT + 1) * P
                        dve.wait_ge(exp_done, UNITS * g + u + 1)
                        link(dve.reciprocal(rowst[:, 3, u % 4:u % 4 + 1], rowst[:, 1, u % 4:u % 4 + 1]))
                        dve.tensor_scalar(prob[:, u % 2, 0:n], prob[:, u % 2, 0:n], rowst[:, 3, u % 4:u % 4 + 1], None,
                                          ALU.mult, ALU.bypass).then_inc(probs_ready, 1)
                    if 2 <= t < UNITS + 2:
                        u = t - 2
                        i = u % TT
                        o = (slice(None), slice(0, i + 1), slice(i * P, (i + 1) * P))
                        dve.wait_ge(pT_rounded, UNITS * g + u + 1)
                        dve.tensor_tensor(pT_lo[o], ps[:, 2 + u % 2, 0:(i + 1) * P].rearrange("p (j n) -> p j n", n=P),
                                          pT_hi[o].bitcast(F32), ALU.subtract).then_inc(pT_split, 1)
                split_pair(1)

            dve.wait_ge(heads_done, NH)
            dve.wait_ge(bc_landed, 16)

            def wide(v):
                return v.unsqueeze(2).to_broadcast([P, PAIRS, GH])

            b_re, b_im, c_re, c_im = (bc_in[:, n, :, :] for n in range(4))
            t0, t1 = bt[:, 0, :, :], bt[:, 1, :, :]
            cmul((ab[:, SUB - 1, 0, :, :], ab[:, SUB - 1, 1, :, :]), (b_re, b_im), (wide(sm("zr")), wide(sm("zi"))), t0, t1)
            for k in range(1, SUB):
                s = SUB - 1 - k
                cmul((ab[:, s, 0, :, :], ab[:, s, 1, :, :]), (ab[:, s + 1, 0, :, :], ab[:, s + 1, 1, :, :]),
                     (wide(a[1][0]), wide(a[1][1])), t0, t1)
            link(dve.tensor_copy(ca[:, 0, 0, :, :], c_re))
            ts(ca[:, 0, 1, :, :], c_im, -1.0, None, ALU.mult, ALU.bypass)
            for k in range(1, SUB + 1):
                ar, ai = wide(a[k][0]), wide(a[k][1])
                tt(t0, c_re, ar, ALU.mult)
                tt(t1, c_im, ai, ALU.mult)
                tt(ca[:, k, 0, :, :], t0, t1, ALU.subtract)
                tt(t0, c_re, ai, ALU.mult)
                tt(t1, c_im, ar, ALU.mult)
                stt(ca[:, k, 1, :, :], t0, -1.0, t1, ALU.mult, ALU.subtract)
            link(dve.memset(ba_blk[:, :, :, :, :], 0.0))
            link(dve.memset(ca_blk[:, :, :, :, :], 0.0))
            dve.memset(m_t[:, 0, :], 0.0).then_inc(compacts_ready, 1)
            dve.wait_ge(compacts_ready, 1)
            link(dve.tensor_copy(kn_hi[:, :, :, :].rearrange("p q s h -> p (q s h)"), m_t[:, 0, :]))
            link(dve.tensor_copy(kn_lo[:, :, :, :].rearrange("p q s h -> p (q s h)"), m_t[:, 0, :]))

            for j in range(NU):
                dve.wait_ge(u_rounded, SUB * PPT * (j + 1))
                for s in range(SUB):
                    for q in range(PPT):
                        o = (slice(HALF * s, HALF * (s + 1)), j, q, slice(None))
                        ins = dve.tensor_tensor(u_lo[o], ps[HALF * q:HALF * (q + 1), j, s::SUB], u_hi[o].bitcast(F32), ALU.subtract)
                        if s == SUB - 1 and q == PPT - 1:
                            ins.then_inc(u_split, 1)

            link(dve.memset(rot_c[:, :, 0:1], 1.0))
            link(dve.memset(rot_s[:, :, 0:1], 0.0))
            m = 1
            while m < NC:
                wr, wi = (v.unsqueeze(2).to_broadcast([P, PAIRS, m]) for v in w[SUB * m])
                s0, s1 = (rt[:, c, 0:PAIRS * m].rearrange("p (q n) -> p q n", q=PAIRS) for c in range(2))
                cmul((rot_c[:, :, m:2 * m], rot_s[:, :, m:2 * m]), (rot_c[:, :, 0:m], rot_s[:, :, 0:m]), (wr, wi), s0, s1)
                m *= 2
            link(dve.memset(m_t[:, 0, 0:2 * PPT], 0.0))
            for t in (s_hi, s_lo):
                link(dve.tensor_copy(t[:, :, :, 0:1], m_t[:, 0, 0:2 * PPT].rearrange("p (c q n) -> p c q n", c=2, n=1)))

            for it in range(NU):
                pr = slice(it * PPT, (it + 1) * PPT)
                for c in range(2):
                    dve.wait_ge(mats_rounded, 8 * it + c + 1)
                    link(dve.tensor_tensor(ca_lo[:, c, :, :, :], ca_blk[:, c, :, 1:SUB + 1, :], ca_hi[:, c, :, :, :].bitcast(F32),
                                           ALU.subtract))
                for c in range(2):
                    dve.wait_ge(mats_rounded, 8 * it + c + 3)
                    ins = dve.tensor_tensor(ba_lo[:, c, :, :], ps[:, c, :].rearrange("p (q n) -> p q n", q=PPT),
                                            ba_hi[:, c, :, :].bitcast(F32), ALU.subtract)
                    if c:
                        ins.then_inc(mats_split, 1)
                eye = ident[0:HALF, 0:HALF].unsqueeze(1).to_broadcast([HALF, PPT, HALF])
                dd = d_skip[:, pr].unsqueeze(2).to_broadcast([HALF, PPT, HALF])
                dt_ = m_t[0:HALF, 0, 0:PPT * HALF].rearrange("p (q h) -> p q h", q=PPT)
                tt(dt_, eye, dd, ALU.mult)
                dve.wait_ge(kn_done, it + 1)
                own = ps[0:HALF, 2, :].rearrange("p (q t h) -> p q t h", q=PPT, t=SUB)
                dve.tensor_tensor(own[:, :, 0, :], own[:, :, 0, :], dt_, ALU.add).then_inc(skip_added, 1)
                link(dve.tensor_copy(decay[:, :, :], sm("m4")[:, pr].unsqueeze(2).to_broadcast([P, PPT, NC])))
                link(dve.memset(decay[:, :, 0:1], 0.0))
                dve.wait_ge(mats_rounded, 8 * (it + 1))
                for s in range(SUB):
                    o = (slice(HALF * s, HALF * (s + 1)), slice(None), slice(s, SUB), slice(None))
                    dve.tensor_tensor(kn_lo[o], own[:, :, 0:SUB - s, :], kn_hi[o].bitcast(F32), ALU.subtract
                                      ).then_inc(mats_split if s == SUB - 1 else dve_step, 1)
                steps[0] += SUB - 1
                dve.wait_ge(bu_done, it + 1)
                rc, rs = (r[:, pr, :].rearrange("p q n -> p (q n)") for r in (rot_c, rot_s))
                br, bi = ps[:, 3, :], ps[:, 4, :]
                zr, zi, mr, mi = z_t[:, 0, :], z_t[:, 1, :], m_t[:, 0, :], m_t[:, 1, :]
                if it:
                    dve.wait_ge(states_rounded, it)
                tt(zr, br, rc, ALU.mult)
                tt(mr, bi, rs, ALU.mult)
                tt(zr, zr, mr, ALU.add)
                tt(zi, bi, rc, ALU.mult)
                tt(mr, br, rs, ALU.mult)
                tt(zi, zi, mr, ALU.subtract)
                dec = decay[:, :, :].rearrange("p q n -> p (q n)")
                link(dve.tensor_tensor_scan(mr, dec, zr, 0.0, ALU.mult, ALU.add))
                link(dve.tensor_tensor_scan(mi, dec, zi, 0.0, ALU.mult, ALU.add))
                tt(dec, mi, rs, ALU.mult)
                tt(zr, mr, rc, ALU.mult)
                tt(zr, zr, dec, ALU.subtract)
                tt(dec, mr, rs, ALU.mult)
                tt(zi, mi, rc, ALU.mult)
                dve.tensor_tensor(zi, zi, dec, ALU.add).then_inc(states_ready, 1)
                dve.wait_ge(states_ready, it + 1)
                dve.wait_ge(states_rounded, it + 1)
                dve.tensor_tensor(s_lo[:, :, :, 1:NC], z_t[:, :, :].rearrange("p c (q n) -> p c q n", q=PPT)[:, :, :, 0:NC - 1],
                                  s_hi[:, :, :, 1:NC].bitcast(F32), ALU.subtract).then_inc(states_split, 1)

            for j in range(NU):
                dve.wait_ge(y_rounded, j + 1)
                dve.tensor_tensor(y_lo[:, j, :], y_f[j][:, :], y_hi[:, j, :].bitcast(F32), ALU.subtract).then_inc(y_split, 1)
            for m in range(NU):
                dve.wait_ge(glu_tanh, m + 1)
                dve.scalar_tensor_tensor(out=glu_y[:, m % 2, :], in0=glu_t[:, m % 2, :], scalar=1.0, in1=y_f[m][:, :],
                                         op0=ALU.add, op1=ALU.mult).then_inc(glu_ready, 1)
                dve.wait_ge(ss_rounded, m + 1)
                dve.scalar_tensor_tensor(out=ss_lo[:, m, :], in0=glu_y[:, m % 2, :], scalar=0.5, in1=ss_hi[:, m, :].bitcast(F32),
                                         op0=ALU.mult, op1=ALU.subtract).then_inc(ss_split, 1)
            for m in range(KD):
                b = 2 * (m % 2)
                ta, tb = mg_t[:, m % 2, 0, :], mg_t[:, m % 2, 1, :]
                dve.wait_ge(chunks_multiplied, END[("attn_out", m)])
                stt(ta, gates[:, m, :], 1.0, ps[:, b, :], ALU.add, ALU.mult)
                dve.wait_ge(chunks_multiplied, END[("ssm_out", m)])
                stt(tb, gates[:, KD + m, :], 1.0, ps[:, b + 1, :], ALU.add, ALU.mult)
                dve.tensor_tensor(ta, ta, tb, ALU.add).then_inc(mg_ready, 1)
                dve.wait_ge(mg_rounded, m + 1)
                dve.scalar_tensor_tensor(out=mg_lo[:, m, :], in0=ta, scalar=0.5, in1=mg_hi[:, m, :].bitcast(F32),
                                         op0=ALU.mult, op1=ALU.subtract).then_inc(mg_split, 1)

            dve.wait_ge(x1_landed, 16 * TT)
            dve.wait_ge(gmid_landed, 32)
            for t in range(TT):
                n = POST + 2 * t
                tokens_ready(dve, POST + t)
                rsqrt_mean(n, D)
                if t >= 2:
                    dve.wait_ge(x_transposed, TT + t - 1)
                stt(xn2[:, t % 2, :], token_bank(t), st(3, n), g_mix_post[:, :],
                    ALU.mult, ALU.mult)
                dve.tensor_tensor(x1[:, t, :], x1[:, t, :], xn2[:, t % 2, :], ALU.add).then_inc(x1_ready, 1)
                rsqrt_mean(n + 1, D)
                dve.scalar_tensor_tensor(out=xn2[:, t % 2, :], in0=x1[:, t, :], scalar=st(3, n + 1), in1=g_ffn_pre[:, :],
                                         op0=ALU.mult, op1=ALU.mult).then_inc(xn_ready, 1)
                if t:
                    split_xT(TT + t - 1)
            split_xT(2 * TT - 1)

            def taps(i, b, v, f):
                q = 2 * b + v
                o, z = conv[:, b, v, :], ps[:, 2 * b + v, :]
                dve.wait_ge(conv_begun, 4 * i + (q + 1))
                dve.scalar_tensor_tensor(out=o[:, 1:L], in0=z[:, 0:L - 1], scalar=cv(1, v, f), in1=o[:, 1:L],
                                         op0=ALU.mult, op1=ALU.add).then_inc(conv_step, 1)
                dve.wait_ge(conv_step, 4 * i + (q + 1))
                dve.scalar_tensor_tensor(out=o[:, 2:L], in0=z[:, 0:L - 2], scalar=cv(0, v, f), in1=o[:, 2:L],
                                         op0=ALU.mult, op1=ALU.add).then_inc(conv_done, 1)

            def up_pair(i, b, f):
                taps(i, b, 0, f)
                taps(i, b, 1, f)
                dve.wait_ge(conv_done, 4 * i + (2 * b + 2))
                dve.wait_ge(gelu_done, 2 * i + (b + 1))
                dve.tensor_tensor(ff_tile(f), gelu[:, b, :], conv[:, b, 1, :], ALU.mult).then_inc(ff_ready, 1)

            for b in range(2):
                up_pair(0, b, b)
            with dve.Fori(1, NF // 2) as i:
                for b in range(2):
                    up_pair(i, b, 2 * i + b)

            def ff_low(i, b, f):
                dve.wait_ge(ff_rounded, 2 * i + (b + 1))
                dve.tensor_tensor(ff_lo[b][:, :], ff_tile(f), ff_hi[b][:, :].bitcast(F32), ALU.subtract).then_inc(ff_split, 1)

            for b in range(2):
                ff_low(0, b, b)
            with dve.Fori(1, NF // 2) as i:
                for b in range(2):
                    ff_low(i, b, 2 * i + b)

            dve.wait_ge(gpost_landed, 16)
            for t in range(TT):
                n = FPOST + t
                tokens_ready(dve, n)
                rsqrt_mean(n, D)
                normed = conv[:, t % 2, :, :].rearrange("p b n -> p (b n)")
                stt(normed, token_bank(t), st(3, n), g_ffn_post[:, :], ALU.mult, ALU.mult)
                dve.tensor_tensor(x1[:, t, :], x1[:, t, :], normed, ALU.add).then_inc(out_ready, 1)


_OUT = (1, L, D)


def _columns():
    r = np.arange(P)
    cols = {}
    for j in range(KQ):
        cols[("cq", j)] = ("w_in", O_CQ + j * P + r)
    for j in range(KKV):
        cols[("ckv", j)] = ("w_in", O_CKV + j * P + r)
    half = ROPE // 2
    cols[("kr", 0)] = ("w_in", O_KR + np.concatenate([np.tile(np.arange(half), 4), np.tile(half + np.arange(half), 4)]))
    for n in range(NG):
        cols[("gate", n)] = ("w_in", O_GATE + n * P + r)
    for j in range(NU):
        cols[("u", j)] = ("w_in", O_U + j * P + r)
    for g in range(2):
        heads = [HG * g + h for h in range(HG)]
        for m in range(2):
            cols[("uq", 3 * g + m)] = ("w_uq", np.concatenate([h * QK + np.arange(NOPE) for h in heads[2 * m:2 * m + 2]]))
        cols[("uq", 3 * g + 2)] = ("w_uq", np.concatenate(
            [h * QK + NOPE + c * half + np.arange(half) for c in range(2) for h in heads]))
    for m in range(NU):
        cols[("glu", m)] = ("w_glu", m * P + r)
    for m in range(KD):
        cols[("attn_out", m)] = ("w_branch_attn", m * P + r)
        cols[("ssm_out", m)] = ("w_branch_ssm", m * P + r)
    for f in range(2 * NF):
        cols[("up", f)] = ("w_up", f * P + r)
    return cols


def _lay_out_stream(w):
    stream = np.zeros((NCHUNK, P, CH), np.float32)
    cols = _columns()
    tiles = CH // P
    for n, (name, part) in enumerate(ORDER):
        kind, j = name
        if name in cols:
            mat, c = cols[name]
            block = w[mat][part * CH:(part + 1) * CH][:, c]
            k = block.shape[0] // P
            stream[n, :, :k * P] = block.reshape(k, P, P).transpose(1, 0, 2).reshape(P, k * P)
        elif kind == "uk":
            block = w["w_uk"][:, j * HG * NOPE:(j + 1) * HG * NOPE]
            stream[n] = block.reshape(KKV, P, tiles // KKV, P).transpose(1, 2, 0, 3).reshape(P, CH)
        elif kind == "uv":
            stream[n] = w["w_uv"][part * P:(part + 1) * P]
        else:
            mat = w[{"w_out": "w_out", "down": "w_down"}[kind]]
            stream[n] = mat[j * P:(j + 1) * P, part * CH:(part + 1) * CH]
    return stream


def kernel(**inputs):
    import concourse.bacc as bacc
    from concourse.bass_utils import run_bass_kernel_spmd as run

    a = {name: np.asarray(v) for name, v in inputs.items()}
    w = {name: a[name][0] for name in ("w_in", "w_uq", "w_uk", "w_uv", "w_glu", "w_branch_attn", "w_branch_ssm",
                                       "w_out", "w_up", "w_down")}

    def tiles(v):
        return v.reshape(-1, P).T

    rows = np.arange(P)
    inv = (np.float32(10000.0) ** (-np.arange(0, ROPE, 2, dtype=np.float32) / np.float32(ROPE))).astype(np.float32)
    shape_columns = np.stack([inv[rows % (ROPE // 2)], (rows % ROPE < ROPE // 2), (rows % ROPE >= ROPE // 2),
                              np.where(rows < P // 2, 1.0, -1.0)], axis=1).astype(np.float32)
    conv_rows = np.concatenate([a["conv_w"][0], a["conv_b"]], axis=0)
    vecs = np.concatenate([tiles(a["q_norm"][0]), tiles(a["kv_norm"][0]), tiles(a["b_gate"][0]), tiles(a["b_glu"][0]),
                           shape_columns, tiles(conv_rows)], axis=1)
    norms = np.concatenate([a["mix_norm_pre"], a["mix_norm_post"], a["ffn_norm_pre"], a["ffn_norm_post"]], axis=0)

    def states(v):
        v = v.reshape(PAIRS, 2, NS, *v.shape[2:])
        return np.moveaxis(v, 0, 2).reshape(P, PAIRS, *v.shape[3:])

    ldt = np.broadcast_to(a["ssm_log_dt"][0][:, None], (GROUPS, NS))
    ssm_small = np.stack([states(a["ssm_lambda_re"][0]), states(a["ssm_lambda_im"][0]), states(ldt)], axis=1)
    ssm_bc = np.stack([states(a["ssm_b_re"][0]), states(a["ssm_b_im"][0]),
                       states(a["ssm_c_re"][0].transpose(0, 2, 1)), states(a["ssm_c_im"][0].transpose(0, 2, 1))], axis=1)
    ssm_d = a["ssm_d"][0].reshape(PAIRS, HALF).T

    nc = bacc.Bacc("TRN2", target_bir_lowering=False, num_devices=1)
    arrays = {"w_stream": _lay_out_stream(w), "x": a["x"][0], "positions": a["positions"], "vecs": vecs, "norms": norms,
              "ssm_small": ssm_small, "ssm_bc": ssm_bc, "ssm_d": ssm_d}
    arrays = {f"in_{n}_dram": np.ascontiguousarray(v) for n, v in arrays.items()}
    args = [nc.dram_tensor(n, v.shape, mybir.dt.from_np(v.dtype), kind="ExternalInput").ap() for n, v in arrays.items()]
    out = nc.dram_tensor("out_0_dram", _OUT, F32, kind="ExternalOutput").ap()
    build(nc, *args, out.rearrange("a l d -> (a l) d"))
    result = run(nc, [arrays], core_ids=[0])
    return result.results[0]["out_0_dram"]
```

```python
from contextlib import ExitStack
import math

import numpy as np

import concourse.bass as bass
from concourse import mybir
from concourse.alu_op_type import AluOpType as ALU

ACT = mybir.ActivationFunctionType
F32 = mybir.dt.float32
F32R = mybir.dt.float32r
I32 = mybir.dt.int32
AX_X = mybir.AxisListType.X

P = 128
D = 1024
L = 512
NH = 8
NOPE = 64
ROPE = 32
QK = NOPE + ROPE
VD = 64
RQ = 384
RKV = 256
WS = 512
GROUPS = 32
GH = 16
NS = 64
FF = 2816
EPS = 1e-6
TT = L // P
KD = D // P
KQ = RQ // P
KKV = RKV // P
NG = 2 * D // P
NF = FF // P
NU = WS // P
HG = NH // 2
CH = 512
RING = 4
HALF = 2 * GH

PAIRS = GROUPS // 2
SUB = 4
NC = L // SUB
PPT = 4

O_CQ, O_CKV, O_KR, O_U, O_GATE = 0, RQ, RQ + RKV, RQ + RKV + ROPE, RQ + RKV + ROPE + WS

ROUND = 12582912.0
TWO_PI = (6.28125, 0.001934051513671875, 2 * math.pi - 6.28125 - 0.001934051513671875)
PI_IN = 3.1415925
LN2 = (0.693359375, math.log(2) - 0.693359375)
EXP_TAYLOR = [1 / math.factorial(n) for n in range(8)]
MASKED = -3.0e38

GATES_FIRST = 3
GATES_SSM = (3, 2, 2, 1)
GATES_ATTN = (1, 2)
GATE_STEPS = ((1, 3), (1, 5, 9, 17))
Y_STEPS = (3, 7, 11, 15)
V_BANK = (0, 1, 3, 4)
KROPE_DMAS, QROPE_DMAS = 4, 8


def stream_plan():
    order = []
    gate = [0]

    def add(name, parts):
        order.extend((name, i) for i in range(parts))

    def gates(n):
        for _ in range(n):
            add(("gate", gate[0]), 2)
            gate[0] += 1

    for j in range(NU):
        add(("u", j), 2)
    for j in range(KQ):
        add(("cq", j), 2)
    for j in range(KKV):
        add(("ckv", j), 2)
    add(("kr", 0), 2)
    gates(GATES_FIRST)
    for n in GATES_SSM:
        gates(n)
    add(("uv", 0), KKV)
    for g in range(2):
        add(("uq", 3 * g + 2), 1)
        gates(1)
        add(("uq", 3 * g), 1)
        add(("uq", 3 * g + 1), 1)
        add(("uk", g), 1)
        gates(GATES_ATTN[g])
    assert gate[0] == NG
    for m in range(NU):
        add(("glu", m), 1)
    for m in range(KD):
        add(("attn_out", m), 1)
        add(("ssm_out", m), 1)
    for j in range(KD):
        add(("w_out", j), 2)
    for f in range(NF):
        add(("up", f), 2)
        add(("up", NF + f), 2)
    for f in range(NF):
        add(("down", f), 2)
    first, end = {}, {}
    for n, (name, _) in enumerate(order):
        first.setdefault(name, n)
        end[name] = n + 1
    return order, first, end


ORDER, FIRST, END = stream_plan()
NCHUNK = len(ORDER)

V_QN, V_KVN = 0, KQ
V_BG = V_KVN + KKV
V_BGLU = V_BG + NG
V_INV = V_BGLU + NU
V_EVEN, V_ODD, V_SIGN = V_INV + 1, V_INV + 2, V_INV + 3
V_CONV = V_SIGN + 1
NV = V_CONV + 4 * 2 * NF

S_NAMES = ["lr", "li", "ldt", "dt", "y", "n", "r", "p", "mag", "ang", "k", "sn", "cs", "ar", "ai",
           "den", "nr", "t0", "t1", "t2", "zr", "zi", "m4"]
S_NAMES += [f"a{k}{c}" for k in (2, 3, 4) for c in "ri"]
S_NAMES += [f"w{k}{c}" for k in (1, 2, 4, 8, 16, 32, 64, 128, 256) for c in "ri"]
SI = {n: i for i, n in enumerate(S_NAMES)}

KB = 1024
BASE = 16512


def build(nc, w_stream, x, positions, vecs, norms, ssm_small, ssm_bc, ssm_d, out):
    x_t = x.rearrange("(t p) d -> t p d", p=P)
    out_t = out.rearrange("(t p) d -> t p d", p=P)
    ctx = ExitStack()
    with ctx:
        def at(name, offset, shape, dt=F32):
            return nc.alloc_sbuf_tensor_at(name, shape, dt, offset=BASE + offset)

        raw = at("raw", 0, [P, RING, CH])
        w_hi = at("w_hi", 8 * KB, [P, RING, CH], F32R)
        w_lo = at("w_lo", 16 * KB, [P, RING, CH], F32R)
        xT_hi = at("xT_hi", 24 * KB, [P, KD, L], F32R)
        xT_lo = at("xT_lo", 40 * KB, [P, KD, L], F32R)
        ident = at("ident", 56 * KB, [P, P])
        causal = at("causal", 56 * KB + 512, [P, P])
        ones = at("ones", 57 * KB, [P, P])
        vec = at("vec", 57 * KB + 512, [P, NV])
        stat = at("stat", 58 * KB + 576, [P, 4, 4 * TT])
        rowst = at("rowst", 58 * KB + 832, [P, 4, 4])
        small = at("small", 58 * KB + 896, [P, len(S_NAMES), PAIRS])
        k_int = at("k_int", 62 * KB, [P, PAIRS], I32)
        d_skip = at("d_skip", 62 * KB + 64, [HALF, PAIRS])
        hb_gate = at("hb_gate", 62 * KB + 128, [P, NG])
        hb_glu = at("hb_glu", 62 * KB + 192, [P, NU])
        R = 62 * KB + 256

        def reg(name, kb, shape, dt=F32):
            return at(name, R + int(kb * KB), shape, dt)

        x_sq = reg("x_sq", 0, [P, 2, D])
        x_in = reg("x_in", 20, [P, TT, D])
        xn = reg("xn", 36, [P, 2, D])
        g_mix_pre = reg("g_mix_pre", 44, [P, D])
        gates = reg("gates", 113, [P, NG, L])
        c_raw = reg("c_raw", 121, [P, KQ + KKV, L])
        r_bc = reg("r_bc", 131, [P, 2, L])
        kr_f = reg("kr_f", 139, [P, L])
        cos_t = reg("cos_t", 141, [P, L])
        sin_t = reg("sin_t", 143, [P, L])
        c_sq = reg("c_sq", 10, [P, KQ + KKV, L])
        cn_hi = reg("cn_hi", 0, [P, KQ + KKV, L], F32R)
        cn_lo = reg("cn_lo", 10, [P, KQ + KKV, L], F32R)
        rot_a = reg("rot_a", 80, [P, L])
        rot_b = reg("rot_b", 82, [P, L])
        ang = reg("ang", 87, [P, L])
        ang_k = reg("ang_k", 89, [P, L])
        pos_i = reg("pos_i", 91, [P, L], I32)
        u_hi = reg("u_hi", 20, [P, NU, PPT, NC], F32R)
        u_lo = reg("u_lo", 28, [P, NU, PPT, NC], F32R)
        rot_c = reg("rot_c", 36, [P, PAIRS, NC])
        rot_s = reg("rot_s", 44, [P, PAIRS, NC])
        ab = reg("ab", 52, [P, SUB, 2, PAIRS, GH])
        ca = reg("ca", 60, [P, SUB + 1, 2, PAIRS, GH])
        ba_blk = reg("ba_blk", 70, [P, 2, PPT, SUB, HALF])
        ca_blk = reg("ca_blk", 74, [P, 2, PPT, SUB + 1, HALF])
        ba_hi = reg("ba_hi", 79, [P, 2, PPT, P], F32R)
        ba_lo = reg("ba_lo", 83, [P, 2, PPT, P], F32R)
        ca_hi = reg("ca_hi", 87, [P, 2, PPT, SUB, HALF], F32R)
        ca_lo = reg("ca_lo", 91, [P, 2, PPT, SUB, HALF], F32R)
        kn_hi = reg("kn_hi", 95, [P, PPT, SUB, HALF], F32R)
        kn_lo = reg("kn_lo", 97, [P, PPT, SUB, HALF], F32R)
        z_t = reg("z_t", 99, [P, 2, L])
        m_t = reg("m_t", 103, [P, 2, L])
        s_hi = reg("s_hi", 107, [P, 2, PPT, NC], F32R)
        s_lo = reg("s_lo", 135, [P, 2, PPT, NC], F32R)
        decay = reg("decay", 111, [P, PPT, NC])
        bc_in = reg("bc_in", 103, [P, 4, PAIRS, GH])
        bt = reg("bt", 107, [P, 2, PAIRS, GH])
        rt = reg("rt", 0, [P, 2, PAIRS * NC // 2])
        y_f = [reg(f"y_f{i}", 20 + 2 * i, [P, L]) for i in range(NU)]
        q_hl = reg("q_hl", 28, [P, 2, HG, L], F32R)
        k_hl = reg("k_hl", 44, [P, 2, HG, L], F32R)
        q_hi, q_lo, k_hi, k_lo = q_hl[:, 0], q_hl[:, 1], k_hl[:, 0], k_hl[:, 1]
        v_hi = reg("v_hi", 60, [P, TT, L], F32R)
        v_lo = reg("v_lo", 68, [P, TT, L], F32R)
        pT_hi = reg("pT_hi", 76, [P, TT, L], F32R)
        pT_lo = reg("pT_lo", 84, [P, TT, L], F32R)
        qr_hl = reg("qr_hl", 76, [P, 2, L], F32R)
        prob = reg("prob", 92, [P, 2, L])
        at_f = reg("at_f", 96, [P, NU, L])
        kr_hl = reg("kr_hl", 104, [P, 2, 2, L], F32R)
        y_hi = reg("y_hi", 0, [P, NU, L], F32R)
        y_lo = reg("y_lo", 8, [P, NU, L], F32R)
        at_hi = reg("at_hi", 28, [P, NU, L], F32R)
        at_lo = reg("at_lo", 36, [P, NU, L], F32R)
        glu_t = reg("glu_t", 44, [P, 2, L])
        glu_y = reg("glu_y", 48, [P, 2, L])
        ss_hi = reg("ss_hi", 52, [P, NU, L], F32R)
        ss_lo = reg("ss_lo", 60, [P, NU, L], F32R)
        mg_hi = reg("mg_hi", 68, [P, KD, L], F32R)
        mg_lo = reg("mg_lo", 84, [P, KD, L], F32R)
        mg_t = reg("mg_t", 100, [P, 2, 2, L])
        x1 = reg("x1", 0, [P, TT, D])
        g_mix_post = reg("g_mix_post", 16, [P, D])
        g_ffn_pre = reg("g_ffn_pre", 20, [P, D])
        xn2 = reg("xn2", 24, [P, 2, D])
        sq = reg("sq", 32, [P, D])
        ff = reg("ff", 36, [P, NF, L])
        g_ffn_post = reg("g_ffn_post", 16, [P, D])
        conv = reg("conv", 80, [P, 2, 2, L])
        gelu = reg("gelu", 88, [P, 2, L])
        ff_hi = [reg(f"ff_hi{i}", 92 + 4 * i, [P, L], F32R) for i in range(2)]
        ff_lo = [reg(f"ff_lo{i}", 94 + 4 * i, [P, L], F32R) for i in range(2)]

        ps = ctx.enter_context(nc.psum_tensor("ps", [P, 8, L], F32))

        def sem(name):
            return ctx.enter_context(nc.semaphore(name))

        x_landed = [sem(f"x_landed{t}") for t in range(TT)]
        raw_landed = [sem(f"raw_landed{s}") for s in range(RING)]
        (g_landed, vec_landed, pos_landed, small_landed, bc_landed, x1_landed, gmid_landed,
         gpost_landed, krope_landed, qrope_landed, out_written) = [sem(n) for n in (
             "g_landed", "vec_landed", "pos_landed", "small_landed", "bc_landed", "x1_landed",
             "gmid_landed", "gpost_landed", "krope_landed", "qrope_landed", "out_written")]
        consts_ready = sem("consts_ready")
        weights_hi, weights_split, chunks_multiplied = sem("weights_hi"), sem("weights_split"), sem("chunks_multiplied")
        dve_step = sem("dve_step")
        sq_summed, ms_ready, rms_ready, xn_ready = sem("sq_summed"), sem("ms_ready"), sem("rms_ready"), sem("xn_ready")
        x_transposed, xT_rounded, xT_split = sem("x_transposed"), sem("xT_rounded"), sem("xT_split")
        x1_ready = sem("x1_ready")
        c_copied, c_squared, c_sums, c_totals = sem("c_copied"), sem("c_squared"), sem("c_sums"), sem("c_totals")
        c_ms, c_rms, cn_ready, cn_rounded, cn_split = (
            sem("c_ms"), sem("c_rms"), sem("cn_ready"), sem("cn_rounded"), sem("cn_split"))
        angle_ready, sine_ready = sem("angle_ready"), sem("sine_ready")
        kr_ready, kr_rounded, kr_split = sem("kr_ready"), sem("kr_rounded"), sem("kr_split")
        gate_done = sem("gate_done")
        v_rounded, v_split = sem("v_rounded"), sem("v_split")
        q_rounded, q_split, k_rounded, k_split = sem("q_rounded"), sem("q_split"), sem("k_rounded"), sem("k_split")
        qr_ready, qr_rounded, qr_split = sem("qr_ready"), sem("qr_rounded"), sem("qr_split")
        scores_done, max_ready, exp_done, probs_ready = sem("scores_done"), sem("max_ready"), sem("exp_done"), sem("probs_ready")
        probs_transposed, pT_rounded, pT_split = sem("probs_transposed"), sem("pT_rounded"), sem("pT_split")
        at_copied = sem("at_copied")
        heads_done, at_rounded, at_split = sem("heads_done"), sem("at_rounded"), sem("at_split")
        u_rounded, u_split = sem("u_rounded"), sem("u_split")
        compacts_ready, blocks_ready, ba_transposed, kn_done = (
            sem("compacts_ready"), sem("blocks_ready"), sem("ba_transposed"), sem("kn_done"))
        skip_added, ba_rounded, ba_split = sem("skip_added"), sem("ba_rounded"), sem("ba_split")
        ca_rounded, ca_split, inputs_read = sem("ca_rounded"), sem("ca_split"), sem("inputs_read")
        bu_done, states_ready, states_rounded, states_split = (
            sem("bu_done"), sem("states_ready"), sem("states_rounded"), sem("states_split"))
        y_summed, y_done, y_rounded, y_split = sem("y_summed"), sem("y_done"), sem("y_rounded"), sem("y_split")
        glu_tanh, glu_ready, ss_rounded, ss_split = sem("glu_tanh"), sem("glu_ready"), sem("ss_rounded"), sem("ss_split")
        mg_ready, mg_rounded, mg_split = sem("mg_ready"), sem("mg_rounded"), sem("mg_split")
        tokens_summed = sem("tokens_summed")
        conv_begun, conv_step, conv_done, gelu_done, ff_ready = (
            sem("conv_begun"), sem("conv_step"), sem("conv_done"), sem("gelu_done"), sem("ff_ready"))
        ff_rounded, ff_split = sem("ff_rounded"), sem("ff_split")
        out_ready = sem("out_ready")

        block = ctx.enter_context(nc.Block())

        PRE, POST, FPRE, FPOST = 0, TT, 2 * TT, 3 * TT

        def st(row, n):
            return stat[:, row, n:n + 1]

        def sm(name):
            return small[:, SI[name], :]

        @block.sync
        def _(sp):
            def load(c, s):
                sp.dma_start(raw[:, s, :], w_stream[bass.ds(c, 1), :, :].rearrange("c p n -> p (c n)")
                             ).then_inc(raw_landed[s], 16)

            for s in range(RING):
                load(s, s)
            whole = NCHUNK // RING
            with sp.Fori(1, whole) as i:
                for s in range(RING):
                    sp.wait_ge(weights_split, RING * i + (s + 1 - RING))
                    load(RING * i + s, s)
            for s in range(NCHUNK % RING):
                sp.wait_ge(weights_split, RING * whole + s + 1 - RING)
                load(RING * whole + s, s)
            for t in range(TT):
                sp.wait_ge(out_ready, t + 1)
                sp.dma_start(out_t[t, :, :], x1[:, t, :]).then_inc(out_written, 16)
            sp.wait_ge(out_written, 16 * TT)

        @block.gpsimd
        def _(pool):
            pool.memset(ident[:, :], 0.0).then_inc(consts_ready, 1)
            pool.memset(causal[:, :], 0.0).then_inc(consts_ready, 1)
            pool.memset(ones[:, :], 1.0).then_inc(consts_ready, 1)
            pool.wait_ge(consts_ready, 3)
            pool.affine_select(out=ident[:, :], in_=ident[:, :], compare_op=ALU.not_equal, fill=1.0,
                               base=0, pattern=[[-1, P]], channel_multiplier=1).then_inc(consts_ready, 1)
            pool.affine_select(out=causal[:, :], in_=causal[:, :], compare_op=ALU.is_ge, fill=MASKED,
                               base=0, pattern=[[-1, P]], channel_multiplier=1).then_inc(consts_ready, 1)

            def split(i, s, first):
                pool.wait_ge(raw_landed[s], 16 * i + 16)
                if not first:
                    pool.wait_ge(chunks_multiplied, RING * i + (s + 1 - RING))
                pool.tensor_tensor(w_hi[:, s, 0:1], raw[:, s, 0:1], ones[:, 0:1], ALU.mult)
                pool.tensor_scalar(w_hi[:, s, 1:CH], raw[:, s, 1:CH], 1.0, 1.0, ALU.mult, ALU.mult).then_inc(weights_hi, 1)
                pool.wait_ge(weights_hi, RING * i + s + 1)
                pool.tensor_tensor(w_lo[:, s, :], raw[:, s, :], w_hi[:, s, :].bitcast(F32),
                                   ALU.subtract).then_inc(weights_split, 1)

            for s in range(RING):
                split(0, s, True)
            whole = NCHUNK // RING
            with pool.Fori(1, whole) as i:
                for s in range(RING):
                    split(i, s, False)
            for s in range(NCHUNK % RING):
                split(whole, s, False)

        @block.tensor
        def _(pe):
            def three(o, wh, wl, xh, xl, start, stop):
                pe.matmul(o, wh, xh, start=start, stop=False, skip_group_check=True)
                pe.matmul(o, wh, xl, start=False, stop=False, skip_group_check=True)
                return pe.matmul(o, wl, xh, start=False, stop=stop, skip_group_check=True)

            def transpose_x(n):
                t = n % TT
                src = xn if n < TT else xn2
                pe.wait_ge(xn_ready, n + 1)
                for k in range(KD):
                    last = pe.transpose(ps[:, 2 * t + k // 4, (k % 4) * P:(k % 4 + 1) * P],
                                        src[:, t % 2, k * P:(k + 1) * P], ident[:, :])
                last.then_inc(x_transposed, 1)

            def chunk(name, part, bank, hi, lo, k0, nk, start, stop):
                c = FIRST[name] + part
                s = c % RING
                pe.wait_ge(weights_split, c + 1)
                for k in range(nk):
                    last = three(ps[:, bank, :], w_hi[:, s, k * P:(k + 1) * P], w_lo[:, s, k * P:(k + 1) * P],
                                 hi[:, k0 + k, :], lo[:, k0 + k, :], start and k == 0, stop and k == nk - 1)
                last.then_inc(chunks_multiplied, 1)

            def in_half(name, part, bank):
                chunk(name, part, bank, xT_hi, xT_lo, 4 * part, 4, part == 0, part == 1)

            def gate_half(n, part):
                if part == 0 and n >= 2:
                    pe.wait_ge(gate_done, n - 1)
                in_half(("gate", n), part, 6 + n % 2)

            def in_tile(name, bank):
                in_half(name, 0, bank)
                in_half(name, 1, bank)

            pe.wait_ge(consts_ready, 5)
            for t in range(TT):
                transpose_x(PRE + t)
            pe.wait_ge(xT_split, 2 * TT)
            for j in range(NU):
                in_tile(("u", j), j)
            for j in range(KQ):
                in_tile(("cq", j), 4 + j)
            in_tile(("ckv", 0), 7)
            pe.wait_ge(u_split, 1)
            in_tile(("ckv", 1), 0)
            pe.wait_ge(u_split, 2)
            in_tile(("kr", 0), 1)

            gate = [0]

            def gate_tiles(n):
                for _ in range(n):
                    gate_half(gate[0], 0)
                    gate_half(gate[0], 1)
                    gate[0] += 1

            pe.wait_ge(c_squared, 4)
            gate_tiles(1)
            pe.wait_ge(c_sums, 2)
            pe.wait_ge(c_copied, KQ + KKV)
            for b, bank in enumerate((5, 0)):
                last = pe.matmul(ps[:, bank, :], ones[:, :], c_sq[:, (0, KQ)[b], :], start=True, stop=True)
            last.then_inc(c_totals, 1)
            gate_tiles(1)

            def system(it):
                pe.wait_ge(blocks_ready, 8 * (it + 1))
                if it == 0:
                    pe.wait_ge(kr_ready, 1)
                    pe.wait_ge(c_ms, 2)
                    pe.wait_ge(u_split, NU)
                else:
                    pe.wait_ge(ba_split, it)
                    pe.wait_ge(ca_split, it)
                for c in range(2):
                    for q in range(PPT):
                        last = pe.transpose(ps[:, c, q * P:(q + 1) * P],
                                            ba_blk[:, c, q, :, :].rearrange("p s h -> p (s h)"), ident[:, :])
                last.then_inc(ba_transposed, 1)
                for q in range(PPT):
                    for c in range(2):
                        last = pe.matmul(ps[0:HALF, 2, q * P:(q + 1) * P], ba_blk[:, c, q, SUB - 1, :],
                                         ca_blk[:, c, q, 0:SUB, :].rearrange("p s h -> p (s h)"),
                                         start=(c == 0), stop=(c == 1), skip_group_check=True)
                last.then_inc(kn_done, 1)

            def state_inputs(it):
                pe.wait_ge(ba_split, it + 1)
                if it:
                    pe.wait_ge(inputs_read, it)
                for c in range(2):
                    for q in range(PPT):
                        last = three(ps[:, 3 + c, q * NC:(q + 1) * NC], ba_hi[:, c, q, :], ba_lo[:, c, q, :],
                                     u_hi[:, it, q, :], u_lo[:, it, q, :], True, True)
                last.then_inc(bu_done, 1)

            def outputs(it):
                pe.wait_ge(ca_split, it + 1)
                pe.wait_ge(states_split, it + 1)
                if it:
                    pe.wait_ge(y_done, SUB * PPT * it)
                for q in range(PPT):
                    o = ps[:, 5, q * NC:(q + 1) * NC]
                    three(o, kn_hi[:, q, :, :].rearrange("p s h -> p (s h)"), kn_lo[:, q, :, :].rearrange("p s h -> p (s h)"),
                          u_hi[:, it, q, :], u_lo[:, it, q, :], True, False)
                    for c in range(2):
                        last = three(o, ca_hi[:, c, q, :, :].rearrange("p s h -> p (s h)"),
                                     ca_lo[:, c, q, :, :].rearrange("p s h -> p (s h)"),
                                     s_hi[:, c, q, :], s_lo[:, c, q, :], False, c == 1)
                last.then_inc(y_summed, 1)

            system(0)
            gate_tiles(GATES_FIRST - 2)
            for it in range(NU):
                state_inputs(it)
                if it:
                    outputs(it - 1)
                if it + 1 < NU:
                    gate_tiles(1)
                    system(it + 1)
                    gate_tiles(GATES_SSM[it] - 1)
                else:
                    gate_tiles(GATES_SSM[it])
            pe.wait_ge(cn_split, KQ + KKV)
            pe.wait_ge(ca_split, NU)
            pe.wait_ge(inputs_read, NU)
            for kk in range(KKV):
                c = FIRST[("uv", 0)] + kk
                s = c % RING
                pe.wait_ge(weights_split, c + 1)
                for t in range(TT):
                    tok = slice(t * P, (t + 1) * P)
                    last = three(ps[:, V_BANK[t], :], cn_hi[:, KQ + kk, tok], cn_lo[:, KQ + kk, tok],
                                 w_hi[:, s, :], w_lo[:, s, :], kk == 0, kk == KKV - 1)
                last.then_inc(chunks_multiplied, 1)
            outputs(NU - 1)

            UNITS = HG * TT
            for g in range(2):
                if g:
                    pe.wait_ge(pT_split, UNITS)
                chunk(("uq", 3 * g + 2), 0, 2, cn_hi, cn_lo, 0, KQ, True, True)
                gate_tiles(1)
                if g == 0:
                    pe.wait_ge(v_split, TT)
                    pe.wait_ge(y_done, SUB * PPT * NU)
                else:
                    pe.wait_ge(at_copied, HG)
                for m, bank in enumerate((4, 5)):
                    chunk(("uq", 3 * g + m), 0, bank, cn_hi, cn_lo, 0, KQ, True, True)
                c = FIRST[("uk", g)]
                s = c % RING
                pe.wait_ge(weights_split, c + 1)
                for m, bank in enumerate((3, 0)):
                    for k in range(KKV):
                        cols = slice((2 * m + k) * P, (2 * m + k + 1) * P)
                        last = three(ps[:, bank, :], w_hi[:, s, cols], w_lo[:, s, cols],
                                     cn_hi[:, KQ + k, :], cn_lo[:, KQ + k, :], k == 0, k == KKV - 1)
                last.then_inc(chunks_multiplied, 1)

                pe.wait_ge(q_split, HG * (g + 1))
                pe.wait_ge(k_split, HG * (g + 1))
                pe.wait_ge(krope_landed, 16 * KROPE_DMAS)
                pe.wait_ge(qrope_landed, 16 * QROPE_DMAS * (g + 1))

                def scores(u):
                    h, i = u // TT, u % TT
                    if u >= 2:
                        pe.wait_ge(exp_done, UNITS * g + u - 1)
                    tok = slice(i * P, (i + 1) * P)
                    n = (i + 1) * P
                    three(ps[:, u % 2, 0:n], q_hi[:, h, tok], q_lo[:, h, tok],
                          k_hi[:, h, 0:n], k_lo[:, h, 0:n], True, True).then_inc(scores_done, 1)

                def turn_probs(u):
                    if u >= 2 or g:
                        pe.wait_ge(pT_split, UNITS * g + u - 1)
                    pe.wait_ge(probs_ready, UNITS * g + u + 1)
                    for j in range(u % TT + 1):
                        last = pe.transpose(ps[:, 2 + u % 2, j * P:(j + 1) * P],
                                            prob[:, u % 2, j * P:(j + 1) * P], ident[:, :])
                    last.then_inc(probs_transposed, 1)

                def values(h):
                    head = HG * g + h
                    pe.wait_ge(pT_split, UNITS * g + TT * (h + 1))
                    if head >= 2:
                        pe.wait_ge(at_copied, 2 * (head // 2))
                    pair = slice((head // 2) * P, (head // 2 + 1) * P)
                    for j in range(TT):
                        last = three(ps[:, 4 + h % 2, j * P:L], v_hi[:, j, pair], v_lo[:, j, pair],
                                     pT_hi[:, j, j * P:L], pT_lo[:, j, j * P:L], j == 0, j == TT - 1)
                    last.then_inc(heads_done, 1)

                half, halves = 0, 2 * GATES_ATTN[g]
                for t in range(UNITS + 3):
                    if t >= 6 and (t - 6) % TT == 0:
                        values((t - 6) // TT)
                    if 2 <= t < UNITS + 2:
                        turn_probs(t - 2)
                    if t < UNITS:
                        scores(t)
                    if half < halves and t in GATE_STEPS[g]:
                        gate_half(gate[0] + half // 2, half % 2)
                        half += 1
                gate[0] += GATES_ATTN[g]

            pe.wait_ge(y_split, NU)
            for m in range(NU):
                chunk(("glu", m), 0, m, y_hi, y_lo, 0, NU, True, True)
            for m in range(KD):
                b = 2 * (m % 2)
                if m >= 2:
                    pe.wait_ge(mg_ready, m - 1)
                else:
                    pe.wait_ge(glu_ready, NU)
                    pe.wait_ge(at_split, NU)
                chunk(("attn_out", m), 0, b, at_hi, at_lo, 0, NU, True, True)
                if m == 0:
                    pe.wait_ge(ss_split, NU)
                chunk(("ssm_out", m), 0, b + 1, ss_hi, ss_lo, 0, NU, True, True)

            def token_sums(c, stat_hi, stat_lo, tiles, half, start, stop, ready=None):
                s = c % RING
                for t in tiles:
                    if ready is not None:
                        ready(t)
                    tok = slice(t * P, (t + 1) * P)
                    last = three(ps[:, 2 * t + half, :], stat_hi[:, tok], stat_lo[:, tok],
                                 w_hi[:, s, :], w_lo[:, s, :], start, stop)
                return last

            def merged_read(t):
                if t == 0:
                    pe.wait_ge(mg_split, KD)

            for j in range(KD - 2):
                pe.wait_ge(mg_split, j + 1)
                for half in range(2):
                    c = FIRST[("w_out", j)] + half
                    pe.wait_ge(weights_split, c + 1)
                    token_sums(c, mg_hi[:, j, :], mg_lo[:, j, :], (2, 3, 0, 1), half, j == 0, False,
                               merged_read if j == 0 else None).then_inc(chunks_multiplied, 1)
            for t in range(TT):
                for j in (KD - 2, KD - 1):
                    for half in range(2):
                        c = FIRST[("w_out", j)] + half
                        pe.wait_ge(weights_split, c + 1)
                        last = token_sums(c, mg_hi[:, j, :], mg_lo[:, j, :], (t,), half, False, j == KD - 1)
                        if t == TT - 1:
                            last.then_inc(chunks_multiplied, 1)
                if t < TT - 1:
                    last.then_inc(tokens_summed, 1)
            for t in range(TT):
                transpose_x(TT + t)

            pe.wait_ge(xT_split, 4 * TT)
            up0 = FIRST[("up", 0)]

            def up_pair(i, b, first):
                if not first:
                    pe.wait_ge(conv_done, 4 * i + 2 * b - 2)
                for v in range(2):
                    for part in range(2):
                        q = 4 * b + 2 * v + part
                        s = (up0 + q) % RING
                        pe.wait_ge(weights_split, 8 * i + (up0 + q + 1))
                        for k in range(4):
                            last = three(ps[:, 2 * b + v, :], w_hi[:, s, k * P:(k + 1) * P],
                                         w_lo[:, s, k * P:(k + 1) * P], xT_hi[:, 4 * part + k, :],
                                         xT_lo[:, 4 * part + k, :], part == 0 and k == 0, part == 1 and k == 3)
                        last.then_inc(chunks_multiplied, 1)

            for b in range(2):
                up_pair(0, b, True)
            with pe.Fori(1, NF // 2) as i:
                for b in range(2):
                    up_pair(i, b, False)

            down0 = FIRST[("down", 0)]

            def down_pair(i, first):
                for b in range(2):
                    pe.wait_ge(ff_split, 2 * i + (b + 1))
                    for half in range(2):
                        q = 2 * b + half
                        pe.wait_ge(weights_split, 4 * i + (down0 + q + 1))
                        token_sums(down0 + q, ff_hi[b], ff_lo[b], (2, 3, 0, 1), half, first and b == 0, False
                                   ).then_inc(chunks_multiplied, 1)

            pe.wait_ge(conv_done, 2 * NF)
            down_pair(0, True)
            with pe.Fori(1, NF // 2 - 1) as i:
                down_pair(i, False)
            for t in range(TT):
                for b in range(2):
                    for half in range(2):
                        c = FIRST[("down", NF - 2 + b)] + half
                        pe.wait_ge(ff_split, NF - 1 + b)
                        pe.wait_ge(weights_split, c + 1)
                        last = token_sums(c, ff_hi[b], ff_lo[b], (t,), half, False, b == 1)
                        if t == TT - 1:
                            last.then_inc(chunks_multiplied, 1)
                if t < TT - 1:
                    last.then_inc(tokens_summed, 1)

        def cv(row, v, f):
            at0 = V_CONV + (2 * row + v) * NF
            return vec[:, at0 + f:at0 + f + 1] if isinstance(f, int) else vec[:, bass.ds(f + at0, 1)]

        def ff_tile(f):
            return ff[:, f, :] if isinstance(f, int) else ff[:, bass.ds(f, 1), :].rearrange("p a n -> p (a n)")

        def token_bank(t):
            return ps[:, 2 * t:2 * t + 2, :].rearrange("p b n -> p (b n)")

        def tokens_ready(eng, n):
            t = n % TT
            if t < TT - 1:
                eng.wait_ge(tokens_summed, (TT - 1) * (n // (2 * TT)) + t + 1)
            else:
                eng.wait_ge(chunks_multiplied, END[("w_out", KD - 1)] if n < FPOST else NCHUNK)

        @block.scalar
        def _(act):
            act.dma_start(small[:, 0:3, :], ssm_small).then_inc(small_landed, 16)
            for t in range(TT):
                act.dma_start(x_in[:, t, :], x_t[t, :, :]).then_inc(x_landed[t], 16)
                if t == 0:
                    act.dma_start(g_mix_pre[:, :], norms[0:1, :].partition_broadcast(P).rearrange("p a d -> p (a d)")).then_inc(g_landed, 16)
            act.dma_start(pos_i[:, :], positions.partition_broadcast(P).rearrange("p a d -> p (a d)")).then_inc(pos_landed, 16)
            act.dma_start(vec[:, :], vecs).then_inc(vec_landed, 16)
            act.dma_start(bc_in[:, :, :, :], ssm_bc).then_inc(bc_landed, 16)
            act.dma_start(d_skip[:, :], ssm_d).then_inc(bc_landed, 16)

            def square_sum(n, squares, src):
                act.activation(squares, src, ACT.Square, accum_out=st(0, n)).then_inc(sq_summed, 1)

            def root(n):
                act.wait_ge(ms_ready, n + 1)
                act.activation(st(2, n), st(1, n), ACT.Sqrt).then_inc(rms_ready, 1)

            def round_xT(n):
                t = n % TT
                act.wait_ge(x_transposed, n + 1)
                for b in range(2):
                    act.activation(xT_hi[:, 4 * b:4 * b + 4, t * P:(t + 1) * P],
                                   ps[:, 2 * t + b, :].rearrange("p (k n) -> p k n", k=4),
                                   ACT.Copy).then_inc(xT_rounded, 1)

            act.wait_ge(angle_ready, 1)
            act.activation(sm("sn"), sm("r"), ACT.Sin).then_inc(sine_ready, 1)
            for t in range(TT):
                act.wait_ge(x_landed[t], 16)
                if t >= 2:
                    act.wait_ge(sq_summed, t - 1)
                square_sum(PRE + t, x_sq[:, t % 2, :], x_in[:, t, :])
                root(PRE + t)
                if t >= 1:
                    round_xT(t - 1)
            round_xT(TT - 1)
            act.wait_ge(angle_ready, 2)
            act.activation(sin_t[:, :], ang[:, :], ACT.Sin).then_inc(sine_ready, 1)
            act.wait_ge(angle_ready, 3)
            act.activation(cos_t[:, :], ang[:, :], ACT.Sin).then_inc(sine_ready, 1)
            act.wait_ge(angle_ready, 4)
            act.activation(sm("cs"), sm("r"), ACT.Sin).then_inc(sine_ready, 1)

            for j in range(NU):
                act.wait_ge(chunks_multiplied, END[("u", j)])
                for s in range(SUB):
                    for q in range(PPT):
                        act.activation(u_hi[HALF * s:HALF * (s + 1), j, q, :],
                                       ps[HALF * q:HALF * (q + 1), j, s::SUB], ACT.Copy).then_inc(u_rounded, 1)
            for j in range(KQ + KKV):
                name = ("cq", j) if j < KQ else ("ckv", j - KQ)
                bank = (4 + j) % 8
                act.wait_ge(chunks_multiplied, END[name])
                act.activation(c_raw[:, j, :], ps[:, bank, :], ACT.Copy).then_inc(c_copied, 1)
                act.activation(c_sq[:, j, :], ps[:, bank, :], ACT.Square).then_inc(c_squared, 1)

            def gate_tanh(n):
                act.wait_ge(chunks_multiplied, END[("gate", n)])
                act.activation(gates[:, n, :], ps[:, 6 + n % 2, :], ACT.Tanh, bias=hb_gate[:, n:n + 1],
                               scale=0.5).then_inc(gate_done, 1)

            gate = [0]

            def gate_tanhs(n):
                for _ in range(n):
                    gate_tanh(gate[0])
                    gate[0] += 1

            def blocks(it):
                pr = slice(it * PPT, (it + 1) * PPT)
                if it == 0:
                    act.wait_ge(compacts_ready, 1)
                else:
                    act.wait_ge(kn_done, it)
                    act.wait_ge(ca_split, it)
                for c in range(2):
                    for e in range(2):
                        rows, cols = slice(NS * e, NS * (e + 1)), slice(GH * e, GH * (e + 1))
                        act.activation(ba_blk[rows, c, :, :, cols], ab[rows, :, c, pr, :].rearrange("p s q h -> p q s h"),
                                       ACT.Copy).then_inc(blocks_ready, 1)
                        act.activation(ca_blk[rows, c, :, :, cols], ca[rows, :, c, pr, :].rearrange("p s q h -> p q s h"),
                                       ACT.Copy).then_inc(blocks_ready, 1)

            def round_inputs(it):
                act.wait_ge(ba_transposed, it + 1)
                if it:
                    act.wait_ge(bu_done, it)
                for c in range(2):
                    act.activation(ba_hi[:, c, :, :], ps[:, c, :].rearrange("p (q n) -> p q n", q=PPT),
                                   ACT.Copy).then_inc(ba_rounded, 1)

            def round_outputs(it):
                act.wait_ge(blocks_ready, 8 * (it + 1))
                if it:
                    act.wait_ge(y_summed, it)
                for c in range(2):
                    act.activation(ca_hi[:, c, :, :, :], ca_blk[:, c, :, 1:SUB + 1, :], ACT.Copy).then_inc(ca_rounded, 1)
                act.wait_ge(skip_added, it + 1)
                for s in range(SUB):
                    act.activation(kn_hi[HALF * s:HALF * (s + 1), :, s:SUB, :],
                                   ps[0:HALF, 2, :].rearrange("p (q t h) -> p q t h", q=PPT, t=SUB)[:, :, 0:SUB - s, :],
                                   ACT.Copy).then_inc(ca_rounded, 1)

            def round_states(it):
                act.wait_ge(states_ready, it + 1)
                act.activation(s_hi[:, :, :, 1:NC], z_t[:, :, :].rearrange("p c (q n) -> p c q n", q=PPT)[:, :, :, 0:NC - 1],
                               ACT.Copy).then_inc(states_rounded, 1)

            def activate(it):
                act.wait_ge(y_summed, it + 1)
                for s in range(SUB):
                    for q in range(PPT):
                        act.activation(y_f[it][HALF * q:HALF * (q + 1), s::SUB],
                                       ps[HALF * s:HALF * (s + 1), 5, q * NC:(q + 1) * NC],
                                       ACT.Gelu_apprx_tanh).then_inc(y_done, 1)

            blocks(0)
            gate_tanhs(1)
            act.wait_ge(c_ms, 2)
            act.activation(r_bc[:, :, :], r_bc[:, :, :], ACT.Sqrt).then_inc(c_rms, 1)
            gate_tanhs(1)
            round_inputs(0)
            round_outputs(0)
            gate_tanhs(GATES_FIRST - 2)
            for it in range(NU):
                if it:
                    round_outputs(it)
                    activate(it - 1)
                if it + 1 < NU:
                    gate_tanhs(1)
                    blocks(it + 1)
                    round_inputs(it + 1)
                round_states(it)
                if it == 0:
                    for j in range(KQ + KKV):
                        act.wait_ge(cn_ready, j + 1)
                        act.activation(cn_hi[:, j, :], c_raw[:, j, :], ACT.Copy).then_inc(cn_rounded, 1)
                    act.wait_ge(cn_split, KQ + KKV)
                gate_tanhs(GATES_SSM[it] - int(it + 1 < NU))
            act.wait_ge(chunks_multiplied, END[("uv", 0)])
            for t in range(TT):
                act.activation(v_hi[:, t, :], ps[:, V_BANK[t], :], ACT.Copy).then_inc(v_rounded, 1)
            activate(NU - 1)
            for e, col in enumerate((V_EVEN, V_ODD)):
                act.activation(kr_hl[:, 0, e, :], kr_f[:, :], ACT.Copy, scale=vec[:, col:col + 1]).then_inc(kr_rounded, 1)

            UNITS = HG * TT
            scale = 1.0 / math.sqrt(QK)
            for g in range(2):
                act.wait_ge(qr_ready, g + 1)
                act.activation(qr_hl[:, 0, :], rot_a[:, :], ACT.Copy, scale=scale).then_inc(qr_rounded, 1)
                if g == 0:
                    act.wait_ge(kr_split, 2)
                    for c in range(2):
                        for pair in range(2):
                            act.dma_start(k_hl[NOPE + 32 * c:NOPE + 32 * (c + 1), :, 2 * pair:2 * pair + 2, :].bitcast(F32),
                                          kr_hl[64 * c:64 * c + 32, :, :, :].bitcast(F32)).then_inc(krope_landed, 16)
                act.wait_ge(qr_split, g + 1)
                for c in range(2):
                    for h in range(HG):
                        act.dma_start(q_hl[NOPE + 32 * c:NOPE + 32 * (c + 1), :, h, :].bitcast(F32),
                                      qr_hl[64 * c + 32 * (h // 2):64 * c + 32 * (h // 2) + 32, :, :].bitcast(F32)).then_inc(qrope_landed, 16)
                gate_tanhs(1)
                for m, bank in enumerate((4, 5)):
                    act.wait_ge(chunks_multiplied, END[("uq", 3 * g + m)])
                    for e in range(2):
                        act.activation(q_hi[0:NOPE, 2 * m + e, :], ps[e * NOPE:(e + 1) * NOPE, bank, :],
                                       ACT.Copy, scale=scale).then_inc(q_rounded, 1)
                act.wait_ge(chunks_multiplied, END[("uk", g)])
                for m, bank in enumerate((3, 0)):
                    for e in range(2):
                        act.activation(k_hi[0:NOPE, 2 * m + e, :], ps[e * NOPE:(e + 1) * NOPE, bank, :],
                                       ACT.Copy).then_inc(k_rounded, 1)

                def copy_pair(pair):
                    act.wait_ge(heads_done, HG * g + 2 * pair + 2)
                    for e in range(2):
                        act.activation(at_f[e * VD:(e + 1) * VD, 2 * g + pair, :], ps[e * VD:(e + 1) * VD, 4 + e, :],
                                       ACT.Copy).then_inc(at_copied, 1)

                half = 0
                for t in range(UNITS + 3):
                    if t == 12:
                        copy_pair(0)
                    if t < UNITS:
                        n = (t % TT + 1) * P
                        act.wait_ge(max_ready, UNITS * g + t + 1)
                        if t >= 2:
                            act.wait_ge(probs_transposed, UNITS * g + t - 1)
                        act.activation(prob[:, t % 2, 0:n], ps[:, t % 2, 0:n], ACT.Exp, bias=rowst[:, 0, t % 4:t % 4 + 1],
                                       accum_out=rowst[:, 1, t % 4:t % 4 + 1]).then_inc(exp_done, 1)
                    if 2 <= t < UNITS + 2:
                        u = t - 2
                        i = u % TT
                        act.wait_ge(probs_transposed, UNITS * g + u + 1)
                        if u >= TT or g:
                            act.wait_ge(heads_done, HG * g + u // TT)
                        act.activation(pT_hi[:, 0:i + 1, i * P:(i + 1) * P],
                                       ps[:, 2 + u % 2, 0:(i + 1) * P].rearrange("p (j n) -> p j n", n=P),
                                       ACT.Copy).then_inc(pT_rounded, 1)
                    if g and t in Y_STEPS:
                        j = Y_STEPS.index(t)
                        act.activation(y_hi[:, j, :], y_f[j][:, :], ACT.Copy).then_inc(y_rounded, 1)
                    if t - 1 in GATE_STEPS[g]:
                        half += 1
                        if half % 2 == 0:
                            gate_tanhs(1)
                copy_pair(1)
            act.wait_ge(at_copied, NH)
            for j in range(NU):
                act.activation(at_hi[:, j, :], at_f[:, j, :], ACT.Copy).then_inc(at_rounded, 1)
            for m in range(NU):
                act.wait_ge(chunks_multiplied, END[("glu", m)])
                if m >= 2:
                    act.wait_ge(glu_ready, m - 1)
                act.activation(glu_t[:, m % 2, :], ps[:, m, :], ACT.Tanh, bias=hb_glu[:, m:m + 1],
                               scale=0.5).then_inc(glu_tanh, 1)
                act.wait_ge(glu_ready, m + 1)
                act.activation(ss_hi[:, m, :], glu_y[:, m % 2, :], ACT.Copy, scale=0.5).then_inc(ss_rounded, 1)
            for m in range(KD):
                act.wait_ge(mg_ready, m + 1)
                act.activation(mg_hi[:, m, :], mg_t[:, m % 2, 0, :], ACT.Copy, scale=0.5).then_inc(mg_rounded, 1)
                if m == 0:
                    act.wait_ge(ss_split, NU)
                    for t in range(TT):
                        act.dma_start(x1[:, t, :], x_t[t, :, :]).then_inc(x1_landed, 16)
                    act.wait_ge(chunks_multiplied, END[("glu", NU - 1)])
                    for n, dst in ((1, g_mix_post), (2, g_ffn_pre)):
                        act.dma_start(dst[:, :], norms[n:n + 1, :].partition_broadcast(P).rearrange("p a d -> p (a d)")).then_inc(gmid_landed, 16)

            act.wait_ge(chunks_multiplied, END[("ssm_out", KD - 1)])
            for t in range(TT):
                tokens_ready(act, POST + t)
                if t:
                    act.wait_ge(sq_summed, POST + 2 * t)
                square_sum(POST + 2 * t, sq[:, :], token_bank(t))
                root(POST + 2 * t)
                act.wait_ge(x1_ready, t + 1)
                square_sum(POST + 2 * t + 1, sq[:, :], x1[:, t, :])
                root(POST + 2 * t + 1)
                if t:
                    round_xT(TT + t - 1)
            round_xT(2 * TT - 1)
            act.wait_ge(xn_ready, 2 * TT)
            act.dma_start(g_ffn_post[:, :], norms[3:4, :].partition_broadcast(P).rearrange("p a d -> p (a d)")).then_inc(gpost_landed, 16)

            up0 = FIRST[("up", 0)]

            def up_pair(i, b, f, first):
                for v in range(2):
                    act.wait_ge(chunks_multiplied, 8 * i + (up0 + 4 * b + 2 * v + 2))
                    if not first:
                        act.wait_ge(ff_ready, 2 * i + (b - 1))
                    act.activation(conv[:, b, v, :], ps[:, 2 * b + v, :], ACT.Identity,
                                   bias=cv(3, v, f), scale=cv(2, v, f)).then_inc(conv_begun, 1)
                act.wait_ge(conv_done, 4 * i + (2 * b + 1))
                act.activation(gelu[:, b, :], conv[:, b, 0, :], ACT.Gelu_apprx_tanh).then_inc(gelu_done, 1)

            for b in range(2):
                up_pair(0, b, b, True)
            with act.Fori(1, NF // 2) as i:
                for b in range(2):
                    up_pair(i, b, 2 * i + b, False)

            down0 = FIRST[("down", 0)]

            def ff_round(i, b, f, first):
                if not first:
                    act.wait_ge(chunks_multiplied, 4 * i + (down0 + 2 * b - 2))
                act.activation(ff_hi[b][:, :], ff_tile(f), ACT.Copy).then_inc(ff_rounded, 1)

            act.wait_ge(ff_ready, NF)
            for b in range(2):
                ff_round(0, b, b, True)
            with act.Fori(1, NF // 2) as i:
                for b in range(2):
                    ff_round(i, b, 2 * i + b, False)
            for t in range(TT):
                tokens_ready(act, FPOST + t)
                act.wait_ge(sq_summed, FPOST + t)
                square_sum(FPOST + t, sq[:, :], token_bank(t))
                root(FPOST + t)

        @block.vector
        def _(dve):
            steps = [0]

            def link(ins):
                ins.then_inc(dve_step, 1)
                steps[0] += 1
                dve.wait_ge(dve_step, steps[0])

            def tt(o, a, b, op):
                link(dve.tensor_tensor(o, a, b, op))

            def ts(o, a, s1, s2, op0, op1):
                link(dve.tensor_scalar(o, a, s1, s2, op0, op1))

            def stt(o, a, s, b, op0, op1):
                link(dve.scalar_tensor_tensor(out=o, in0=a, scalar=s, in1=b, op0=op0, op1=op1))

            def rsqrt_mean(n, count):
                dve.wait_ge(sq_summed, n + 1)
                dve.tensor_scalar(st(1, n), st(0, n), 1.0 / count, EPS, ALU.mult, ALU.add).then_inc(ms_ready, 1)
                dve.wait_ge(rms_ready, n + 1)
                link(dve.reciprocal(st(3, n), st(2, n)))

            def split_xT(n):
                t = n % TT
                for b in range(2):
                    dve.wait_ge(xT_rounded, 2 * n + b + 1)
                    o = (slice(None), slice(4 * b, 4 * b + 4), slice(t * P, (t + 1) * P))
                    dve.tensor_tensor(xT_lo[o], ps[:, 2 * t + b, :].rearrange("p (k n) -> p k n", k=4),
                                      xT_hi[o].bitcast(F32), ALU.subtract).then_inc(xT_split, 1)

            def reduce_angle(a, k):
                ts(k, a, 1.0 / (2 * math.pi), ROUND, ALU.mult, ALU.add)
                ts(k, k, ROUND, None, ALU.subtract, ALU.bypass)
                for part in TWO_PI:
                    stt(a, k, -part, a, ALU.mult, ALU.add)

            def quarter_turn(a, k):
                ts(a, a, math.pi / 2, None, ALU.add, ALU.bypass)
                ts(k, a, math.pi, -2 * math.pi, ALU.is_gt, ALU.mult)
                tt(a, a, k, ALU.add)

            def clamp(a, signal):
                dve.tensor_scalar(a, a, PI_IN, -PI_IN, ALU.min, ALU.max).then_inc(angle_ready, 1)
                dve.wait_ge(angle_ready, signal)

            def exponential(o, y):
                n, r, p = sm("n"), sm("r"), sm("p")
                ts(sm("y"), y, -90.0, 89.0, ALU.max, ALU.min)
                ts(n, sm("y"), 1.0 / math.log(2), ROUND, ALU.mult, ALU.add)
                ts(n, n, ROUND, None, ALU.subtract, ALU.bypass)
                stt(r, n, -LN2[0], sm("y"), ALU.mult, ALU.add)
                stt(r, n, -LN2[1], r, ALU.mult, ALU.add)
                ts(p, r, EXP_TAYLOR[7], None, ALU.mult, ALU.bypass)
                for c in EXP_TAYLOR[6:0:-1]:
                    stt(p, p, c, r, ALU.add, ALU.mult)
                ts(p, p, 1.0, None, ALU.add, ALU.bypass)
                ts(n, n, -127.0, 128.0, ALU.max, ALU.min)
                ts(n, n, 127.0, None, ALU.add, ALU.bypass)
                link(dve.tensor_copy(k_int[:, :], n))
                ts(k_int[:, :], k_int[:, :], 23, None, ALU.logical_shift_left, ALU.bypass)
                tt(o, p, k_int[:, :].bitcast(F32), ALU.mult)

            def cmul(outs, a, b, t0, t1):
                tt(t0, a[0], b[0], ALU.mult)
                tt(t1, a[1], b[1], ALU.mult)
                tt(outs[0], t0, t1, ALU.subtract)
                tt(t0, a[0], b[1], ALU.mult)
                tt(t1, a[1], b[0], ALU.mult)
                tt(outs[1], t0, t1, ALU.add)

            dve.wait_ge(small_landed, 16)
            exponential(sm("dt"), sm("ldt"))
            tt(sm("t0"), sm("lr"), sm("dt"), ALU.mult)
            exponential(sm("mag"), sm("t0"))
            tt(sm("ang"), sm("li"), sm("dt"), ALU.mult)
            link(dve.tensor_copy(sm("r"), sm("ang")))
            reduce_angle(sm("r"), sm("k"))
            clamp(sm("r"), 1)
            for t in range(TT):
                rsqrt_mean(PRE + t, D)
                if t == 0:
                    dve.wait_ge(g_landed, 16)
                if t >= 2:
                    dve.wait_ge(x_transposed, t - 1)
                dve.scalar_tensor_tensor(out=xn[:, t % 2, :], in0=x_in[:, t, :], scalar=st(3, PRE + t),
                                         in1=g_mix_pre[:, :], op0=ALU.mult, op1=ALU.mult).then_inc(xn_ready, 1)
                if t:
                    split_xT(t - 1)
            split_xT(TT - 1)

            dve.wait_ge(pos_landed, 16)
            dve.wait_ge(vec_landed, 16)
            link(dve.tensor_copy(ang[:, :], pos_i[:, :]))
            ts(ang[:, :], ang[:, :], vec[:, V_INV:V_INV + 1], None, ALU.mult, ALU.bypass)
            reduce_angle(ang[:, :], ang_k[:, :])
            clamp(ang[:, :], 2)
            dve.wait_ge(sine_ready, 2)
            quarter_turn(ang[:, :], ang_k[:, :])
            clamp(ang[:, :], 3)
            dve.wait_ge(sine_ready, 3)
            ts(sin_t[:, :], sin_t[:, :], vec[:, V_SIGN:V_SIGN + 1], None, ALU.mult, ALU.bypass)
            ts(hb_gate[:, :], vec[:, V_BG:V_BG + NG], 0.5, None, ALU.mult, ALU.bypass)
            ts(hb_glu[:, :], vec[:, V_BGLU:V_BGLU + NU], 0.5, None, ALU.mult, ALU.bypass)

            quarter_turn(sm("r"), sm("k"))
            clamp(sm("r"), 4)
            dve.wait_ge(sine_ready, 4)
            tt(sm("ar"), sm("mag"), sm("cs"), ALU.mult)
            tt(sm("ai"), sm("mag"), sm("sn"), ALU.mult)
            tt(sm("t0"), sm("lr"), sm("lr"), ALU.mult)
            tt(sm("t1"), sm("li"), sm("li"), ALU.mult)
            tt(sm("den"), sm("t0"), sm("t1"), ALU.add)
            link(dve.reciprocal(sm("den"), sm("den")))
            ts(sm("nr"), sm("ar"), -1.0, None, ALU.add, ALU.bypass)
            tt(sm("t0"), sm("nr"), sm("lr"), ALU.mult)
            tt(sm("t1"), sm("ai"), sm("li"), ALU.mult)
            tt(sm("t0"), sm("t0"), sm("t1"), ALU.add)
            tt(sm("zr"), sm("t0"), sm("den"), ALU.mult)
            tt(sm("t0"), sm("ai"), sm("lr"), ALU.mult)
            tt(sm("t1"), sm("nr"), sm("li"), ALU.mult)
            tt(sm("t0"), sm("t0"), sm("t1"), ALU.subtract)
            tt(sm("zi"), sm("t0"), sm("den"), ALU.mult)
            a = {1: (sm("ar"), sm("ai"))}
            for k in (2, 3, 4):
                a[k] = (sm(f"a{k}r"), sm(f"a{k}i"))
                cmul(a[k], a[k - 1], a[1], sm("t0"), sm("t1"))
            tt(sm("m4"), sm("mag"), sm("mag"), ALU.mult)
            tt(sm("m4"), sm("m4"), sm("m4"), ALU.mult)
            w = {1: (sm("cs"), sm("sn"))}
            for k in (2, 4, 8, 16, 32, 64, 128, 256):
                w[k] = (sm(f"w{k}r"), sm(f"w{k}i"))
                cmul(w[k], w[k // 2], w[k // 2], sm("t0"), sm("t1"))
                tt(sm("t0"), w[k][0], w[k][0], ALU.mult)
                tt(sm("t1"), w[k][1], w[k][1], ALU.mult)
                tt(sm("t0"), sm("t0"), sm("t1"), ALU.add)
                ts(sm("t0"), sm("t0"), -0.5, 1.5, ALU.mult, ALU.add)
                tt(w[k][0], w[k][0], sm("t0"), ALU.mult)
                tt(w[k][1], w[k][1], sm("t0"), ALU.mult)

            def split_u(j):
                dve.wait_ge(u_rounded, SUB * PPT * (j + 1))
                for s in range(SUB):
                    for q in range(PPT):
                        o = (slice(HALF * s, HALF * (s + 1)), j, q, slice(None))
                        ins = dve.tensor_tensor(u_lo[o], ps[HALF * q:HALF * (q + 1), j, s::SUB], u_hi[o].bitcast(F32), ALU.subtract)
                        if s == SUB - 1 and q == PPT - 1:
                            ins.then_inc(u_split, 1)

            dve.wait_ge(bc_landed, 32)

            def wide(v):
                return v.unsqueeze(2).to_broadcast([P, PAIRS, GH])

            b_re, b_im, c_re, c_im = (bc_in[:, n, :, :] for n in range(4))
            t0, t1 = bt[:, 0, :, :], bt[:, 1, :, :]
            cmul((ab[:, SUB - 1, 0, :, :], ab[:, SUB - 1, 1, :, :]), (b_re, b_im), (wide(sm("zr")), wide(sm("zi"))), t0, t1)
            for k in range(1, SUB):
                s = SUB - 1 - k
                cmul((ab[:, s, 0, :, :], ab[:, s, 1, :, :]), (ab[:, s + 1, 0, :, :], ab[:, s + 1, 1, :, :]),
                     (wide(a[1][0]), wide(a[1][1])), t0, t1)
            split_u(0)
            split_u(1)
            link(dve.tensor_copy(ca[:, 0, 0, :, :], c_re))
            ts(ca[:, 0, 1, :, :], c_im, -1.0, None, ALU.mult, ALU.bypass)
            for k in range(1, SUB + 1):
                ar, ai = wide(a[k][0]), wide(a[k][1])
                tt(t0, c_re, ar, ALU.mult)
                tt(t1, c_im, ai, ALU.mult)
                tt(ca[:, k, 0, :, :], t0, t1, ALU.subtract)
                tt(t0, c_re, ai, ALU.mult)
                tt(t1, c_im, ar, ALU.mult)
                stt(ca[:, k, 1, :, :], t0, -1.0, t1, ALU.mult, ALU.subtract)
            link(dve.memset(ba_blk[:, :, :, :, :], 0.0))
            link(dve.memset(ca_blk[:, :, :, :, :], 0.0))
            dve.memset(m_t[:, 0, :], 0.0).then_inc(compacts_ready, 1)
            dve.wait_ge(compacts_ready, 1)
            link(dve.tensor_copy(kn_hi[:, :, :, :].rearrange("p q s h -> p (q s h)"), m_t[:, 0, :]))
            link(dve.tensor_copy(kn_lo[:, :, :, :].rearrange("p q s h -> p (q s h)"), m_t[:, 0, :]))

            link(dve.memset(m_t[:, 0, 0:2 * PPT], 0.0))
            for t in (s_hi, s_lo):
                link(dve.tensor_copy(t[:, :, :, 0:1], m_t[:, 0, 0:2 * PPT].rearrange("p (c q n) -> p c q n", c=2, n=1)))
            split_u(2)
            split_u(3)

            dve.wait_ge(c_squared, KQ)
            tt(c_sq[:, 0, :], c_sq[:, 0, :], c_sq[:, 1, :], ALU.add)
            dve.tensor_tensor(c_sq[:, 0, :], c_sq[:, 0, :], c_sq[:, 2, :], ALU.add).then_inc(c_sums, 1)
            dve.wait_ge(c_squared, KQ + KKV)
            dve.tensor_tensor(c_sq[:, KQ, :], c_sq[:, KQ, :], c_sq[:, KQ + 1, :], ALU.add).then_inc(c_sums, 1)

            def rotate(bank, o, signal):
                tt(rot_a[:, :], ps[:, bank, :], cos_t[:, :], ALU.mult)
                tt(rot_b[0:64, :], ps[64:P, bank, :], sin_t[64:P, :], ALU.mult)
                tt(rot_b[64:P, :], ps[0:64, bank, :], sin_t[0:64, :], ALU.mult)
                dve.tensor_tensor(o, rot_a[:, :], rot_b[:, :], ALU.add).then_inc(signal, 1)

            dve.wait_ge(chunks_multiplied, END[("kr", 0)])
            rotate(1, kr_f[:, :], kr_ready)
            dve.wait_ge(c_totals, 1)
            for b, (bank, count) in enumerate(((5, RQ), (0, RKV))):
                dve.tensor_scalar(r_bc[:, b, :], ps[:, bank, :], 1.0 / count, EPS, ALU.mult, ALU.add).then_inc(c_ms, 1)

            def split_inputs(it):
                for c in range(2):
                    dve.wait_ge(ba_rounded, 2 * it + c + 1)
                    ins = dve.tensor_tensor(ba_lo[:, c, :, :], ps[:, c, :].rearrange("p (q n) -> p q n", q=PPT),
                                            ba_hi[:, c, :, :].bitcast(F32), ALU.subtract)
                    if c:
                        ins.then_inc(ba_split, 1)

            def own_kernel():
                return ps[0:HALF, 2, :].rearrange("p (q t h) -> p q t h", q=PPT, t=SUB)

            def add_skip(it):
                eye = ident[0:HALF, 0:HALF].unsqueeze(1).to_broadcast([HALF, PPT, HALF])
                dd = d_skip[:, it * PPT:(it + 1) * PPT].unsqueeze(2).to_broadcast([HALF, PPT, HALF])
                dt_ = m_t[0:HALF, 0, 0:PPT * HALF].rearrange("p (q h) -> p q h", q=PPT)
                tt(dt_, eye, dd, ALU.mult)
                dve.wait_ge(kn_done, it + 1)
                own = own_kernel()
                dve.tensor_tensor(own[:, :, 0, :], own[:, :, 0, :], dt_, ALU.add).then_inc(skip_added, 1)

            def split_outputs(it):
                for c in range(2):
                    dve.wait_ge(ca_rounded, 6 * it + c + 1)
                    link(dve.tensor_tensor(ca_lo[:, c, :, :, :], ca_blk[:, c, :, 1:SUB + 1, :], ca_hi[:, c, :, :, :].bitcast(F32),
                                           ALU.subtract))
                dve.wait_ge(ca_rounded, 6 * (it + 1))
                for s in range(SUB):
                    o = (slice(HALF * s, HALF * (s + 1)), slice(None), slice(s, SUB), slice(None))
                    ins = dve.tensor_tensor(kn_lo[o], own_kernel()[:, :, 0:SUB - s, :], kn_hi[o].bitcast(F32), ALU.subtract)
                    if s == SUB - 1:
                        ins.then_inc(ca_split, 1)

            link(dve.memset(rot_c[:, :, 0:1], 1.0))
            link(dve.memset(rot_s[:, :, 0:1], 0.0))
            m = 1
            while m < NC:
                if 2 * m == NC:
                    split_inputs(0)
                    add_skip(0)
                wr, wi = (v.unsqueeze(2).to_broadcast([P, PAIRS, m]) for v in w[SUB * m])
                s0, s1 = (rt[:, c, 0:PAIRS * m].rearrange("p (q n) -> p q n", q=PAIRS) for c in range(2))
                cmul((rot_c[:, :, m:2 * m], rot_s[:, :, m:2 * m]), (rot_c[:, :, 0:m], rot_s[:, :, 0:m]), (wr, wi), s0, s1)
                m *= 2

            zr, zi, mr, mi = z_t[:, 0, :], z_t[:, 1, :], m_t[:, 0, :], m_t[:, 1, :]
            dec = decay[:, :, :].rearrange("p q n -> p (q n)")
            for it in range(NU):
                pr = slice(it * PPT, (it + 1) * PPT)
                link(dve.tensor_copy(decay[:, :, :], sm("m4")[:, pr].unsqueeze(2).to_broadcast([P, PPT, NC])))
                link(dve.memset(decay[:, :, 0:1], 0.0))
                dve.wait_ge(bu_done, it + 1)
                rc, rs = (r[:, pr, :].rearrange("p q n -> p (q n)") for r in (rot_c, rot_s))
                br, bi = ps[:, 3, :], ps[:, 4, :]
                if it:
                    dve.wait_ge(states_rounded, it)
                tt(zr, br, rc, ALU.mult)
                tt(mr, bi, rs, ALU.mult)
                tt(zr, zr, mr, ALU.add)
                tt(zi, bi, rc, ALU.mult)
                dve.tensor_tensor(mr, br, rs, ALU.mult).then_inc(inputs_read, 1)
                dve.wait_ge(inputs_read, it + 1)
                tt(zi, zi, mr, ALU.subtract)
                link(dve.tensor_tensor_scan(mr, dec, zr, 0.0, ALU.mult, ALU.add))
                link(dve.tensor_tensor_scan(mi, dec, zi, 0.0, ALU.mult, ALU.add))
                split_outputs(it)
                tt(dec, mi, rs, ALU.mult)
                tt(zr, mr, rc, ALU.mult)
                tt(zr, zr, dec, ALU.subtract)
                tt(dec, mr, rs, ALU.mult)
                tt(zi, mi, rc, ALU.mult)
                dve.tensor_tensor(zi, zi, dec, ALU.add).then_inc(states_ready, 1)
                if it + 1 < NU:
                    split_inputs(it + 1)
                    add_skip(it + 1)
                dve.wait_ge(states_ready, it + 1)
                dve.wait_ge(states_rounded, it + 1)
                dve.tensor_tensor(s_lo[:, :, :, 1:NC], z_t[:, :, :].rearrange("p c (q n) -> p c q n", q=PPT)[:, :, :, 0:NC - 1],
                                  s_hi[:, :, :, 1:NC].bitcast(F32), ALU.subtract).then_inc(states_split, 1)
                if it == 0:
                    dve.wait_ge(c_rms, 1)
                    link(dve.reciprocal(r_bc[:, :, :], r_bc[:, :, :]))
                    for j in range(KQ + KKV):
                        dve.scalar_tensor_tensor(out=c_raw[:, j, :], in0=c_raw[:, j, :], scalar=vec[:, V_QN + j:V_QN + j + 1],
                                                 in1=r_bc[:, int(j >= KQ), :], op0=ALU.mult, op1=ALU.mult).then_inc(cn_ready, 1)
                    for j in range(KQ + KKV):
                        dve.wait_ge(cn_rounded, j + 1)
                        dve.tensor_tensor(cn_lo[:, j, :], c_raw[:, j, :], cn_hi[:, j, :].bitcast(F32), ALU.subtract).then_inc(cn_split, 1)

            for t in range(TT):
                dve.wait_ge(v_rounded, t + 1)
                dve.tensor_tensor(v_lo[:, t, :], ps[:, V_BANK[t], :], v_hi[:, t, :].bitcast(F32), ALU.subtract).then_inc(v_split, 1)
            for e, col in enumerate((V_EVEN, V_ODD)):
                dve.wait_ge(kr_rounded, e + 1)
                dve.scalar_tensor_tensor(out=kr_hl[:, 1, e, :], in0=kr_f[:, :], scalar=vec[:, col:col + 1],
                                         in1=kr_hl[:, 0, e, :].bitcast(F32), op0=ALU.mult, op1=ALU.subtract).then_inc(kr_split, 1)

            UNITS = HG * TT
            scale = 1.0 / math.sqrt(QK)
            for g in range(2):
                dve.wait_ge(chunks_multiplied, END[("uq", 3 * g + 2)])
                rotate(2, rot_a[:, :], qr_ready)
                dve.wait_ge(qr_rounded, g + 1)
                dve.scalar_tensor_tensor(out=qr_hl[:, 1, :], in0=rot_a[:, :], scalar=scale, in1=qr_hl[:, 0, :].bitcast(F32),
                                         op0=ALU.mult, op1=ALU.subtract).then_inc(qr_split, 1)
                for m, bank in enumerate((4, 5)):
                    for e in range(2):
                        dve.wait_ge(q_rounded, HG * g + 2 * m + e + 1)
                        o = (slice(0, NOPE), 2 * m + e, slice(None))
                        dve.scalar_tensor_tensor(out=q_lo[o], in0=ps[e * NOPE:(e + 1) * NOPE, bank, :], scalar=scale,
                                                 in1=q_hi[o].bitcast(F32), op0=ALU.mult, op1=ALU.subtract).then_inc(q_split, 1)
                for m, bank in enumerate((3, 0)):
                    for e in range(2):
                        dve.wait_ge(k_rounded, HG * g + 2 * m + e + 1)
                        o = (slice(0, NOPE), 2 * m + e, slice(None))
                        dve.tensor_tensor(k_lo[o], ps[e * NOPE:(e + 1) * NOPE, bank, :], k_hi[o].bitcast(F32),
                                          ALU.subtract).then_inc(k_split, 1)

                for t in range(UNITS + 3):
                    if t < UNITS:
                        i = t % TT
                        n = (i + 1) * P
                        dve.wait_ge(scores_done, UNITS * g + t + 1)
                        own = ps[:, t % 2, i * P:n]
                        tt(own, own, causal[:, :], ALU.add)
                        dve.tensor_reduce(rowst[:, 0, t % 4:t % 4 + 1], ps[:, t % 2, 0:n], AX_X, ALU.max,
                                          negate=True).then_inc(max_ready, 1)
                    if 1 <= t < UNITS + 1:
                        u = t - 1
                        n = (u % TT + 1) * P
                        dve.wait_ge(exp_done, UNITS * g + u + 1)
                        link(dve.reciprocal(rowst[:, 3, u % 4:u % 4 + 1], rowst[:, 1, u % 4:u % 4 + 1]))
                        dve.tensor_scalar(prob[:, u % 2, 0:n], prob[:, u % 2, 0:n], rowst[:, 3, u % 4:u % 4 + 1], None,
                                          ALU.mult, ALU.bypass).then_inc(probs_ready, 1)
                    if 2 <= t < UNITS + 2:
                        u = t - 2
                        i = u % TT
                        o = (slice(None), slice(0, i + 1), slice(i * P, (i + 1) * P))
                        dve.wait_ge(pT_rounded, UNITS * g + u + 1)
                        dve.tensor_tensor(pT_lo[o], ps[:, 2 + u % 2, 0:(i + 1) * P].rearrange("p (j n) -> p j n", n=P),
                                          pT_hi[o].bitcast(F32), ALU.subtract).then_inc(pT_split, 1)
                    if g and t - 1 in Y_STEPS:
                        j = Y_STEPS.index(t - 1)
                        dve.wait_ge(y_rounded, j + 1)
                        dve.tensor_tensor(y_lo[:, j, :], y_f[j][:, :], y_hi[:, j, :].bitcast(F32), ALU.subtract).then_inc(y_split, 1)
            for j in range(NU):
                dve.wait_ge(at_rounded, j + 1)
                dve.tensor_tensor(at_lo[:, j, :], at_f[:, j, :], at_hi[:, j, :].bitcast(F32), ALU.subtract).then_inc(at_split, 1)

            for m in range(NU):
                dve.wait_ge(glu_tanh, m + 1)
                dve.scalar_tensor_tensor(out=glu_y[:, m % 2, :], in0=glu_t[:, m % 2, :], scalar=1.0, in1=y_f[m][:, :],
                                         op0=ALU.add, op1=ALU.mult).then_inc(glu_ready, 1)
                dve.wait_ge(ss_rounded, m + 1)
                dve.scalar_tensor_tensor(out=ss_lo[:, m, :], in0=glu_y[:, m % 2, :], scalar=0.5, in1=ss_hi[:, m, :].bitcast(F32),
                                         op0=ALU.mult, op1=ALU.subtract).then_inc(ss_split, 1)
            for m in range(KD):
                b = 2 * (m % 2)
                ta, tb = mg_t[:, m % 2, 0, :], mg_t[:, m % 2, 1, :]
                dve.wait_ge(chunks_multiplied, END[("attn_out", m)])
                stt(ta, gates[:, m, :], 1.0, ps[:, b, :], ALU.add, ALU.mult)
                dve.wait_ge(chunks_multiplied, END[("ssm_out", m)])
                stt(tb, gates[:, KD + m, :], 1.0, ps[:, b + 1, :], ALU.add, ALU.mult)
                dve.tensor_tensor(ta, ta, tb, ALU.add).then_inc(mg_ready, 1)
                dve.wait_ge(mg_rounded, m + 1)
                dve.scalar_tensor_tensor(out=mg_lo[:, m, :], in0=ta, scalar=0.5, in1=mg_hi[:, m, :].bitcast(F32),
                                         op0=ALU.mult, op1=ALU.subtract).then_inc(mg_split, 1)

            dve.wait_ge(x1_landed, 16 * TT)
            dve.wait_ge(gmid_landed, 32)
            for t in range(TT):
                n = POST + 2 * t
                tokens_ready(dve, POST + t)
                rsqrt_mean(n, D)
                if t >= 2:
                    dve.wait_ge(x_transposed, TT + t - 1)
                stt(xn2[:, t % 2, :], token_bank(t), st(3, n), g_mix_post[:, :],
                    ALU.mult, ALU.mult)
                dve.tensor_tensor(x1[:, t, :], x1[:, t, :], xn2[:, t % 2, :], ALU.add).then_inc(x1_ready, 1)
                rsqrt_mean(n + 1, D)
                dve.scalar_tensor_tensor(out=xn2[:, t % 2, :], in0=x1[:, t, :], scalar=st(3, n + 1), in1=g_ffn_pre[:, :],
                                         op0=ALU.mult, op1=ALU.mult).then_inc(xn_ready, 1)
                if t:
                    split_xT(TT + t - 1)
            split_xT(2 * TT - 1)

            def taps(i, b, v, f):
                q = 2 * b + v
                o, z = conv[:, b, v, :], ps[:, 2 * b + v, :]
                dve.wait_ge(conv_begun, 4 * i + (q + 1))
                dve.scalar_tensor_tensor(out=o[:, 1:L], in0=z[:, 0:L - 1], scalar=cv(1, v, f), in1=o[:, 1:L],
                                         op0=ALU.mult, op1=ALU.add).then_inc(conv_step, 1)
                dve.wait_ge(conv_step, 4 * i + (q + 1))
                dve.scalar_tensor_tensor(out=o[:, 2:L], in0=z[:, 0:L - 2], scalar=cv(0, v, f), in1=o[:, 2:L],
                                         op0=ALU.mult, op1=ALU.add).then_inc(conv_done, 1)

            def up_pair(i, b, f):
                taps(i, b, 0, f)
                taps(i, b, 1, f)
                dve.wait_ge(conv_done, 4 * i + (2 * b + 2))
                dve.wait_ge(gelu_done, 2 * i + (b + 1))
                dve.tensor_tensor(ff_tile(f), gelu[:, b, :], conv[:, b, 1, :], ALU.mult).then_inc(ff_ready, 1)

            for b in range(2):
                up_pair(0, b, b)
            with dve.Fori(1, NF // 2) as i:
                for b in range(2):
                    up_pair(i, b, 2 * i + b)

            def ff_low(i, b, f):
                dve.wait_ge(ff_rounded, 2 * i + (b + 1))
                dve.tensor_tensor(ff_lo[b][:, :], ff_tile(f), ff_hi[b][:, :].bitcast(F32), ALU.subtract).then_inc(ff_split, 1)

            for b in range(2):
                ff_low(0, b, b)
            with dve.Fori(1, NF // 2) as i:
                for b in range(2):
                    ff_low(i, b, 2 * i + b)

            dve.wait_ge(gpost_landed, 16)
            for t in range(TT):
                n = FPOST + t
                tokens_ready(dve, n)
                rsqrt_mean(n, D)
                normed = conv[:, t % 2, :, :].rearrange("p b n -> p (b n)")
                stt(normed, token_bank(t), st(3, n), g_ffn_post[:, :], ALU.mult, ALU.mult)
                dve.tensor_tensor(x1[:, t, :], x1[:, t, :], normed, ALU.add).then_inc(out_ready, 1)


_OUT = (1, L, D)


def _columns():
    r = np.arange(P)
    cols = {}
    for j in range(KQ):
        cols[("cq", j)] = ("w_in", O_CQ + j * P + r)
    for j in range(KKV):
        cols[("ckv", j)] = ("w_in", O_CKV + j * P + r)
    half = ROPE // 2
    cols[("kr", 0)] = ("w_in", O_KR + np.concatenate([np.tile(np.arange(half), 4), np.tile(half + np.arange(half), 4)]))
    for n in range(NG):
        cols[("gate", n)] = ("w_in", O_GATE + n * P + r)
    for j in range(NU):
        cols[("u", j)] = ("w_in", O_U + j * P + r)
    for g in range(2):
        heads = [HG * g + h for h in range(HG)]
        for m in range(2):
            cols[("uq", 3 * g + m)] = ("w_uq", np.concatenate([h * QK + np.arange(NOPE) for h in heads[2 * m:2 * m + 2]]))
        cols[("uq", 3 * g + 2)] = ("w_uq", np.concatenate(
            [h * QK + NOPE + c * half + np.arange(half) for c in range(2) for h in heads]))
    for m in range(NU):
        cols[("glu", m)] = ("w_glu", m * P + r)
    for m in range(KD):
        cols[("attn_out", m)] = ("w_branch_attn", m * P + r)
        cols[("ssm_out", m)] = ("w_branch_ssm", m * P + r)
    for f in range(2 * NF):
        cols[("up", f)] = ("w_up", f * P + r)
    return cols


def _lay_out_stream(w):
    stream = np.zeros((NCHUNK, P, CH), np.float32)
    cols = _columns()
    tiles = CH // P
    for n, (name, part) in enumerate(ORDER):
        kind, j = name
        if name in cols:
            mat, c = cols[name]
            block = w[mat][part * CH:(part + 1) * CH][:, c]
            k = block.shape[0] // P
            stream[n, :, :k * P] = block.reshape(k, P, P).transpose(1, 0, 2).reshape(P, k * P)
        elif kind == "uk":
            block = w["w_uk"][:, j * HG * NOPE:(j + 1) * HG * NOPE]
            stream[n] = block.reshape(KKV, P, tiles // KKV, P).transpose(1, 2, 0, 3).reshape(P, CH)
        elif kind == "uv":
            stream[n] = w["w_uv"][part * P:(part + 1) * P]
        else:
            mat = w[{"w_out": "w_out", "down": "w_down"}[kind]]
            stream[n] = mat[j * P:(j + 1) * P, part * CH:(part + 1) * CH]
    return stream


def kernel(**inputs):
    import concourse.bacc as bacc
    from concourse.bass_utils import run_bass_kernel_spmd as run

    a = {name: np.asarray(v) for name, v in inputs.items()}
    w = {name: a[name][0] for name in ("w_in", "w_uq", "w_uk", "w_uv", "w_glu", "w_branch_attn", "w_branch_ssm",
                                       "w_out", "w_up", "w_down")}

    def tiles(v):
        return v.reshape(-1, P).T

    rows = np.arange(P)
    inv = (np.float32(10000.0) ** (-np.arange(0, ROPE, 2, dtype=np.float32) / np.float32(ROPE))).astype(np.float32)
    shape_columns = np.stack([inv[rows % (ROPE // 2)], (rows % ROPE < ROPE // 2), (rows % ROPE >= ROPE // 2),
                              np.where(rows < P // 2, 1.0, -1.0)], axis=1).astype(np.float32)
    conv_rows = np.concatenate([a["conv_w"][0], a["conv_b"]], axis=0)
    vecs = np.concatenate([tiles(a["q_norm"][0]), tiles(a["kv_norm"][0]), tiles(a["b_gate"][0]), tiles(a["b_glu"][0]),
                           shape_columns, tiles(conv_rows)], axis=1)
    norms = np.concatenate([a["mix_norm_pre"], a["mix_norm_post"], a["ffn_norm_pre"], a["ffn_norm_post"]], axis=0)

    def states(v):
        v = v.reshape(PAIRS, 2, NS, *v.shape[2:])
        return np.moveaxis(v, 0, 2).reshape(P, PAIRS, *v.shape[3:])

    ldt = np.broadcast_to(a["ssm_log_dt"][0][:, None], (GROUPS, NS))
    ssm_small = np.stack([states(a["ssm_lambda_re"][0]), states(a["ssm_lambda_im"][0]), states(ldt)], axis=1)
    ssm_bc = np.stack([states(a["ssm_b_re"][0]), states(a["ssm_b_im"][0]),
                       states(a["ssm_c_re"][0].transpose(0, 2, 1)), states(a["ssm_c_im"][0].transpose(0, 2, 1))], axis=1)
    ssm_d = a["ssm_d"][0].reshape(PAIRS, HALF).T

    nc = bacc.Bacc("TRN2", target_bir_lowering=False, num_devices=1)
    arrays = {"w_stream": _lay_out_stream(w), "x": a["x"][0], "positions": a["positions"], "vecs": vecs, "norms": norms,
              "ssm_small": ssm_small, "ssm_bc": ssm_bc, "ssm_d": ssm_d}
    arrays = {f"in_{n}_dram": np.ascontiguousarray(v) for n, v in arrays.items()}
    args = [nc.dram_tensor(n, v.shape, mybir.dt.from_np(v.dtype), kind="ExternalInput").ap() for n, v in arrays.items()]
    out = nc.dram_tensor("out_0_dram", _OUT, F32, kind="ExternalOutput").ap()
    build(nc, *args, out.rearrange("a l d -> (a l) d"))
    result = run(nc, [arrays], core_ids=[0])
    return result.results[0]["out_0_dram"]
```

```python
from contextlib import ExitStack
import math

import numpy as np

import concourse.bass as bass
from concourse import mybir
from concourse.alu_op_type import AluOpType as ALU

ACT = mybir.ActivationFunctionType
F32 = mybir.dt.float32
F32R = mybir.dt.float32r
I32 = mybir.dt.int32
AX_X = mybir.AxisListType.X

P = 128
D = 1024
L = 512
NH = 8
NOPE = 64
ROPE = 32
QK = NOPE + ROPE
VD = 64
RQ = 384
RKV = 256
WS = 512
GROUPS = 32
GH = 16
NS = 64
FF = 2816
EPS = 1e-6
TT = L // P
KD = D // P
KQ = RQ // P
KKV = RKV // P
NG = 2 * D // P
NF = FF // P
NU = WS // P
HG = NH // 2
CH = 512
RING = 4
HALF = 2 * GH

PAIRS = GROUPS // 2
SUB = 4
NC = L // SUB
PPT = 4

O_CQ, O_CKV, O_KR, O_U, O_GATE = 0, RQ, RQ + RKV, RQ + RKV + ROPE, RQ + RKV + ROPE + WS

ROUND = 12582912.0
TURN_UNIT = 65536.0
TURN_IN = 0.4999999
TURNS = (round(SUB / (2 * math.pi) * 4096) / 4096, SUB / (2 * math.pi) - round(SUB / (2 * math.pi) * 4096) / 4096)
TWO_PI = (6.28125, 0.001934051513671875, 2 * math.pi - 6.28125 - 0.001934051513671875)
PI_IN = 3.1415925
LN2 = (0.693359375, math.log(2) - 0.693359375)
EXP_TAYLOR = [1 / math.factorial(n) for n in range(8)]
MASKED = -3.0e38

GATES_FIRST = 3
GATES_SSM = (2, 2, 2, 1)
GATES_ATTN = (2, 2)
Y_STEPS = (3, 7, 11, 15)
ANGLE_ROUNDS = ((6, 7), (8, 9), (9, 9))
V_BANK = (0, 1, 3, 4)
KROPE_DMAS, QROPE_DMAS = 4, 8


def stream_plan():
    order = []
    gate = [0]

    def add(name, parts):
        order.extend((name, i) for i in range(parts))

    def gates(n):
        for _ in range(n):
            add(("gate", gate[0]), 2)
            gate[0] += 1

    for j in range(NU):
        add(("u", j), 2)
    for j in range(KQ):
        add(("cq", j), 2)
    for j in range(KKV):
        add(("ckv", j), 2)
    add(("kr", 0), 2)
    gates(GATES_FIRST)
    for n in GATES_SSM:
        gates(n)
    add(("uq", 2), 1)
    add(("uv", 0), KKV)
    for g in range(2):
        if g:
            add(("uq", 3 * g + 2), 1)
        add(("uk", g), 1)
        add(("uq", 3 * g), 1)
        add(("uq", 3 * g + 1), 1)
        gates(1)
        gates(GATES_ATTN[g])
    assert gate[0] == NG
    for m in range(NU):
        add(("glu", m), 1)
    for m in range(KD):
        add(("attn_out", m), 1)
        add(("ssm_out", m), 1)
    for j in range(KD):
        add(("w_out", j), 2)
    for f in range(NF):
        add(("up", f), 2)
        add(("up", NF + f), 2)
    for f in range(NF):
        add(("down", f), 2)
    first, end = {}, {}
    for n, (name, _) in enumerate(order):
        first.setdefault(name, n)
        end[name] = n + 1
    return order, first, end


ORDER, FIRST, END = stream_plan()
GATES_BEFORE = {name: sum(other[0] == "gate" for other in FIRST if FIRST[other] < FIRST[name]) for name in FIRST}
NCHUNK = len(ORDER)

ROPE_ROUNDS = tuple((END[("uq", 3 * g + 1)] + RING) // RING for g in range(2))

V_QN, V_KVN = 0, KQ
V_BG = V_KVN + KKV
V_BGLU = V_BG + NG
V_INV = V_BGLU + NU
V_EVEN, V_ODD, V_SIGN = V_INV + 1, V_INV + 2, V_INV + 3
V_QUARTER = V_SIGN + 1
V_CONV = V_QUARTER + 1
NV = V_CONV + 4 * 2 * NF

S_NAMES = ["lr", "li", "ldt", "dt", "y", "n", "r", "p", "mag", "ang", "k", "sn", "cs", "ar", "ai",
           "den", "t0", "t1", "t2", "zr", "zi", "m4"]
S_NAMES += ["t3", "turn", "turn_hi", "turn_lo"]
SI = {n: i for i, n in enumerate(S_NAMES)}

KB = 1024
BASE = 16512


def build(nc, w_stream, x, positions, vecs, steps_row, norms, ssm_small, ssm_bc, ssm_d, out):
    x_t = x.rearrange("(t p) d -> t p d", p=P)
    out_t = out.rearrange("(t p) d -> t p d", p=P)
    ctx = ExitStack()
    with ctx:
        def at(name, offset, shape, dt=F32):
            return nc.alloc_sbuf_tensor_at(name, shape, dt, offset=BASE + offset)

        raw = at("raw", 0, [P, RING, CH])
        w_hi = at("w_hi", 8 * KB, [P, RING, CH], F32R)
        w_lo = at("w_lo", 16 * KB, [P, RING, CH], F32R)
        xT_hi = at("xT_hi", 24 * KB, [P, KD, L], F32R)
        xT_lo = at("xT_lo", 40 * KB, [P, KD, L], F32R)
        ident = at("ident", 56 * KB, [P, P])
        causal_r = at("causal_r", 56 * KB + 512, [P, P], F32R)
        ones = at("ones", 57 * KB, [P, P])
        vec = at("vec", 57 * KB + 512, [P, NV])
        stat = at("stat", 58 * KB + 576, [P, 4, 4 * TT])
        rowst = at("rowst", 58 * KB + 832, [P, 4, 4])
        small = at("small", 58 * KB + 896, [P, len(S_NAMES), PAIRS])
        pw = at("pw", 60 * KB + 512, [P, 2, SUB, PAIRS])
        za = at("za", 61 * KB, [P, 2, SUB, PAIRS])
        ident_r = at("ident_r", 61 * KB + 512, [P, P], F32R)
        k_int = at("k_int", 62 * KB, [P, PAIRS], I32)
        d_skip = at("d_skip", 62 * KB + 64, [HALF, PAIRS])
        hb_gate = at("hb_gate", 62 * KB + 128, [P, NG])
        hb_glu = at("hb_glu", 62 * KB + 192, [P, NU])
        R = 62 * KB + 256

        def reg(name, kb, shape, dt=F32):
            return at(name, R + int(kb * KB), shape, dt)

        x_sq = reg("x_sq", 0, [P, 2, D])
        x_in = reg("x_in", 20, [P, TT, D])
        xn = reg("xn", 121, [P, 2, D])
        g_mix_pre = reg("g_mix_pre", 129, [P, D])
        causal = reg("causal", 133, [P, P])
        turn_steps = reg("turn_steps", 145, [P, NC])
        gates = reg("gates", 113, [P, NG, L])
        c_raw = reg("c_raw", 121, [P, KQ + KKV, L])
        r_bc = reg("r_bc", 131, [P, 2, L])
        kr_f = reg("kr_f", 139, [P, L])
        cos_t = reg("cos_t", 141, [P, L])
        sin_t = reg("sin_t", 143, [P, L])
        c_sq = reg("c_sq", 10, [P, KQ + KKV, L])
        cn_hi = reg("cn_hi", 0, [P, KQ + KKV, L], F32R)
        cn_lo = reg("cn_lo", 10, [P, KQ + KKV, L], F32R)
        rot_ab = [(reg("rot_a0", 80, [P, L]), reg("rot_b0", 82, [P, L])), (reg("rot_a1", 105, [P, L]), reg("rot_b1", 107, [P, L]))]
        ang = reg("ang", 87, [P, L])
        ang_k = reg("ang_k", 89, [P, L])
        pos_i = reg("pos_i", 91, [P, L], I32)
        u_hi = reg("u_hi", 20, [P, NU, PPT, NC], F32R)
        u_lo = reg("u_lo", 28, [P, NU, PPT, NC], F32R)
        rot_c = reg("rot_c", 36, [P, PAIRS, NC])
        rot_s = reg("rot_s", 44, [P, PAIRS, NC])
        ab = reg("ab", 52, [P, SUB, 2, PAIRS, GH])
        ca = reg("ca", 60, [P, SUB + 1, 2, PAIRS, GH])
        ba_blk = reg("ba_blk", 70, [P, 2, PPT, SUB, HALF])
        ca_blk = reg("ca_blk", 74, [P, 2, PPT, SUB + 1, HALF])
        ba_hi = reg("ba_hi", 79, [P, 2, PPT, P], F32R)
        ba_lo = reg("ba_lo", 83, [P, 2, PPT, P], F32R)
        ca_hi = reg("ca_hi", 87, [P, 2, PPT, SUB, HALF], F32R)
        ca_lo = reg("ca_lo", 91, [P, 2, PPT, SUB, HALF], F32R)
        kn_hi = reg("kn_hi", 95, [P, PPT, SUB, HALF], F32R)
        kn_lo = reg("kn_lo", 97, [P, PPT, SUB, HALF], F32R)
        z_t = reg("z_t", 99, [P, 2, L])
        m_t = reg("m_t", 103, [P, 2, L])
        s_hi = reg("s_hi", 107, [P, 2, PPT, NC], F32R)
        s_lo = reg("s_lo", 135, [P, 2, PPT, NC], F32R)
        decay = reg("decay", 111, [P, PPT, NC])
        bc_in = reg("bc_in", 103, [P, 4, PAIRS, GH])
        bt = reg("bt", 0, [P, 2, SUB, PAIRS, GH])
        y_f = [reg(f"y_f{i}", 20 + 2 * i, [P, L]) for i in range(NU)]
        q_hl = reg("q_hl", 28, [P, 2, HG, L], F32R)
        k_hl = reg("k_hl", 44, [P, 2, HG, L], F32R)
        q_hi, q_lo, k_hi, k_lo = q_hl[:, 0], q_hl[:, 1], k_hl[:, 0], k_hl[:, 1]
        v_hi = reg("v_hi", 60, [P, TT, L], F32R)
        v_lo = reg("v_lo", 68, [P, TT, L], F32R)
        pT_hi = reg("pT_hi", 76, [P, TT, L], F32R)
        pT_lo = reg("pT_lo", 84, [P, TT, L], F32R)
        qr_hl = [reg("qr_hl0", 76, [P, 2, L], F32R), reg("qr_hl1", 109, [P, 2, L], F32R)]
        prob = reg("prob", 92, [P, 2, L])
        at_f = reg("at_f", 96, [P, NU, L])
        kr_hl = reg("kr_hl", 99, [P, 2, 2, L], F32R)
        y_hi = reg("y_hi", 0, [P, NU, L], F32R)
        y_lo = reg("y_lo", 8, [P, NU, L], F32R)
        at_hi = reg("at_hi", 28, [P, NU, L], F32R)
        at_lo = reg("at_lo", 36, [P, NU, L], F32R)
        glu_t = reg("glu_t", 44, [P, 2, L])
        glu_y = reg("glu_y", 48, [P, 2, L])
        ss_hi = reg("ss_hi", 52, [P, NU, L], F32R)
        ss_lo = reg("ss_lo", 60, [P, NU, L], F32R)
        mg_hi = reg("mg_hi", 68, [P, KD, L], F32R)
        mg_lo = reg("mg_lo", 84, [P, KD, L], F32R)
        mg_t = reg("mg_t", 100, [P, 2, 2, L])
        x1 = reg("x1", 0, [P, TT, D])
        g_mix_post = reg("g_mix_post", 16, [P, D])
        g_ffn_pre = reg("g_ffn_pre", 20, [P, D])
        xn2 = reg("xn2", 24, [P, 2, D])
        sq = reg("sq", 32, [P, D])
        mixed = reg("mixed", 36, [P, 2, D])
        ff = reg("ff", 36, [P, NF, L])
        g_ffn_post = reg("g_ffn_post", 16, [P, D])
        conv = reg("conv", 80, [P, 2, 2, L])
        gelu = reg("gelu", 88, [P, 2, L])
        ff_hi = [reg(f"ff_hi{i}", 92 + 4 * i, [P, L], F32R) for i in range(2)]
        ff_lo = [reg(f"ff_lo{i}", 94 + 4 * i, [P, L], F32R) for i in range(2)]

        ps = ctx.enter_context(nc.psum_tensor("ps", [P, 8, L], F32))

        def sem(name):
            return ctx.enter_context(nc.semaphore(name))

        x_landed = [sem(f"x_landed{t}") for t in range(TT)]
        raw_landed = [sem(f"raw_landed{s}") for s in range(RING)]
        (g_landed, vec_landed, pos_landed, small_landed, bc_landed, x1_landed, gmid_landed,
         gpost_landed, krope_landed, qrope_landed, out_written) = [sem(n) for n in (
             "g_landed", "vec_landed", "pos_landed", "small_landed", "bc_landed", "x1_landed",
             "gmid_landed", "gpost_landed", "krope_landed", "qrope_landed", "out_written")]
        consts_ready, masks_rounded = sem("consts_ready"), sem("masks_rounded")
        weights_hi, weights_split, chunks_multiplied = sem("weights_hi"), sem("weights_split"), sem("chunks_multiplied")
        dve_step, pool_step, turn_split = sem("dve_step"), sem("pool_step"), sem("turn_split")
        sq_summed, ms_ready, rms_ready, xn_ready = sem("sq_summed"), sem("ms_ready"), sem("rms_ready"), sem("xn_ready")
        x_transposed, xT_rounded, xT_split = sem("x_transposed"), sem("xT_rounded"), sem("xT_split")
        x1_ready, mixed_ready = sem("x1_ready"), sem("mixed_ready")
        c_copied, c_squared, c_sums, c_totals = sem("c_copied"), sem("c_squared"), sem("c_sums"), sem("c_totals")
        c_ms, c_rms, cn_ready, cn_rounded, cn_split = (
            sem("c_ms"), sem("c_rms"), sem("cn_ready"), sem("cn_rounded"), sem("cn_split"))
        angle_ready, sine_ready = sem("angle_ready"), sem("sine_ready")
        kr_ready, kr_rounded, kr_split = sem("kr_ready"), sem("kr_rounded"), sem("kr_split")
        gate_done = sem("gate_done")
        v_rounded, v_split = sem("v_rounded"), sem("v_split")
        q_rounded, q_split, k_rounded, k_split = sem("q_rounded"), sem("q_split"), sem("k_rounded"), sem("k_split")
        qr_ready, qr_rounded, qr_split = sem("qr_ready"), sem("qr_rounded"), sem("qr_split")
        scores_done, max_ready, exp_done, probs_ready = sem("scores_done"), sem("max_ready"), sem("exp_done"), sem("probs_ready")
        probs_transposed, pT_rounded, pT_split = sem("probs_transposed"), sem("pT_rounded"), sem("pT_split")
        at_copied = sem("at_copied")
        values_summed, at_rounded, at_split = sem("values_summed"), sem("at_rounded"), sem("at_split")
        u_rounded, u_split = sem("u_rounded"), sem("u_split")
        compacts_ready, ba_blocks_ready, ca_blocks_ready, ba_transposed, kn_done = (
            sem("compacts_ready"), sem("ba_blocks_ready"), sem("ca_blocks_ready"), sem("ba_transposed"), sem("kn_done"))
        turns_folded = sem("turns_folded")
        first_turns_ready = sem("first_turns_ready")
        turns_ready, rotations_ready = sem("turns_ready"), sem("rotations_ready")
        skip_added, ba_rounded, ba_split = sem("skip_added"), sem("ba_rounded"), sem("ba_split")
        ca_rounded, ca_split, inputs_read = sem("ca_rounded"), sem("ca_split"), sem("inputs_read")
        bu_done, states_ready, states_rounded, states_split = (
            sem("bu_done"), sem("states_ready"), sem("states_rounded"), sem("states_split"))
        y_activated = sem("y_activated")
        y_summed, y_done, y_rounded, y_split = sem("y_summed"), sem("y_done"), sem("y_rounded"), sem("y_split")
        glu_tanh, glu_ready, ss_rounded, ss_split = sem("glu_tanh"), sem("glu_ready"), sem("ss_rounded"), sem("ss_split")
        mg_ready, mg_rounded, mg_split = sem("mg_ready"), sem("mg_rounded"), sem("mg_split")
        tokens_summed = sem("tokens_summed")
        conv_begun, conv_step, conv_done, gelu_done, ff_ready = (
            sem("conv_begun"), sem("conv_step"), sem("conv_done"), sem("gelu_done"), sem("ff_ready"))
        ff_rounded, ff_split = sem("ff_rounded"), sem("ff_split")
        out_ready, table_loaded = sem("out_ready"), sem("table_loaded")

        block = ctx.enter_context(nc.Block())

        PRE, POST, FPOST = 0, TT, 3 * TT
        MID = [(t, which) for step in range(TT + 1) for t, which in ((step, 0), (step - 1, 1)) if 0 <= t < TT]

        def st(row, n):
            return stat[:, row, n:n + 1]

        def sm(name):
            return small[:, SI[name], :]

        def rotation_angles(eng, link, signal):
            def angles(it, part):
                pr = slice(it * PPT, (it + 1) * PPT)
                n = turn_steps[:, :].unsqueeze(1).to_broadcast([P, PPT, NC])
                tn, th, tl = (sm(v)[:, pr].unsqueeze(2).to_broadcast([P, PPT, NC]) for v in ("turn", "turn_hi", "turn_lo"))
                a, b = rot_s[:, pr, :], rot_c[:, pr, :]
                if part == 0:
                    link(eng.tensor_tensor(b, n, tn, ALU.mult))
                    link(eng.tensor_scalar(b, b, ROUND, None, ALU.add, ALU.bypass))
                    link(eng.tensor_scalar(b, b, ROUND, None, ALU.subtract, ALU.bypass))
                    link(eng.tensor_tensor(a, n, th, ALU.mult))
                else:
                    link(eng.tensor_tensor(a, a, b, ALU.subtract))
                    link(eng.tensor_tensor(b, n, tl, ALU.mult))
                    link(eng.tensor_tensor(a, a, b, ALU.add))
                    eng.tensor_scalar(a, a, TURN_IN, -TURN_IN, ALU.min, ALU.max).then_inc(signal, 1)
            return angles

        @block.sync
        def _(sp):
            def load(c, s):
                sp.dma_start(raw[:, s, :], w_stream[bass.ds(c, 1), :, :].rearrange("c p n -> p (c n)")
                             ).then_inc(raw_landed[s], 16)

            sp.dma_start(small[:, 0:3, :], ssm_small).then_inc(small_landed, 16)
            for s in range(RING):
                load(s, s)
            sp.dma_start(pos_i[:, :], positions.partition_broadcast(P).rearrange("p a d -> p (a d)")).then_inc(pos_landed, 16)
            sp.dma_start(vec[:, :], vecs).then_inc(vec_landed, 16)
            sp.dma_start(turn_steps[:, :], steps_row.partition_broadcast(P).rearrange("p a d -> p (a d)")).then_inc(vec_landed, 16)
            sp.dma_start(bc_in[:, :, :, :], ssm_bc).then_inc(bc_landed, 16)
            sp.dma_start(d_skip[:, :], ssm_d).then_inc(bc_landed, 16)
            def rotary_keys():
                sp.wait_ge(kr_split, 2)
                for c in range(2):
                    for pair in range(2):
                        sp.dma_start(k_hl[NOPE + 32 * c:NOPE + 32 * (c + 1), :, 2 * pair:2 * pair + 2, :].bitcast(F32),
                                     kr_hl[64 * c:64 * c + 32, :, :, :].bitcast(F32)).then_inc(krope_landed, 16)

            def rotary_queries(g):
                if g:
                    sp.wait_ge(scores_done, HG * TT)
                else:
                    sp.wait_ge(y_summed, NU)
                sp.wait_ge(qr_split, g + 1)
                for c in range(2):
                    for h in range(HG):
                        sp.dma_start(q_hl[NOPE + 32 * c:NOPE + 32 * (c + 1), :, h, :].bitcast(F32),
                                     qr_hl[g][64 * c + 32 * (h // 2):64 * c + 32 * (h // 2) + 32, :, :].bitcast(F32)).then_inc(qrope_landed, 16)

            whole = NCHUNK // RING
            for part, (begin, end_) in enumerate(zip((1,) + ROPE_ROUNDS, ROPE_ROUNDS + (whole,))):
                if part == 1:
                    rotary_keys()
                if part:
                    rotary_queries(part - 1)
                with sp.Fori(begin, end_) as i:
                    for s in range(RING):
                        sp.wait_ge(weights_split, RING * i + (s + 1 - RING))
                        load(RING * i + s, s)
            for s in range(NCHUNK % RING):
                sp.wait_ge(weights_split, RING * whole + s + 1 - RING)
                load(RING * whole + s, s)
            for t in range(TT):
                sp.wait_ge(out_ready, t + 1)
                sp.dma_start(out_t[t, :, :], x1[:, t, :]).then_inc(out_written, 16)
            sp.wait_ge(out_written, 16 * TT)

        @block.gpsimd
        def _(pool):
            pool.memset(ident[:, :], 0.0).then_inc(consts_ready, 1)
            pool.memset(causal[:, :], 0.0).then_inc(consts_ready, 1)
            pool.memset(ones[:, :], 1.0).then_inc(consts_ready, 1)
            pool.wait_ge(consts_ready, 3)
            pool.affine_select(out=ident[:, :], in_=ident[:, :], compare_op=ALU.not_equal, fill=1.0,
                               base=0, pattern=[[-1, P]], channel_multiplier=1).then_inc(consts_ready, 1)
            pool.affine_select(out=causal[:, :], in_=causal[:, :], compare_op=ALU.is_ge, fill=MASKED,
                               base=0, pattern=[[-1, P]], channel_multiplier=1).then_inc(consts_ready, 1)

            steps = [0]

            def link(ins):
                ins.then_inc(pool_step, 1)
                steps[0] += 1
                pool.wait_ge(pool_step, steps[0])

            def split(i, s, first):
                pool.wait_ge(raw_landed[s], 16 * i + 16)
                if not first:
                    pool.wait_ge(chunks_multiplied, RING * i + (s + 1 - RING))
                pool.tensor_tensor(w_hi[:, s, 0:1], raw[:, s, 0:1], ones[:, 0:1], ALU.mult)
                pool.tensor_scalar(w_hi[:, s, 1:CH], raw[:, s, 1:CH], 1.0, 1.0, ALU.mult, ALU.mult).then_inc(weights_hi, 1)
                pool.wait_ge(weights_hi, RING * i + s + 1)
                pool.tensor_tensor(w_lo[:, s, :], raw[:, s, :], w_hi[:, s, :].bitcast(F32),
                                   ALU.subtract).then_inc(weights_split, 1)

            angles = rotation_angles(pool, link, turns_ready)

            for s in range(RING):
                split(0, s, True)
            round_ = 1
            for it in range(1, NU):
                for part in range(2):
                    until = ANGLE_ROUNDS[it - 1][part]
                    if until > round_:
                        with pool.Fori(round_, until) as i:
                            for s in range(RING):
                                split(i, s, False)
                    if part == 0:
                        pool.wait_ge(turn_split, 1)
                    angles(it, part)
                    round_ = max(until, round_)
            last_round, places = divmod(END[("w_out", KD - 1)], RING)
            with pool.Fori(round_, last_round) as i:
                for s in range(RING):
                    split(i, s, False)
            for s in range(places):
                split(last_round, s, False)
            pool.wait_ge(x1_landed, 16 * TT)
            for t in range(TT):
                pool.wait_ge(mixed_ready, t + 1)
                pool.tensor_tensor(x1[:, t, :], x1[:, t, :], mixed[:, t % 2, :], ALU.add).then_inc(x1_ready, 1)
            for s in range(places, RING):
                split(last_round, s, False)
            whole = NCHUNK // RING
            with pool.Fori(last_round + 1, whole) as i:
                for s in range(RING):
                    split(i, s, False)
            for s in range(NCHUNK % RING):
                split(whole, s, False)

        @block.tensor
        def _(pe):
            def three(o, wh, wl, xh, xl, start, stop):
                pe.matmul(o, wh, xh, start=start, stop=False, skip_group_check=True)
                pe.matmul(o, wh, xl, start=False, stop=False, skip_group_check=True)
                return pe.matmul(o, wl, xh, start=False, stop=stop, skip_group_check=True)

            def transpose_x(n):
                t = n % TT
                src = xn if n < TT else xn2
                pe.wait_ge(xn_ready, n + 1)
                for k in range(KD):
                    last = pe.transpose(ps[:, 2 * t + k // 4, (k % 4) * P:(k % 4 + 1) * P],
                                        src[:, t % 2, k * P:(k + 1) * P], ident[:, :])
                last.then_inc(x_transposed, 1)

            def chunk(name, part, bank, hi, lo, k0, nk, start, stop):
                c = FIRST[name] + part
                s = c % RING
                pe.wait_ge(weights_split, c + 1)
                for k in range(nk):
                    last = three(ps[:, bank, :], w_hi[:, s, k * P:(k + 1) * P], w_lo[:, s, k * P:(k + 1) * P],
                                 hi[:, k0 + k, :], lo[:, k0 + k, :], start and k == 0, stop and k == nk - 1)
                last.then_inc(chunks_multiplied, 1)

            def in_half(name, part, bank):
                chunk(name, part, bank, xT_hi, xT_lo, 4 * part, 4, part == 0, part == 1)

            def gate_half(n, part):
                if part == 0 and n >= 2:
                    pe.wait_ge(gate_done, n - 1)
                in_half(("gate", n), part, 6 + n % 2)

            def gate_piece(n, k):
                if k == 0:
                    pe.wait_ge(gate_done, n - 1)
                part = k // 4
                c = FIRST[("gate", n)] + part
                s = c % RING
                if k % 4 == 0:
                    pe.wait_ge(weights_split, c + 1)
                cols = slice((k % 4) * P, (k % 4 + 1) * P)
                last = three(ps[:, 6 + n % 2, :], w_hi[:, s, cols], w_lo[:, s, cols], xT_hi[:, k, :], xT_lo[:, k, :],
                             k == 0, k == KD - 1)
                if k % 4 == 3:
                    last.then_inc(chunks_multiplied, 1)

            def in_tile(name, bank):
                in_half(name, 0, bank)
                in_half(name, 1, bank)

            pe.wait_ge(consts_ready, 5)
            for t in range(TT):
                transpose_x(PRE + t)
            pe.wait_ge(xT_split, 2 * TT)
            for j in range(NU):
                in_tile(("u", j), j)
            for j in range(KQ):
                in_tile(("cq", j), 4 + j)
            in_tile(("ckv", 0), 7)
            pe.wait_ge(u_split, 1)
            in_tile(("ckv", 1), 0)
            pe.wait_ge(u_split, 2)
            in_tile(("kr", 0), 1)

            gate = [0]

            def gate_tiles(n):
                for _ in range(n):
                    gate_half(gate[0], 0)
                    gate_half(gate[0], 1)
                    gate[0] += 1

            pe.wait_ge(c_squared, 4)
            gate_tiles(2)
            pe.wait_ge(c_sums, 2)
            pe.wait_ge(c_copied, KQ + KKV)
            for b, bank in enumerate((5, 0)):
                last = pe.matmul(ps[:, bank, :], ones[:, :], c_sq[:, (0, KQ)[b], :], start=True, stop=True)
            last.then_inc(c_totals, 1)

            def turn_inputs(it):
                pe.wait_ge(ba_blocks_ready, 4 * (it + 1))
                if it == 0:
                    pe.wait_ge(kr_ready, 1)
                    pe.wait_ge(c_ms, 2)
                else:
                    pe.wait_ge(ba_split, it)
                for c in range(2):
                    for q in range(PPT):
                        last = pe.transpose(ps[:, c, q * P:(q + 1) * P],
                                            ba_blk[:, c, q, :, :].rearrange("p s h -> p (s h)"), ident[:, :])
                last.then_inc(ba_transposed, 1)

            def own_tokens(it):
                pe.wait_ge(ca_blocks_ready, 4 * (it + 1))
                if it == 0:
                    pe.wait_ge(u_split, NU)
                else:
                    pe.wait_ge(ca_split, it)
                for q in range(PPT):
                    for c in range(2):
                        last = pe.matmul(ps[0:HALF, 2, q * P:(q + 1) * P], ba_blk[:, c, q, SUB - 1, :],
                                         ca_blk[:, c, q, 0:SUB, :].rearrange("p s h -> p (s h)"),
                                         start=(c == 0), stop=(c == 1), skip_group_check=True)
                last.then_inc(kn_done, 1)

            def state_inputs(it):
                pe.wait_ge(ba_split, it + 1)
                if it:
                    pe.wait_ge(inputs_read, it)
                for c in range(2):
                    for q in range(PPT):
                        last = three(ps[:, 3 + c, q * NC:(q + 1) * NC], ba_hi[:, c, q, :], ba_lo[:, c, q, :],
                                     u_hi[:, it, q, :], u_lo[:, it, q, :], True, True)
                last.then_inc(bu_done, 1)

            def outputs(it):
                pe.wait_ge(ca_split, it + 1)
                pe.wait_ge(states_split, it + 1)
                if it:
                    pe.wait_ge(y_done, SUB * PPT * it)
                for q in range(PPT):
                    o = ps[:, 5, q * NC:(q + 1) * NC]
                    three(o, kn_hi[:, q, :, :].rearrange("p s h -> p (s h)"), kn_lo[:, q, :, :].rearrange("p s h -> p (s h)"),
                          u_hi[:, it, q, :], u_lo[:, it, q, :], True, False)
                    for c in range(2):
                        last = three(o, ca_hi[:, c, q, :, :].rearrange("p s h -> p (s h)"),
                                     ca_lo[:, c, q, :, :].rearrange("p s h -> p (s h)"),
                                     s_hi[:, c, q, :], s_lo[:, c, q, :], False, c == 1)
                last.then_inc(y_summed, 1)

            turn_inputs(0)
            own_tokens(0)
            gate_tiles(GATES_FIRST - 2)
            state_inputs(0)
            for it in range(NU - 1):
                gate_tiles(1)
                turn_inputs(it + 1)
                gate_tiles(GATES_SSM[it] - 1)
                state_inputs(it + 1)
                own_tokens(it + 1)
                outputs(it)
            gate_tiles(GATES_SSM[NU - 1])
            def rotary_queries(g):
                n = gate[0]
                pe.wait_ge(cn_split, KQ + KKV)
                pe.wait_ge(gate_done, n - 1)
                chunk(("uq", 3 * g + 2), 0, 6 + n % 2, cn_hi, cn_lo, 0, KQ, True, True)

            rotary_queries(0)
            pe.wait_ge(cn_split, KQ + KKV)
            pe.wait_ge(ca_split, NU)
            pe.wait_ge(inputs_read, NU)
            for kk in range(KKV):
                c = FIRST[("uv", 0)] + kk
                s = c % RING
                pe.wait_ge(weights_split, c + 1)
                for t in range(TT):
                    tok = slice(t * P, (t + 1) * P)
                    last = three(ps[:, V_BANK[t], :], cn_hi[:, KQ + kk, tok], cn_lo[:, KQ + kk, tok],
                                 w_hi[:, s, :], w_lo[:, s, :], kk == 0, kk == KKV - 1)
                last.then_inc(chunks_multiplied, 1)
            outputs(NU - 1)

            UNITS = HG * TT
            for g in range(2):
                pe.wait_ge(v_split, TT)
                if g:
                    pe.wait_ge(pT_split, UNITS)
                c = FIRST[("uk", g)]
                s = c % RING
                pe.wait_ge(weights_split, c + 1)
                for m, bank in enumerate((3, 0)):
                    for k in range(KKV):
                        cols = slice((2 * m + k) * P, (2 * m + k + 1) * P)
                        last = three(ps[:, bank, :], w_hi[:, s, cols], w_lo[:, s, cols],
                                     cn_hi[:, KQ + k, :], cn_lo[:, KQ + k, :], k == 0, k == KKV - 1)
                last.then_inc(chunks_multiplied, 1)
                for m, bank in enumerate((4, 5)):
                    if g:
                        pe.wait_ge(at_copied, HG - 1 + m)
                    elif m == 1:
                        pe.wait_ge(y_done, SUB * PPT * NU)
                    chunk(("uq", 3 * g + m), 0, bank, cn_hi, cn_lo, 0, KQ, True, True)
                pe.wait_ge(qr_ready, g + 1)
                gate_tiles(1)

                pe.wait_ge(q_split, HG * (g + 1))
                pe.wait_ge(k_split, HG * (g + 1))
                pe.wait_ge(krope_landed, 16 * KROPE_DMAS)
                pe.wait_ge(qrope_landed, 16 * QROPE_DMAS * (g + 1))
                pe.wait_ge(masks_rounded, 2)

                def scores(u):
                    h, i = u // TT, u % TT
                    if u >= 2:
                        pe.wait_ge(exp_done, UNITS * g + u - 1)
                    tok = slice(i * P, (i + 1) * P)
                    n = (i + 1) * P
                    three(ps[:, u % 2, 0:n], q_hi[:, h, tok], q_lo[:, h, tok],
                          k_hi[:, h, 0:n], k_lo[:, h, 0:n], True, False)
                    pe.matmul(ps[:, u % 2, i * P:n], ident_r[:, :], causal_r[:, :], start=False, stop=True,
                              skip_group_check=True).then_inc(scores_done, 1)

                def turn_probs(u):
                    if u >= 2 or g:
                        pe.wait_ge(pT_split, UNITS * g + u - 1)
                    pe.wait_ge(probs_ready, UNITS * g + u + 1)
                    for j in range(u % TT + 1):
                        last = pe.transpose(ps[:, 2 + u % 2, j * P:(j + 1) * P],
                                            prob[:, u % 2, j * P:(j + 1) * P], ident[:, :])
                    last.then_inc(probs_transposed, 1)

                def values(h, j):
                    head = HG * g + h
                    if j == 0:
                        pe.wait_ge(pT_split, UNITS * g + TT * (h + 1))
                        if head >= 2:
                            pe.wait_ge(at_copied, head - 1)
                    pair = slice((head // 2) * P, (head // 2 + 1) * P)
                    three(ps[:, 4 + h % 2, j * P:L], v_hi[:, j, pair], v_lo[:, j, pair],
                          pT_hi[:, j, j * P:L], pT_lo[:, j, j * P:L], j == 0, j == TT - 1).then_inc(values_summed, 1)

                piece = 0
                for t in range(UNITS + TT + 2):
                    if t < UNITS:
                        scores(t)
                    if t >= 6:
                        values((t - 6) // TT, (t - 6) % TT)
                    if 2 <= t < UNITS + 2:
                        turn_probs(t - 2)
                    if piece < KD * GATES_ATTN[g]:
                        gate_piece(gate[0], piece % KD)
                        piece += 1
                        if piece % KD == 0:
                            gate[0] += 1
                            if g == 0 and piece == KD * GATES_ATTN[g]:
                                rotary_queries(1)

            pe.wait_ge(y_split, NU)
            for m in range(NU):
                chunk(("glu", m), 0, m, y_hi, y_lo, 0, NU, True, True)
            for m in range(KD):
                b = 2 * (m % 2)
                if m >= 2:
                    pe.wait_ge(mg_ready, m - 1)
                else:
                    pe.wait_ge(glu_ready, NU)
                    pe.wait_ge(at_split, NU)
                chunk(("attn_out", m), 0, b, at_hi, at_lo, 0, NU, True, True)
                if m == 0:
                    pe.wait_ge(ss_split, NU)
                chunk(("ssm_out", m), 0, b + 1, ss_hi, ss_lo, 0, NU, True, True)

            def token_sums(c, stat_hi, stat_lo, tiles, half, start, stop, ready=None):
                s = c % RING
                for t in tiles:
                    if ready is not None:
                        ready(t)
                    tok = slice(t * P, (t + 1) * P)
                    last = three(ps[:, 2 * t + half, :], stat_hi[:, tok], stat_lo[:, tok],
                                 w_hi[:, s, :], w_lo[:, s, :], start, stop)
                return last

            def merged_read(t):
                if t == 0:
                    pe.wait_ge(mg_split, KD)

            for j in range(KD - 2):
                pe.wait_ge(mg_split, j + 1)
                for half in range(2):
                    c = FIRST[("w_out", j)] + half
                    pe.wait_ge(weights_split, c + 1)
                    token_sums(c, mg_hi[:, j, :], mg_lo[:, j, :], (2, 3, 0, 1), half, j == 0, False,
                               merged_read if j == 0 else None).then_inc(chunks_multiplied, 1)
            for t in range(TT):
                for j in (KD - 2, KD - 1):
                    for half in range(2):
                        c = FIRST[("w_out", j)] + half
                        pe.wait_ge(weights_split, c + 1)
                        last = token_sums(c, mg_hi[:, j, :], mg_lo[:, j, :], (t,), half, False, j == KD - 1)
                        if t == TT - 1:
                            last.then_inc(chunks_multiplied, 1)
                if t < TT - 1:
                    last.then_inc(tokens_summed, 1)
            for t in range(TT):
                transpose_x(TT + t)

            pe.wait_ge(xT_split, 4 * TT)
            up0 = FIRST[("up", 0)]

            def up_pair(i, b, first):
                if not first:
                    pe.wait_ge(conv_done, 4 * i + 2 * b - 2)
                for v in range(2):
                    for part in range(2):
                        q = 4 * b + 2 * v + part
                        s = (up0 + q) % RING
                        pe.wait_ge(weights_split, 8 * i + (up0 + q + 1))
                        for k in range(4):
                            last = three(ps[:, 2 * b + v, :], w_hi[:, s, k * P:(k + 1) * P],
                                         w_lo[:, s, k * P:(k + 1) * P], xT_hi[:, 4 * part + k, :],
                                         xT_lo[:, 4 * part + k, :], part == 0 and k == 0, part == 1 and k == 3)
                        last.then_inc(chunks_multiplied, 1)

            for b in range(2):
                up_pair(0, b, True)
            with pe.Fori(1, NF // 2) as i:
                for b in range(2):
                    up_pair(i, b, False)

            down0 = FIRST[("down", 0)]

            def down_pair(i):
                for b in range(2):
                    pe.wait_ge(ff_split, 2 * i + (b + 1))
                    for half in range(2):
                        q = 2 * b + half
                        pe.wait_ge(weights_split, 4 * i + (down0 + q + 1))
                        token_sums(down0 + q, ff_hi[b], ff_lo[b], (2, 3, 0, 1), half, False, False
                                   ).then_inc(chunks_multiplied, 1)

            for tokens in ((2, 3), (0, 1)):
                if tokens[0] == 0:
                    pe.wait_ge(conv_done, 2 * NF)
                for b in range(2):
                    pe.wait_ge(ff_split, b + 1)
                    for half in range(2):
                        c = down0 + 2 * b + half
                        pe.wait_ge(weights_split, c + 1)
                        last = token_sums(c, ff_hi[b], ff_lo[b], tokens, half, b == 0, False)
                        if tokens[0] == 0:
                            last.then_inc(chunks_multiplied, 1)
            with pe.Fori(1, NF // 2 - 1) as i:
                down_pair(i)
            for t in range(TT):
                for b in range(2):
                    for half in range(2):
                        c = FIRST[("down", NF - 2 + b)] + half
                        pe.wait_ge(ff_split, NF - 1 + b)
                        pe.wait_ge(weights_split, c + 1)
                        last = token_sums(c, ff_hi[b], ff_lo[b], (t,), half, False, b == 1)
                        if t == TT - 1:
                            last.then_inc(chunks_multiplied, 1)
                if t < TT - 1:
                    last.then_inc(tokens_summed, 1)

        def cv(row, v, f):
            at0 = V_CONV + (2 * row + v) * NF
            return vec[:, at0 + f:at0 + f + 1] if isinstance(f, int) else vec[:, bass.ds(f + at0, 1)]

        def ff_tile(f):
            return ff[:, f, :] if isinstance(f, int) else ff[:, bass.ds(f, 1), :].rearrange("p a n -> p (a n)")

        def token_bank(t):
            return ps[:, 2 * t:2 * t + 2, :].rearrange("p b n -> p (b n)")

        def tokens_ready(eng, n):
            t = n % TT
            if t < TT - 1:
                eng.wait_ge(tokens_summed, (TT - 1) * (n // (2 * TT)) + t + 1)
            else:
                eng.wait_ge(chunks_multiplied, END[("w_out", KD - 1)] if n < FPOST else NCHUNK)

        @block.scalar
        def _(act):
            for t in range(TT):
                act.dma_start(x_in[:, t, :], x_t[t, :, :]).then_inc(x_landed[t], 16)
                if t == 0:
                    act.dma_start(g_mix_pre[:, :], norms[0:1, :].partition_broadcast(P).rearrange("p a d -> p (a d)")).then_inc(g_landed, 16)

            def square_sum(n, squares, src):
                act.activation(squares, src, ACT.Square, accum_out=st(0, n)).then_inc(sq_summed, 1)

            def root(n):
                act.wait_ge(ms_ready, n + 1)
                act.activation(st(2, n), st(1, n), ACT.Sqrt).then_inc(rms_ready, 1)

            def round_xT(n):
                t = n % TT
                act.wait_ge(x_transposed, n + 1)
                for b in range(2):
                    act.activation(xT_hi[:, 4 * b:4 * b + 4, t * P:(t + 1) * P],
                                   ps[:, 2 * t + b, :].rearrange("p (k n) -> p k n", k=4),
                                   ACT.Copy).then_inc(xT_rounded, 1)

            for t in range(TT):
                act.wait_ge(x_landed[t], 16)
                if t >= 2:
                    act.wait_ge(sq_summed, t - 1)
                square_sum(PRE + t, x_sq[:, t % 2, :], x_in[:, t, :])
                root(PRE + t)
                if t >= 1:
                    round_xT(t - 1)
            round_xT(TT - 1)
            act.wait_ge(angle_ready, 1)
            act.activation(sm("sn"), sm("r"), ACT.Sin).then_inc(sine_ready, 1)
            act.wait_ge(angle_ready, 2)
            act.activation(sin_t[:, :], ang[:, :], ACT.Sin).then_inc(sine_ready, 1)
            act.wait_ge(angle_ready, 3)
            act.activation(cos_t[:, :], ang[:, :], ACT.Sin).then_inc(sine_ready, 1)
            act.wait_ge(angle_ready, 4)
            act.activation(sm("cs"), sm("r"), ACT.Sin).then_inc(sine_ready, 1)

            for j in range(NU):
                act.wait_ge(chunks_multiplied, END[("u", j)])
                for s in range(SUB):
                    for q in range(PPT):
                        act.activation(u_hi[HALF * s:HALF * (s + 1), j, q, :],
                                       ps[HALF * q:HALF * (q + 1), j, s::SUB], ACT.Copy).then_inc(u_rounded, 1)
            for j in range(KQ + KKV):
                name = ("cq", j) if j < KQ else ("ckv", j - KQ)
                bank = (4 + j) % 8
                act.wait_ge(chunks_multiplied, END[name])
                act.activation(c_raw[:, j, :], ps[:, bank, :], ACT.Copy).then_inc(c_copied, 1)
                act.activation(c_sq[:, j, :], ps[:, bank, :], ACT.Square).then_inc(c_squared, 1)

            def gate_tanh(n):
                act.wait_ge(chunks_multiplied, END[("gate", n)])
                act.activation(gates[:, n, :], ps[:, 6 + n % 2, :], ACT.Tanh, bias=hb_gate[:, n:n + 1],
                               scale=0.5).then_inc(gate_done, 1)

            gate = [0]

            def gate_tanhs(n):
                for _ in range(n):
                    gate_tanh(gate[0])
                    gate[0] += 1

            def blocks(dst, src, it, ready):
                pr = slice(it * PPT, (it + 1) * PPT)
                for c in range(2):
                    for e in range(2):
                        rows, cols = slice(NS * e, NS * (e + 1)), slice(GH * e, GH * (e + 1))
                        act.activation(dst[rows, c, :, :, cols], src[rows, :, c, pr, :].rearrange("p s q h -> p q s h"),
                                       ACT.Copy).then_inc(ready, 1)

            def rotations(it):
                pr = slice(it * PPT, (it + 1) * PPT)
                if it == 0:
                    act.wait_ge(first_turns_ready, 1)
                else:
                    act.wait_ge(turns_ready, it)
                act.activation(rot_c[:, pr, :], rot_s[:, pr, :], ACT.Abs).then_inc(turns_folded, 1)
                act.wait_ge(turns_folded, it + 1)
                act.activation(rot_c[:, pr, :], rot_c[:, pr, :], ACT.Sin, bias=vec[:, V_QUARTER:V_QUARTER + 1],
                               scale=-2 * math.pi)
                act.activation(rot_s[:, pr, :], rot_s[:, pr, :], ACT.Sin, scale=2 * math.pi).then_inc(rotations_ready, 1)

            def round_inputs(it):
                act.wait_ge(ba_transposed, it + 1)
                if it:
                    act.wait_ge(bu_done, it)
                for c in range(2):
                    act.activation(ba_hi[:, c, :, :], ps[:, c, :].rearrange("p (q n) -> p q n", q=PPT),
                                   ACT.Copy).then_inc(ba_rounded, 1)

            def round_outputs(it):
                act.wait_ge(ca_blocks_ready, 4 * (it + 1))
                if it:
                    act.wait_ge(y_summed, it)
                for c in range(2):
                    act.activation(ca_hi[:, c, :, :, :], ca_blk[:, c, :, 1:SUB + 1, :], ACT.Copy).then_inc(ca_rounded, 1)
                act.wait_ge(skip_added, it + 1)
                for s in range(SUB):
                    act.activation(kn_hi[HALF * s:HALF * (s + 1), :, s:SUB, :],
                                   ps[0:HALF, 2, :].rearrange("p (q t h) -> p q t h", q=PPT, t=SUB)[:, :, 0:SUB - s, :],
                                   ACT.Copy).then_inc(ca_rounded, 1)

            def round_states(it):
                act.wait_ge(states_ready, it + 1)
                act.activation(s_hi[:, :, :, 1:NC], z_t[:, :, :].rearrange("p c (q n) -> p c q n", q=PPT)[:, :, :, 0:NC - 1],
                               ACT.Copy).then_inc(states_rounded, 1)

            def unfold(it, function):
                act.wait_ge(y_summed, it + 1)
                for s in range(SUB):
                    for q in range(PPT):
                        act.activation(y_f[it][HALF * q:HALF * (q + 1), s::SUB],
                                       ps[HALF * s:HALF * (s + 1), 5, q * NC:(q + 1) * NC],
                                       function).then_inc(y_done, 1)

            act.wait_ge(compacts_ready, 1)
            blocks(ba_blk, ab, 0, ba_blocks_ready)
            blocks(ca_blk, ca, 0, ca_blocks_ready)
            gate_tanhs(2)
            act.wait_ge(c_ms, 2)
            act.activation(r_bc[:, :, :], r_bc[:, :, :], ACT.Sqrt).then_inc(c_rms, 1)
            rotations(0)
            round_inputs(0)
            round_outputs(0)
            gate_tanhs(GATES_FIRST - 2)
            for j in range(KQ + KKV):
                act.wait_ge(cn_ready, j + 1)
                act.activation(cn_hi[:, j, :], c_raw[:, j, :], ACT.Copy).then_inc(cn_rounded, 1)
            for it in range(NU):
                if it + 1 < NU:
                    act.wait_ge(kn_done, it + 1)
                    blocks(ba_blk, ab, it + 1, ba_blocks_ready)
                if it:
                    round_outputs(it)
                    unfold(it - 1, ACT.Copy)
                if it + 1 < NU:
                    round_inputs(it + 1)
                    gate_tanhs(1)
                    act.wait_ge(ca_split, it + 1)
                    blocks(ca_blk, ca, it + 1, ca_blocks_ready)
                round_states(it)
                if it + 1 < NU:
                    rotations(it + 1)
                if it == 0:
                    act.wait_ge(cn_split, KQ + KKV)
                gate_tanhs(GATES_SSM[it] - int(it + 1 < NU))
            act.wait_ge(chunks_multiplied, END[("uv", 0)])
            for t in range(TT):
                act.activation(v_hi[:, t, :], ps[:, V_BANK[t], :], ACT.Copy).then_inc(v_rounded, 1)
            act.wait_ge(states_split, NU)
            for e, col in enumerate((V_EVEN, V_ODD)):
                act.activation(kr_hl[:, 0, e, :], kr_f[:, :], ACT.Copy, scale=vec[:, col:col + 1]).then_inc(kr_rounded, 1)

            UNITS = HG * TT
            scale = 1.0 / math.sqrt(QK)

            def round_rotary(g):
                act.wait_ge(qr_ready, g + 1)
                act.activation(qr_hl[g][:, 0, :], rot_ab[g][0][:, :], ACT.Copy, scale=scale).then_inc(qr_rounded, 1)

            act.wait_ge(y_done, SUB * PPT * (NU - 1))
            for j in range(NU - 1):
                act.activation(y_f[j][:, :], y_f[j][:, :], ACT.Gelu_apprx_tanh).then_inc(y_activated, 1)
            unfold(NU - 1, ACT.Gelu_apprx_tanh)
            for g in range(2):
                if g == 0:
                    round_rotary(0)
                act.wait_ge(chunks_multiplied, END[("uk", g)])
                for m, bank in enumerate((3, 0)):
                    for e in range(2):
                        act.activation(k_hi[0:NOPE, 2 * m + e, :], ps[e * NOPE:(e + 1) * NOPE, bank, :],
                                       ACT.Copy).then_inc(k_rounded, 1)
                for m, bank in enumerate((4, 5)):
                    act.wait_ge(chunks_multiplied, END[("uq", 3 * g + m)])
                    for e in range(2):
                        act.activation(q_hi[0:NOPE, 2 * m + e, :], ps[e * NOPE:(e + 1) * NOPE, bank, :],
                                       ACT.Copy, scale=scale).then_inc(q_rounded, 1)
                gate_tanhs(1)

                def copy_head(h):
                    head, e = HG * g + h, h % 2
                    act.wait_ge(values_summed, TT * (head + 1))
                    act.activation(at_f[e * VD:(e + 1) * VD, head // 2, :], ps[e * VD:(e + 1) * VD, 4 + e, :],
                                   ACT.Copy).then_inc(at_copied, 1)

                for t in range(UNITS + TT + 3):
                    if t < UNITS:
                        n = (t % TT + 1) * P
                        act.wait_ge(max_ready, UNITS * g + t + 1)
                        if t >= 2:
                            act.wait_ge(probs_transposed, UNITS * g + t - 1)
                        act.activation(prob[:, t % 2, 0:n], ps[:, t % 2, 0:n], ACT.Exp, bias=rowst[:, 0, t % 4:t % 4 + 1],
                                       accum_out=rowst[:, 1, t % 4:t % 4 + 1]).then_inc(exp_done, 1)
                    if 2 <= t < UNITS + 2:
                        u = t - 2
                        i = u % TT
                        act.wait_ge(probs_transposed, UNITS * g + u + 1)
                        if u >= TT or g:
                            act.wait_ge(values_summed, UNITS * g + u - TT + 1)
                        act.activation(pT_hi[:, 0:i + 1, i * P:(i + 1) * P],
                                       ps[:, 2 + u % 2, 0:(i + 1) * P].rearrange("p (j n) -> p j n", n=P),
                                       ACT.Copy).then_inc(pT_rounded, 1)
                    if g == 0 and t == UNITS + 2:
                        round_rotary(1)
                    if t >= 10 and (t - 10) % TT == 0:
                        copy_head((t - 10) // TT)
                    if g and t in Y_STEPS:
                        j = Y_STEPS.index(t)
                        act.wait_ge(y_activated, NU - 1)
                        act.wait_ge(y_done, SUB * PPT * NU)
                        act.activation(y_hi[:, j, :], y_f[j][:, :], ACT.Copy).then_inc(y_rounded, 1)
                    if t % KD == 0 and 0 < t // KD <= GATES_ATTN[g]:
                        gate_tanhs(1)
            act.wait_ge(at_copied, NH)
            for j in range(NU):
                act.activation(at_hi[:, j, :], at_f[:, j, :], ACT.Copy).then_inc(at_rounded, 1)
            for m in range(NU):
                act.wait_ge(chunks_multiplied, END[("glu", m)])
                if m >= 2:
                    act.wait_ge(glu_ready, m - 1)
                act.activation(glu_t[:, m % 2, :], ps[:, m, :], ACT.Tanh, bias=hb_glu[:, m:m + 1],
                               scale=0.5).then_inc(glu_tanh, 1)
                act.wait_ge(glu_ready, m + 1)
                act.activation(ss_hi[:, m, :], glu_y[:, m % 2, :], ACT.Copy, scale=0.5).then_inc(ss_rounded, 1)
            for m in range(KD):
                act.wait_ge(mg_ready, m + 1)
                act.activation(mg_hi[:, m, :], mg_t[:, m % 2, 0, :], ACT.Copy, scale=0.5).then_inc(mg_rounded, 1)
                if m == 0:
                    act.wait_ge(ss_split, NU)
                    for t in range(TT):
                        act.dma_start(x1[:, t, :], x_t[t, :, :]).then_inc(x1_landed, 16)
                    act.wait_ge(chunks_multiplied, END[("glu", NU - 1)])
                    for n, dst in ((1, g_mix_post), (2, g_ffn_pre)):
                        act.dma_start(dst[:, :], norms[n:n + 1, :].partition_broadcast(P).rearrange("p a d -> p (a d)")).then_inc(gmid_landed, 16)

            act.activation(st(2, POST), ones[:, 0:1], ACT.Sqrt).then_inc(table_loaded, 1)
            act.wait_ge(table_loaded, 1)
            act.wait_ge(chunks_multiplied, END[("ssm_out", KD - 1)])
            for n, (t, second) in enumerate(MID, POST):
                if second:
                    act.wait_ge(x1_ready, t + 1)
                else:
                    tokens_ready(act, POST + t)
                if n > POST:
                    act.wait_ge(sq_summed, n)
                square_sum(n, sq[:, :], x1[:, t, :] if second else token_bank(t))
                root(n)
                if second and t:
                    round_xT(TT + t - 1)
            round_xT(2 * TT - 1)
            act.wait_ge(xn_ready, 2 * TT)
            act.dma_start(g_ffn_post[:, :], norms[3:4, :].partition_broadcast(P).rearrange("p a d -> p (a d)")).then_inc(gpost_landed, 16)

            up0 = FIRST[("up", 0)]

            def up_pair(i, b, f, first):
                for v in range(2):
                    act.wait_ge(chunks_multiplied, 8 * i + (up0 + 4 * b + 2 * v + 2))
                    if not first:
                        act.wait_ge(ff_ready, 2 * i + (b - 1))
                    act.activation(conv[:, b, v, :], ps[:, 2 * b + v, :], ACT.Identity,
                                   bias=cv(3, v, f), scale=cv(2, v, f)).then_inc(conv_begun, 1)
                act.wait_ge(conv_done, 4 * i + (2 * b + 1))
                act.activation(gelu[:, b, :], conv[:, b, 0, :], ACT.Gelu_apprx_tanh).then_inc(gelu_done, 1)

            for b in range(2):
                up_pair(0, b, b, True)
            with act.Fori(1, NF // 2 - 1) as i:
                for b in range(2):
                    up_pair(i, b, 2 * i + b, False)

            down0 = FIRST[("down", 0)]

            def ff_round(i, b, f, first):
                if not first:
                    act.wait_ge(chunks_multiplied, 4 * i + (down0 + 2 * b - 2))
                act.activation(ff_hi[b][:, :], ff_tile(f), ACT.Copy).then_inc(ff_rounded, 1)

            for b in range(2):
                ff_round(0, b, b, True)
            for b in range(2):
                up_pair(NF // 2 - 1, b, NF - 2 + b, False)
            act.wait_ge(ff_ready, NF)
            with act.Fori(1, NF // 2) as i:
                for b in range(2):
                    ff_round(i, b, 2 * i + b, False)
            for t in range(TT):
                tokens_ready(act, FPOST + t)
                act.wait_ge(sq_summed, FPOST + t)
                square_sum(FPOST + t, sq[:, :], token_bank(t))
                root(FPOST + t)

        @block.vector
        def _(dve):
            steps = [0]

            def link(ins):
                ins.then_inc(dve_step, 1)
                steps[0] += 1
                dve.wait_ge(dve_step, steps[0])

            def tt(o, a, b, op):
                link(dve.tensor_tensor(o, a, b, op))

            def ts(o, a, s1, s2, op0, op1):
                link(dve.tensor_scalar(o, a, s1, s2, op0, op1))

            def stt(o, a, s, b, op0, op1):
                link(dve.scalar_tensor_tensor(out=o, in0=a, scalar=s, in1=b, op0=op0, op1=op1))

            def rsqrt_mean(n, count):
                dve.wait_ge(sq_summed, n + 1)
                dve.tensor_scalar(st(1, n), st(0, n), 1.0 / count, EPS, ALU.mult, ALU.add).then_inc(ms_ready, 1)
                dve.wait_ge(rms_ready, n + 1)
                link(dve.reciprocal(st(3, n), st(2, n)))

            def split_xT(n):
                t = n % TT
                for b in range(2):
                    dve.wait_ge(xT_rounded, 2 * n + b + 1)
                    o = (slice(None), slice(4 * b, 4 * b + 4), slice(t * P, (t + 1) * P))
                    dve.tensor_tensor(xT_lo[o], ps[:, 2 * t + b, :].rearrange("p (k n) -> p k n", k=4),
                                      xT_hi[o].bitcast(F32), ALU.subtract).then_inc(xT_split, 1)

            def reduce_angle(a, k):
                ts(k, a, 1.0 / (2 * math.pi), ROUND, ALU.mult, ALU.add)
                ts(k, k, ROUND, None, ALU.subtract, ALU.bypass)
                for part in TWO_PI:
                    stt(a, k, -part, a, ALU.mult, ALU.add)

            def quarter_turn(a, k):
                ts(a, a, math.pi / 2, None, ALU.add, ALU.bypass)
                ts(k, a, math.pi, -2 * math.pi, ALU.is_gt, ALU.mult)
                tt(a, a, k, ALU.add)

            def clamp(a, signal):
                dve.tensor_scalar(a, a, PI_IN, -PI_IN, ALU.min, ALU.max).then_inc(angle_ready, 1)
                dve.wait_ge(angle_ready, signal)

            def exponential(o, y):
                n, r, p = sm("n"), sm("r"), sm("p")
                ts(sm("y"), y, -90.0, 89.0, ALU.max, ALU.min)
                ts(n, sm("y"), 1.0 / math.log(2), ROUND, ALU.mult, ALU.add)
                ts(n, n, ROUND, None, ALU.subtract, ALU.bypass)
                stt(r, n, -LN2[0], sm("y"), ALU.mult, ALU.add)
                stt(r, n, -LN2[1], r, ALU.mult, ALU.add)
                ts(p, r, EXP_TAYLOR[7], None, ALU.mult, ALU.bypass)
                for c in EXP_TAYLOR[6:0:-1]:
                    stt(p, p, c, r, ALU.add, ALU.mult)
                ts(p, p, 1.0, None, ALU.add, ALU.bypass)
                ts(n, n, -127.0, 128.0, ALU.max, ALU.min)
                ts(n, n, 127.0, None, ALU.add, ALU.bypass)
                link(dve.tensor_copy(k_int[:, :], n))
                ts(k_int[:, :], k_int[:, :], 23, None, ALU.logical_shift_left, ALU.bypass)
                tt(o, p, k_int[:, :].bitcast(F32), ALU.mult)

            def together(*products):
                for o, a, b, op in products:
                    dve.tensor_tensor(o, a, b, op).then_inc(dve_step, 1)
                steps[0] += len(products)
                dve.wait_ge(dve_step, steps[0])

            def cmul(outs, a, b, t):
                together((t[0], a[0], b[0], ALU.mult), (t[1], a[1], b[1], ALU.mult),
                         (t[2], a[0], b[1], ALU.mult), (t[3], a[1], b[0], ALU.mult))
                together((outs[0], t[0], t[1], ALU.subtract), (outs[1], t[2], t[3], ALU.add))

            dve.wait_ge(small_landed, 16)
            exponential(sm("dt"), sm("ldt"))
            for t in range(TT):
                rsqrt_mean(PRE + t, D)
                if t == 0:
                    dve.wait_ge(g_landed, 16)
                if t >= 2:
                    dve.wait_ge(x_transposed, t - 1)
                dve.scalar_tensor_tensor(out=xn[:, t % 2, :], in0=x_in[:, t, :], scalar=st(3, PRE + t),
                                         in1=g_mix_pre[:, :], op0=ALU.mult, op1=ALU.mult).then_inc(xn_ready, 1)
                if t:
                    split_xT(t - 1)
            split_xT(TT - 1)
            tt(sm("ang"), sm("li"), sm("dt"), ALU.mult)
            link(dve.tensor_copy(sm("r"), sm("ang")))
            reduce_angle(sm("r"), sm("k"))
            link(dve.tensor_copy(sm("ang"), sm("r")))
            clamp(sm("r"), 1)

            dve.wait_ge(consts_ready, 5)
            dve.tensor_copy(ident_r[:, :], ident[:, :]).then_inc(masks_rounded, 1)
            dve.tensor_copy(causal_r[:, :], causal[:, :]).then_inc(masks_rounded, 1)
            dve.wait_ge(pos_landed, 16)
            dve.wait_ge(vec_landed, 32)
            link(dve.tensor_copy(ang[:, :], pos_i[:, :]))
            ts(ang[:, :], ang[:, :], vec[:, V_INV:V_INV + 1], None, ALU.mult, ALU.bypass)
            reduce_angle(ang[:, :], ang_k[:, :])
            clamp(ang[:, :], 2)
            dve.wait_ge(sine_ready, 2)
            quarter_turn(ang[:, :], ang_k[:, :])
            clamp(ang[:, :], 3)
            dve.wait_ge(sine_ready, 3)
            ts(sin_t[:, :], sin_t[:, :], vec[:, V_SIGN:V_SIGN + 1], None, ALU.mult, ALU.bypass)
            ts(hb_gate[:, :], vec[:, V_BG:V_BG + NG], 0.5, None, ALU.mult, ALU.bypass)
            ts(hb_glu[:, :], vec[:, V_BGLU:V_BGLU + NU], 0.5, None, ALU.mult, ALU.bypass)

            ah, al, p, q = sm("t0"), sm("t1"), sm("t2"), sm("y")
            th, tl = sm("turn_hi"), sm("turn_lo")
            ts(ah, sm("ang"), ROUND / 1024, None, ALU.add, ALU.bypass)
            ts(ah, ah, ROUND / 1024, None, ALU.subtract, ALU.bypass)
            tt(al, sm("ang"), ah, ALU.subtract)
            ts(p, ah, TURNS[0], None, ALU.mult, ALU.bypass)
            ts(q, p, ROUND, None, ALU.add, ALU.bypass)
            ts(q, q, ROUND, None, ALU.subtract, ALU.bypass)
            tt(p, p, q, ALU.subtract)
            stt(q, al, TURNS[0], p, ALU.mult, ALU.add)
            stt(q, sm("ang"), TURNS[1], q, ALU.mult, ALU.add)
            ts(th, q, ROUND / TURN_UNIT, None, ALU.add, ALU.bypass)
            ts(th, th, ROUND / TURN_UNIT, None, ALU.subtract, ALU.bypass)
            tt(tl, p, th, ALU.subtract)
            link(dve.tensor_copy(sm("turn"), q))
            stt(tl, al, TURNS[0], tl, ALU.mult, ALU.add)
            dve.scalar_tensor_tensor(out=tl, in0=sm("ang"), scalar=TURNS[1], in1=tl, op0=ALU.mult, op1=ALU.add).then_inc(turn_split, 1)

            quarter_turn(sm("r"), sm("k"))
            clamp(sm("r"), 4)
            dve.wait_ge(sine_ready, 4)
            tt(sm("t0"), sm("lr"), sm("dt"), ALU.mult)
            exponential(sm("mag"), sm("t0"))
            tt(sm("ar"), sm("mag"), sm("cs"), ALU.mult)
            tt(sm("ai"), sm("mag"), sm("sn"), ALU.mult)
            t = [sm(f"t{n}") for n in range(4)]
            ts(sm("dt"), sm("ar"), -1.0, None, ALU.add, ALU.bypass)
            together((t[0], sm("lr"), sm("lr"), ALU.mult), (t[1], sm("li"), sm("li"), ALU.mult),
                     (t[2], sm("dt"), sm("lr"), ALU.mult), (t[3], sm("ai"), sm("li"), ALU.mult))
            together((sm("den"), t[0], t[1], ALU.add), (sm("zr"), t[2], t[3], ALU.add),
                     (sm("zi"), sm("ai"), sm("lr"), ALU.mult), (sm("p"), sm("dt"), sm("li"), ALU.mult))
            together((sm("zi"), sm("zi"), sm("p"), ALU.subtract))
            link(dve.reciprocal(sm("den"), sm("den")))
            together((za[:, 0, SUB - 1, :], sm("zr"), sm("den"), ALU.mult), (za[:, 1, SUB - 1, :], sm("zi"), sm("den"), ALU.mult))
            link(dve.tensor_copy(pw[:, 0, 0, :], sm("ar")))
            link(dve.tensor_copy(pw[:, 1, 0, :], sm("ai")))
            a1 = (pw[:, 0, 0, :], pw[:, 1, 0, :])
            for k in range(1, SUB):
                cmul((pw[:, 0, k, :], pw[:, 1, k, :]), (pw[:, 0, k - 1, :], pw[:, 1, k - 1, :]), a1, t)
                s = SUB - 1 - k
                cmul((za[:, 0, s, :], za[:, 1, s, :]), (za[:, 0, s + 1, :], za[:, 1, s + 1, :]), a1, t)
            tt(sm("m4"), sm("mag"), sm("mag"), ALU.mult)
            tt(sm("m4"), sm("m4"), sm("m4"), ALU.mult)
            def split_u(j):
                dve.wait_ge(u_rounded, SUB * PPT * (j + 1))
                for s in range(SUB):
                    for q in range(PPT):
                        o = (slice(HALF * s, HALF * (s + 1)), j, q, slice(None))
                        ins = dve.tensor_tensor(u_lo[o], ps[HALF * q:HALF * (q + 1), j, s::SUB], u_hi[o].bitcast(F32), ALU.subtract)
                        if s == SUB - 1 and q == PPT - 1:
                            ins.then_inc(u_split, 1)

            dve.wait_ge(bc_landed, 32)

            def over_h(v, n):
                return v.unsqueeze(3).to_broadcast([P, n, PAIRS, GH])

            def over_k(v, n):
                return v.unsqueeze(1).to_broadcast([P, n, PAIRS, GH])

            b_re, b_im, c_re, c_im = (bc_in[:, n, :, :] for n in range(4))
            t0, t1 = bt[:, 0], bt[:, 1]
            br4, bi4 = over_k(b_re, SUB), over_k(b_im, SUB)
            zr4, zi4 = (over_h(za[:, c, :, :], SUB) for c in range(2))
            together((t0, br4, zr4, ALU.mult), (t1, bi4, zi4, ALU.mult))
            together((ab[:, :, 0, :, :], t0, t1, ALU.subtract))
            together((t0, br4, zi4, ALU.mult), (t1, bi4, zr4, ALU.mult))
            together((ab[:, :, 1, :, :], t0, t1, ALU.add))
            split_u(0)
            split_u(1)
            cr4, ci4 = over_k(c_re, SUB), over_k(c_im, SUB)
            ar4, ai4 = (over_h(pw[:, c, :, :], SUB) for c in range(2))
            link(dve.tensor_copy(ca[:, 0, 0, :, :], c_re))
            ts(ca[:, 0, 1, :, :], c_im, -1.0, None, ALU.mult, ALU.bypass)
            together((t0, cr4, ar4, ALU.mult), (t1, ci4, ai4, ALU.mult))
            together((ca[:, 1:SUB + 1, 0, :, :], t0, t1, ALU.subtract))
            together((t0, cr4, ai4, ALU.mult), (t1, ci4, ar4, ALU.mult))
            stt(ca[:, 1:SUB + 1, 1, :, :], t0, -1.0, t1, ALU.mult, ALU.subtract)
            link(dve.memset(ba_blk[:, :, :, :, :], 0.0))
            link(dve.memset(ca_blk[:, :, :, :, :], 0.0))
            dve.memset(m_t[:, 0, :], 0.0).then_inc(compacts_ready, 1)
            dve.wait_ge(compacts_ready, 1)
            link(dve.tensor_copy(kn_hi[:, :, :, :].rearrange("p q s h -> p (q s h)"), m_t[:, 0, :]))
            link(dve.tensor_copy(kn_lo[:, :, :, :].rearrange("p q s h -> p (q s h)"), m_t[:, 0, :]))

            link(dve.memset(m_t[:, 0, 0:2 * PPT], 0.0))
            for t in (s_hi, s_lo):
                link(dve.tensor_copy(t[:, :, :, 0:1], m_t[:, 0, 0:2 * PPT].rearrange("p (c q n) -> p c q n", c=2, n=1)))
            split_u(2)
            split_u(3)

            dve.wait_ge(c_squared, KQ)
            tt(c_sq[:, 0, :], c_sq[:, 0, :], c_sq[:, 1, :], ALU.add)
            dve.tensor_tensor(c_sq[:, 0, :], c_sq[:, 0, :], c_sq[:, 2, :], ALU.add).then_inc(c_sums, 1)
            dve.wait_ge(c_squared, KQ + KKV)
            dve.tensor_tensor(c_sq[:, KQ, :], c_sq[:, KQ, :], c_sq[:, KQ + 1, :], ALU.add).then_inc(c_sums, 1)

            def rotate(bank, ab_, o, signal):
                rot_a, rot_b = ab_
                for ins in (dve.tensor_tensor(rot_a[:, :], ps[:, bank, :], cos_t[:, :], ALU.mult),
                            dve.tensor_tensor(rot_b[0:64, :], ps[64:P, bank, :], sin_t[64:P, :], ALU.mult),
                            dve.tensor_tensor(rot_b[64:P, :], ps[0:64, bank, :], sin_t[0:64, :], ALU.mult)):
                    ins.then_inc(dve_step, 1)
                steps[0] += 3
                dve.wait_ge(dve_step, steps[0])
                dve.tensor_tensor(o, rot_a[:, :], rot_b[:, :], ALU.add).then_inc(signal, 1)

            dve.wait_ge(chunks_multiplied, END[("kr", 0)])
            rotate(1, rot_ab[0], kr_f[:, :], kr_ready)
            dve.wait_ge(c_totals, 1)
            for b, (bank, count) in enumerate(((5, RQ), (0, RKV))):
                dve.tensor_scalar(r_bc[:, b, :], ps[:, bank, :], 1.0 / count, EPS, ALU.mult, ALU.add).then_inc(c_ms, 1)

            def split_inputs(it):
                for c in range(2):
                    dve.wait_ge(ba_rounded, 2 * it + c + 1)
                    ins = dve.tensor_tensor(ba_lo[:, c, :, :], ps[:, c, :].rearrange("p (q n) -> p q n", q=PPT),
                                            ba_hi[:, c, :, :].bitcast(F32), ALU.subtract)
                    if c:
                        ins.then_inc(ba_split, 1)

            def own_kernel():
                return ps[0:HALF, 2, :].rearrange("p (q t h) -> p q t h", q=PPT, t=SUB)

            def add_skip(it):
                eye = ident[0:HALF, 0:HALF].unsqueeze(1).to_broadcast([HALF, PPT, HALF])
                dd = d_skip[:, it * PPT:(it + 1) * PPT].unsqueeze(2).to_broadcast([HALF, PPT, HALF])
                dt_ = m_t[0:HALF, 0, 0:PPT * HALF].rearrange("p (q h) -> p q h", q=PPT)
                tt(dt_, eye, dd, ALU.mult)
                dve.wait_ge(kn_done, it + 1)
                own = own_kernel()
                dve.tensor_tensor(own[:, :, 0, :], own[:, :, 0, :], dt_, ALU.add).then_inc(skip_added, 1)

            def split_outputs(it):
                for c in range(2):
                    dve.wait_ge(ca_rounded, 6 * it + c + 1)
                    link(dve.tensor_tensor(ca_lo[:, c, :, :, :], ca_blk[:, c, :, 1:SUB + 1, :], ca_hi[:, c, :, :, :].bitcast(F32),
                                           ALU.subtract))
                dve.wait_ge(ca_rounded, 6 * (it + 1))
                for s in range(SUB):
                    o = (slice(HALF * s, HALF * (s + 1)), slice(None), slice(s, SUB), slice(None))
                    ins = dve.tensor_tensor(kn_lo[o], own_kernel()[:, :, 0:SUB - s, :], kn_hi[o].bitcast(F32), ALU.subtract)
                    if s == SUB - 1:
                        ins.then_inc(ca_split, 1)

            angles = rotation_angles(dve, link, first_turns_ready)
            angles(0, 0)
            angles(0, 1)
            split_inputs(0)
            add_skip(0)
            dve.wait_ge(c_rms, 1)
            link(dve.reciprocal(r_bc[:, :, :], r_bc[:, :, :]))
            for j in range(KQ + KKV):
                dve.scalar_tensor_tensor(out=c_raw[:, j, :], in0=c_raw[:, j, :], scalar=vec[:, V_QN + j:V_QN + j + 1],
                                         in1=r_bc[:, int(j >= KQ), :], op0=ALU.mult, op1=ALU.mult).then_inc(cn_ready, 1)

            def rotary_queries(g):
                name = ("uq", 3 * g + 2)
                dve.wait_ge(chunks_multiplied, END[name])
                rotate(6 + GATES_BEFORE[name] % 2, rot_ab[g], rot_ab[g][0][:, :], qr_ready)

            def split_rotary(g):
                dve.wait_ge(qr_ready, g + 1)
                dve.wait_ge(qr_rounded, g + 1)
                dve.scalar_tensor_tensor(out=qr_hl[g][:, 1, :], in0=rot_ab[g][0][:, :], scalar=1.0 / math.sqrt(QK),
                                         in1=qr_hl[g][:, 0, :].bitcast(F32), op0=ALU.mult, op1=ALU.subtract).then_inc(qr_split, 1)

            zr, zi, mr, mi = z_t[:, 0, :], z_t[:, 1, :], m_t[:, 0, :], m_t[:, 1, :]
            dec = decay[:, :, :].rearrange("p q n -> p (q n)")
            for it in range(NU):
                pr = slice(it * PPT, (it + 1) * PPT)
                link(dve.tensor_copy(decay[:, :, :], sm("m4")[:, pr].unsqueeze(2).to_broadcast([P, PPT, NC])))
                link(dve.memset(decay[:, :, 0:1], 0.0))
                dve.wait_ge(bu_done, it + 1)
                rc, rs = (r[:, pr, :].rearrange("p q n -> p (q n)") for r in (rot_c, rot_s))
                dve.wait_ge(rotations_ready, it + 1)
                br, bi = ps[:, 3, :], ps[:, 4, :]
                if it:
                    dve.wait_ge(states_rounded, it)
                tt(zr, br, rc, ALU.mult)
                tt(mr, bi, rs, ALU.mult)
                tt(zr, zr, mr, ALU.add)
                tt(zi, bi, rc, ALU.mult)
                dve.tensor_tensor(mr, br, rs, ALU.mult).then_inc(inputs_read, 1)
                dve.wait_ge(inputs_read, it + 1)
                tt(zi, zi, mr, ALU.subtract)
                link(dve.tensor_tensor_scan(mr, dec, zr, 0.0, ALU.mult, ALU.add))
                link(dve.tensor_tensor_scan(mi, dec, zi, 0.0, ALU.mult, ALU.add))
                split_outputs(it)
                if it + 1 < NU:
                    split_inputs(it + 1)
                tt(dec, mi, rs, ALU.mult)
                tt(zr, mr, rc, ALU.mult)
                tt(zr, zr, dec, ALU.subtract)
                tt(dec, mr, rs, ALU.mult)
                tt(zi, mi, rc, ALU.mult)
                dve.tensor_tensor(zi, zi, dec, ALU.add).then_inc(states_ready, 1)
                if it + 1 < NU:
                    add_skip(it + 1)
                dve.wait_ge(states_ready, it + 1)
                dve.wait_ge(states_rounded, it + 1)
                dve.tensor_tensor(s_lo[:, :, :, 1:NC], z_t[:, :, :].rearrange("p c (q n) -> p c q n", q=PPT)[:, :, :, 0:NC - 1],
                                  s_hi[:, :, :, 1:NC].bitcast(F32), ALU.subtract).then_inc(states_split, 1)
                if it == 0:
                    for j in range(KQ + KKV):
                        dve.wait_ge(cn_rounded, j + 1)
                        dve.tensor_tensor(cn_lo[:, j, :], c_raw[:, j, :], cn_hi[:, j, :].bitcast(F32), ALU.subtract).then_inc(cn_split, 1)

            for t in range(TT):
                dve.wait_ge(v_rounded, t + 1)
                dve.tensor_tensor(v_lo[:, t, :], ps[:, V_BANK[t], :], v_hi[:, t, :].bitcast(F32), ALU.subtract).then_inc(v_split, 1)
            for e, col in enumerate((V_EVEN, V_ODD)):
                dve.wait_ge(kr_rounded, e + 1)
                dve.scalar_tensor_tensor(out=kr_hl[:, 1, e, :], in0=kr_f[:, :], scalar=vec[:, col:col + 1],
                                         in1=kr_hl[:, 0, e, :].bitcast(F32), op0=ALU.mult, op1=ALU.subtract).then_inc(kr_split, 1)

            rotary_queries(0)
            split_rotary(0)

            UNITS = HG * TT
            scale = 1.0 / math.sqrt(QK)
            for g in range(2):
                for m, bank in enumerate((3, 0)):
                    for e in range(2):
                        dve.wait_ge(k_rounded, HG * g + 2 * m + e + 1)
                        o = (slice(0, NOPE), 2 * m + e, slice(None))
                        dve.tensor_tensor(k_lo[o], ps[e * NOPE:(e + 1) * NOPE, bank, :], k_hi[o].bitcast(F32),
                                          ALU.subtract).then_inc(k_split, 1)
                for m, bank in enumerate((4, 5)):
                    for e in range(2):
                        dve.wait_ge(q_rounded, HG * g + 2 * m + e + 1)
                        o = (slice(0, NOPE), 2 * m + e, slice(None))
                        dve.scalar_tensor_tensor(out=q_lo[o], in0=ps[e * NOPE:(e + 1) * NOPE, bank, :], scalar=scale,
                                                 in1=q_hi[o].bitcast(F32), op0=ALU.mult, op1=ALU.subtract).then_inc(q_split, 1)

                for t in range(UNITS + 3):
                    if 3 <= t < UNITS + 3:
                        u = t - 3
                        i = u % TT
                        o = (slice(None), slice(0, i + 1), slice(i * P, (i + 1) * P))
                        dve.wait_ge(pT_rounded, UNITS * g + u + 1)
                        dve.tensor_tensor(pT_lo[o], ps[:, 2 + u % 2, 0:(i + 1) * P].rearrange("p (j n) -> p j n", n=P),
                                          pT_hi[o].bitcast(F32), ALU.subtract).then_inc(pT_split, 1)
                    if t < UNITS:
                        i = t % TT
                        n = (i + 1) * P
                        dve.wait_ge(scores_done, UNITS * g + t + 1)
                        dve.tensor_reduce(rowst[:, 0, t % 4:t % 4 + 1], ps[:, t % 2, 0:n], AX_X, ALU.max,
                                          negate=True).then_inc(max_ready, 1)
                    if 1 <= t < UNITS + 1:
                        u = t - 1
                        n = (u % TT + 1) * P
                        dve.wait_ge(exp_done, UNITS * g + u + 1)
                        link(dve.reciprocal(rowst[:, 3, u % 4:u % 4 + 1], rowst[:, 1, u % 4:u % 4 + 1]))
                        dve.tensor_scalar(prob[:, u % 2, 0:n], prob[:, u % 2, 0:n], rowst[:, 3, u % 4:u % 4 + 1], None,
                                          ALU.mult, ALU.bypass).then_inc(probs_ready, 1)
                    if g == 0 and t == UNITS + 2:
                        rotary_queries(1)
                        split_rotary(1)
                    if g and t - 1 in Y_STEPS:
                        j = Y_STEPS.index(t - 1)
                        dve.wait_ge(y_rounded, j + 1)
                        dve.tensor_tensor(y_lo[:, j, :], y_f[j][:, :], y_hi[:, j, :].bitcast(F32), ALU.subtract).then_inc(y_split, 1)
            for j in range(NU):
                dve.wait_ge(at_rounded, j + 1)
                dve.tensor_tensor(at_lo[:, j, :], at_f[:, j, :], at_hi[:, j, :].bitcast(F32), ALU.subtract).then_inc(at_split, 1)

            for m in range(NU):
                dve.wait_ge(glu_tanh, m + 1)
                dve.scalar_tensor_tensor(out=glu_y[:, m % 2, :], in0=glu_t[:, m % 2, :], scalar=1.0, in1=y_f[m][:, :],
                                         op0=ALU.add, op1=ALU.mult).then_inc(glu_ready, 1)
                dve.wait_ge(ss_rounded, m + 1)
                dve.scalar_tensor_tensor(out=ss_lo[:, m, :], in0=glu_y[:, m % 2, :], scalar=0.5, in1=ss_hi[:, m, :].bitcast(F32),
                                         op0=ALU.mult, op1=ALU.subtract).then_inc(ss_split, 1)
            for m in range(KD):
                b = 2 * (m % 2)
                ta, tb = mg_t[:, m % 2, 0, :], mg_t[:, m % 2, 1, :]
                dve.wait_ge(chunks_multiplied, END[("attn_out", m)])
                stt(ta, gates[:, m, :], 1.0, ps[:, b, :], ALU.add, ALU.mult)
                dve.wait_ge(chunks_multiplied, END[("ssm_out", m)])
                stt(tb, gates[:, KD + m, :], 1.0, ps[:, b + 1, :], ALU.add, ALU.mult)
                dve.tensor_tensor(ta, ta, tb, ALU.add).then_inc(mg_ready, 1)
                dve.wait_ge(mg_rounded, m + 1)
                dve.scalar_tensor_tensor(out=mg_lo[:, m, :], in0=ta, scalar=0.5, in1=mg_hi[:, m, :].bitcast(F32),
                                         op0=ALU.mult, op1=ALU.subtract).then_inc(mg_split, 1)

            dve.wait_ge(x1_landed, 16 * TT)
            dve.wait_ge(gmid_landed, 32)
            for n, (t, second) in enumerate(MID, POST):
                if second:
                    dve.wait_ge(x1_ready, t + 1)
                    rsqrt_mean(n, D)
                    if t >= 2:
                        dve.wait_ge(x_transposed, TT + t - 1)
                    dve.scalar_tensor_tensor(out=xn2[:, t % 2, :], in0=x1[:, t, :], scalar=st(3, n), in1=g_ffn_pre[:, :],
                                             op0=ALU.mult, op1=ALU.mult).then_inc(xn_ready, 1)
                    if t:
                        split_xT(TT + t - 1)
                else:
                    tokens_ready(dve, POST + t)
                    rsqrt_mean(n, D)
                    if t >= 2:
                        dve.wait_ge(x1_ready, t - 1)
                    dve.scalar_tensor_tensor(out=mixed[:, t % 2, :], in0=token_bank(t), scalar=st(3, n), in1=g_mix_post[:, :],
                                             op0=ALU.mult, op1=ALU.mult).then_inc(mixed_ready, 1)
            split_xT(2 * TT - 1)

            def taps(i, b, v, f):
                q = 2 * b + v
                o, z = conv[:, b, v, :], ps[:, 2 * b + v, :]
                dve.wait_ge(conv_begun, 4 * i + (q + 1))
                dve.scalar_tensor_tensor(out=o[:, 1:L], in0=z[:, 0:L - 1], scalar=cv(1, v, f), in1=o[:, 1:L],
                                         op0=ALU.mult, op1=ALU.add).then_inc(conv_step, 1)
                dve.wait_ge(conv_step, 4 * i + (q + 1))
                dve.scalar_tensor_tensor(out=o[:, 2:L], in0=z[:, 0:L - 2], scalar=cv(0, v, f), in1=o[:, 2:L],
                                         op0=ALU.mult, op1=ALU.add).then_inc(conv_done, 1)

            def up_pair(i, b, f):
                taps(i, b, 0, f)
                taps(i, b, 1, f)
                dve.wait_ge(conv_done, 4 * i + (2 * b + 2))
                dve.wait_ge(gelu_done, 2 * i + (b + 1))
                dve.tensor_tensor(ff_tile(f), gelu[:, b, :], conv[:, b, 1, :], ALU.mult).then_inc(ff_ready, 1)

            for b in range(2):
                up_pair(0, b, b)
            with dve.Fori(1, NF // 2 - 1) as i:
                for b in range(2):
                    up_pair(i, b, 2 * i + b)

            def ff_low(i, b, f):
                dve.wait_ge(ff_rounded, 2 * i + (b + 1))
                dve.tensor_tensor(ff_lo[b][:, :], ff_tile(f), ff_hi[b][:, :].bitcast(F32), ALU.subtract).then_inc(ff_split, 1)

            for b in range(2):
                ff_low(0, b, b)
            for b in range(2):
                up_pair(NF // 2 - 1, b, NF - 2 + b)
            with dve.Fori(1, NF // 2) as i:
                for b in range(2):
                    ff_low(i, b, 2 * i + b)

            dve.wait_ge(gpost_landed, 16)
            for t in range(TT):
                n = FPOST + t
                tokens_ready(dve, n)
                rsqrt_mean(n, D)
                normed = conv[:, t % 2, :, :].rearrange("p b n -> p (b n)")
                stt(normed, token_bank(t), st(3, n), g_ffn_post[:, :], ALU.mult, ALU.mult)
                dve.tensor_tensor(x1[:, t, :], x1[:, t, :], normed, ALU.add).then_inc(out_ready, 1)


_OUT = (1, L, D)


def _columns():
    r = np.arange(P)
    cols = {}
    for j in range(KQ):
        cols[("cq", j)] = ("w_in", O_CQ + j * P + r)
    for j in range(KKV):
        cols[("ckv", j)] = ("w_in", O_CKV + j * P + r)
    half = ROPE // 2
    cols[("kr", 0)] = ("w_in", O_KR + np.concatenate([np.tile(np.arange(half), 4), np.tile(half + np.arange(half), 4)]))
    for n in range(NG):
        cols[("gate", n)] = ("w_in", O_GATE + n * P + r)
    for j in range(NU):
        cols[("u", j)] = ("w_in", O_U + j * P + r)
    for g in range(2):
        heads = [HG * g + h for h in range(HG)]
        for m in range(2):
            cols[("uq", 3 * g + m)] = ("w_uq", np.concatenate([h * QK + np.arange(NOPE) for h in heads[2 * m:2 * m + 2]]))
        cols[("uq", 3 * g + 2)] = ("w_uq", np.concatenate(
            [h * QK + NOPE + c * half + np.arange(half) for c in range(2) for h in heads]))
    for m in range(NU):
        cols[("glu", m)] = ("w_glu", m * P + r)
    for m in range(KD):
        cols[("attn_out", m)] = ("w_branch_attn", m * P + r)
        cols[("ssm_out", m)] = ("w_branch_ssm", m * P + r)
    for f in range(2 * NF):
        cols[("up", f)] = ("w_up", f * P + r)
    return cols


def _lay_out_stream(w):
    stream = np.zeros((NCHUNK, P, CH), np.float32)
    cols = _columns()
    tiles = CH // P
    for n, (name, part) in enumerate(ORDER):
        kind, j = name
        if name in cols:
            mat, c = cols[name]
            block = w[mat][part * CH:(part + 1) * CH][:, c]
            k = block.shape[0] // P
            stream[n, :, :k * P] = block.reshape(k, P, P).transpose(1, 0, 2).reshape(P, k * P)
        elif kind == "uk":
            block = w["w_uk"][:, j * HG * NOPE:(j + 1) * HG * NOPE]
            stream[n] = block.reshape(KKV, P, tiles // KKV, P).transpose(1, 2, 0, 3).reshape(P, CH)
        elif kind == "uv":
            stream[n] = w["w_uv"][part * P:(part + 1) * P]
        else:
            mat = w[{"w_out": "w_out", "down": "w_down"}[kind]]
            stream[n] = mat[j * P:(j + 1) * P, part * CH:(part + 1) * CH]
    return stream


def kernel(**inputs):
    import concourse.bacc as bacc
    from concourse.bass_utils import run_bass_kernel_spmd as run

    a = {name: np.asarray(v) for name, v in inputs.items()}
    w = {name: a[name][0] for name in ("w_in", "w_uq", "w_uk", "w_uv", "w_glu", "w_branch_attn", "w_branch_ssm",
                                       "w_out", "w_up", "w_down")}

    def tiles(v):
        return v.reshape(-1, P).T

    rows = np.arange(P)
    inv = (np.float32(10000.0) ** (-np.arange(0, ROPE, 2, dtype=np.float32) / np.float32(ROPE))).astype(np.float32)
    shape_columns = np.stack([inv[rows % (ROPE // 2)], (rows % ROPE < ROPE // 2), (rows % ROPE >= ROPE // 2),
                              np.where(rows < P // 2, 1.0, -1.0), np.full(P, math.pi / 2)], axis=1).astype(np.float32)
    conv_rows = np.concatenate([a["conv_w"][0], a["conv_b"]], axis=0)
    vecs = np.concatenate([tiles(a["q_norm"][0]), tiles(a["kv_norm"][0]), tiles(a["b_gate"][0]), tiles(a["b_glu"][0]),
                           shape_columns, tiles(conv_rows)], axis=1)
    norms = np.concatenate([a["mix_norm_pre"], a["mix_norm_post"], a["ffn_norm_pre"], a["ffn_norm_post"]], axis=0)

    def states(v):
        v = v.reshape(PAIRS, 2, NS, *v.shape[2:])
        return np.moveaxis(v, 0, 2).reshape(P, PAIRS, *v.shape[3:])

    ldt = np.broadcast_to(a["ssm_log_dt"][0][:, None], (GROUPS, NS))
    ssm_small = np.stack([states(a["ssm_lambda_re"][0]), states(a["ssm_lambda_im"][0]), states(ldt)], axis=1)
    ssm_bc = np.stack([states(a["ssm_b_re"][0]), states(a["ssm_b_im"][0]),
                       states(a["ssm_c_re"][0].transpose(0, 2, 1)), states(a["ssm_c_im"][0].transpose(0, 2, 1))], axis=1)
    ssm_d = a["ssm_d"][0].reshape(PAIRS, HALF).T

    nc = bacc.Bacc("TRN2", target_bir_lowering=False, num_devices=1)
    arrays = {"w_stream": _lay_out_stream(w), "x": a["x"][0], "positions": a["positions"], "vecs": vecs,
              "steps_row": np.arange(NC, dtype=np.float32)[None, :], "norms": norms,
              "ssm_small": ssm_small, "ssm_bc": ssm_bc, "ssm_d": ssm_d}
    arrays = {f"in_{n}_dram": np.ascontiguousarray(v) for n, v in arrays.items()}
    args = [nc.dram_tensor(n, v.shape, mybir.dt.from_np(v.dtype), kind="ExternalInput").ap() for n, v in arrays.items()]
    out = nc.dram_tensor("out_0_dram", _OUT, F32, kind="ExternalOutput").ap()
    build(nc, *args, out.rearrange("a l d -> (a l) d"))
    result = run(nc, [arrays], core_ids=[0])
    return result.results[0]["out_0_dram"]
```
